# Optimizing a Trainium2 kernel written in Bass

```python
import jax, jax.numpy as jnp
from jax import lax
import numpy as np

D_MODEL = 1024
BATCH = 1
SEQ = 2048
DEPTH = 1
DEC_BATCH = 1
DEC_SEQ = 32
PAST_LEN = 1024

CHUNK = 64
D_MIX = D_MODEL
ML_HEADS = 4
ML_DIM = 128
ML_WIDTH = ML_HEADS * ML_DIM
SB_HEADS = 8
SB_DIM = 64
SB_WIDTH = SB_HEADS * SB_DIM
Q_BLOCK = 128
D_FF = 2816
CONV_W = 3
EPS = 1e-6
SPLIT_SIZES = (ML_WIDTH, ML_WIDTH, ML_WIDTH, ML_WIDTH, ML_HEADS, ML_HEADS, SB_WIDTH, SB_WIDTH, SB_WIDTH)
D_IN = 4 * ML_WIDTH + 2 * ML_HEADS + 3 * SB_WIDTH

kernel_name = "hymba_mlstm_stickbreaking_convffn_step"

def rmsnorm(x, w):
    xf = x.astype(jnp.float32)
    y = xf * lax.rsqrt(jnp.mean(xf * xf, axis=-1, keepdims=True) + EPS)
    return (y * w.astype(jnp.float32)).astype(x.dtype)

def adaln(c, w_ada, b_ada):
    mod = jax.nn.silu(c) @ w_ada + b_ada
    return jnp.split(mod[:, None, :], 6, axis=-1)

def split_proj(proj):
    idx, acc = [], 0
    for s in SPLIT_SIZES[:-1]:
        acc += s
        idx.append(acc)
    return jnp.split(proj, idx, axis=-1)

def mlstm_chunk(state, inp):
    C, n, m = state
    q, k, v, ig, lf = inp
    L = q.shape[2]
    b = jnp.cumsum(lf, axis=-1)
    causal = jnp.tril(jnp.ones((L, L), dtype=bool))
    d_log = jnp.where(causal, b[..., :, None] - b[..., None, :] + ig[..., None, :], -jnp.inf)
    inter = b + m[..., None]
    m_t = jnp.maximum(inter, jnp.max(d_log, axis=-1))
    w_intra = jnp.exp(d_log - m_t[..., None])
    w_inter = jnp.exp(inter - m_t)
    s = jnp.einsum('bhtd,bhsd->bhts', q, k) * w_intra
    num = w_inter[..., None] * jnp.einsum('bhtd,bhde->bhte', q, C) + jnp.einsum('bhts,bhse->bhte', s, v)
    den = w_inter * jnp.einsum('bhtd,bhd->bht', q, n) + jnp.sum(s, axis=-1)
    h = num / jnp.maximum(jnp.abs(den), jnp.exp(-m_t))[..., None]
    b_last = b[..., -1]
    w_k = b_last[..., None] - b + ig
    m_new = jnp.maximum(b_last + m, jnp.max(w_k, axis=-1))
    decay = jnp.exp(b_last + m - m_new)
    wk = jnp.exp(w_k - m_new[..., None])
    C_new = decay[..., None, None] * C + jnp.einsum('bhs,bhsd,bhse->bhde', wk, k, v)
    n_new = decay[..., None] * n + jnp.einsum('bhs,bhsd->bhd', wk, k)
    return (C_new, n_new, m_new), h

def mlstm_prompt(q, k, v, ig, lf):
    B, H, T, _ = q.shape
    nc = T // CHUNK

    def to_chunks(t):
        return jnp.moveaxis(t.reshape(t.shape[:2] + (nc, CHUNK) + t.shape[3:]), 2, 0)

    init = (jnp.zeros((B, H, ML_DIM, ML_DIM), jnp.float32),
            jnp.zeros((B, H, ML_DIM), jnp.float32),
            jnp.zeros((B, H), jnp.float32))
    state, h = lax.scan(mlstm_chunk, init, (to_chunks(q), to_chunks(k), to_chunks(v), to_chunks(ig), to_chunks(lf)))
    h = jnp.moveaxis(h, 0, 2).reshape(B, H, T, ML_DIM)
    return h, state

def stick_breaking_block(q, k, v, q_pos, k_pos):
    z = jnp.einsum('bhtd,bhsd->bhts', q, k).astype(jnp.float32) * (SB_DIM ** -0.5)
    mask = k_pos[None, :] < q_pos[:, None]
    log_beta = jnp.where(mask, jax.nn.log_sigmoid(z), -jnp.inf)
    log_1m = jnp.where(mask, jax.nn.log_sigmoid(-z), 0.0)
    rest = lax.cumsum(log_1m, axis=3, reverse=True) - log_1m
    a = jnp.exp(log_beta + rest)
    return jnp.einsum('bhts,bhsd->bhtd', a.astype(v.dtype), v)

def sb_prompt(q, k, v):
    B, H, T, d = q.shape
    nb = T // Q_BLOCK
    qb = jnp.moveaxis(q.reshape(B, H, nb, Q_BLOCK, d), 2, 0)
    k_pos = jnp.arange(T)

    def one_block(args):
        q_blk, start = args
        return stick_breaking_block(q_blk, k, v, start + jnp.arange(Q_BLOCK), k_pos)

    o = lax.map(one_block, (qb, jnp.arange(nb) * Q_BLOCK))
    return jnp.moveaxis(o, 0, 2).reshape(B, H, T, d)

def conv_ffn(h, conv_state, w_up, w_conv, b_conv, w_down):
    u = h @ w_up
    T = u.shape[1]
    padded = jnp.concatenate([conv_state.astype(u.dtype), u], axis=1)
    uc = sum(padded[:, j:j + T] * w_conv[j] for j in range(CONV_W)) + b_conv
    a, g = jnp.split(uc, 2, axis=-1)
    out = (jax.nn.silu(a) * g) @ w_down
    return out, padded[:, -(CONV_W - 1):]

def trunk_layer(x, c, p, ml_state=None, k_past=None, v_past=None, conv_state=None):
    B, T, _ = x.shape
    sh1, sc1, g1, sh2, sc2, g2 = adaln(c, p['w_ada'], p['b_ada'])
    h = rmsnorm(x, p['norm1_w']) * (1 + sc1) + sh1
    mq, mk, mv, mo, mi, mf, sq, sk, sv = split_proj(h @ p['w_in'])

    def heads(t, nh):
        return t.reshape(B, T, nh, -1).transpose(0, 2, 1, 3).astype(jnp.float32)
    q_a = heads(mq, ML_HEADS)
    k_a = heads(mk, ML_HEADS) * (ML_DIM ** -0.5)
    v_a = heads(mv, ML_HEADS)
    ig = (mi + p['b_ig']).astype(jnp.float32).transpose(0, 2, 1)
    lf = jax.nn.log_sigmoid((mf + p['b_fg']).astype(jnp.float32)).transpose(0, 2, 1)
    if ml_state is None:
        h_cell, ml_new = mlstm_prompt(q_a, k_a, v_a, ig, lf)
    else:
        st = tuple(s.astype(jnp.float32) for s in ml_state)
        ml_new, h_cell = mlstm_chunk(st, (q_a, k_a, v_a, ig, lf))
    h_cell = rmsnorm(h_cell.transpose(0, 2, 1, 3), p['ml_norm_w']).reshape(B, T, ML_WIDTH).astype(x.dtype)
    y_a = h_cell * jax.nn.sigmoid(mo)

    q_b = rmsnorm(sq.reshape(B, T, SB_HEADS, SB_DIM), p['sb_q_norm_w'])
    k_rows = rmsnorm(sk.reshape(B, T, SB_HEADS, SB_DIM), p['sb_k_norm_w'])
    v_rows = sv.reshape(B, T, SB_HEADS, SB_DIM)
    if k_past is None:
        o_b = sb_prompt(q_b.transpose(0, 2, 1, 3), k_rows.transpose(0, 2, 1, 3), v_rows.transpose(0, 2, 1, 3))
    else:
        P = k_past.shape[1]
        k_all = jnp.concatenate([k_past.astype(k_rows.dtype), k_rows], axis=1).transpose(0, 2, 1, 3)
        v_all = jnp.concatenate([v_past.astype(v_rows.dtype), v_rows], axis=1).transpose(0, 2, 1, 3)
        o_b = stick_breaking_block(q_b.transpose(0, 2, 1, 3), k_all, v_all, P + jnp.arange(T), jnp.arange(P + T))
    y_b = rmsnorm(o_b.transpose(0, 2, 1, 3).reshape(B, T, SB_WIDTH), p['sb_out_norm_w'])

    mix = jnp.concatenate([y_a, y_b], axis=-1) @ p['w_out']
    x = x + g1 * mix

    h2 = rmsnorm(x, p['norm2_w']) * (1 + sc2) + sh2
    if conv_state is None:
        conv_state = jnp.zeros((B, CONV_W - 1, 2 * D_FF), x.dtype)
    f_out, conv_new = conv_ffn(h2, conv_state, p['w_up'], p['w_conv'], p['b_conv'], p['w_down'])
    x = x + g2 * f_out
    return x, ml_new, k_rows, v_rows, conv_new

def setup_inputs(seed: int = 0) -> dict:
    key = jax.random.key(seed)
    ks = jax.random.split(key, 32)
    nrm = lambda k, shape: jax.random.normal(k, shape, jnp.float32)
    return {
        "x_prompt": nrm(ks[0], (BATCH, SEQ, D_MODEL)),
        "x_sample": nrm(ks[1], (DEC_BATCH, DEC_SEQ, D_MODEL)),
        "c_prompt": nrm(ks[2], (BATCH, D_MODEL)),
        "c_sample": nrm(ks[3], (DEC_BATCH, D_MODEL)),
        "state_mlstm_c": 0.1 * nrm(ks[4], (DEPTH, DEC_BATCH, ML_HEADS, ML_DIM, ML_DIM)),
        "state_mlstm_n": 0.5 * nrm(ks[5], (DEPTH, DEC_BATCH, ML_HEADS, ML_DIM)),
        "state_mlstm_m": 0.5 * nrm(ks[6], (DEPTH, DEC_BATCH, ML_HEADS)),
        "cache_sb_k": nrm(ks[7], (DEPTH, DEC_BATCH, PAST_LEN, SB_HEADS, SB_DIM)),
        "cache_sb_v": nrm(ks[8], (DEPTH, DEC_BATCH, PAST_LEN, SB_HEADS, SB_DIM)),
        "state_ffn_conv": nrm(ks[9], (DEPTH, DEC_BATCH, CONV_W - 1, 2 * D_FF)),
        "w_ada": 0.5 * D_MODEL ** -0.5 * nrm(ks[10], (DEPTH, D_MODEL, 6 * D_MODEL)),
        "b_ada": 0.01 * nrm(ks[11], (DEPTH, 6 * D_MODEL)),
        "norm1_w": 1.0 + 0.02 * nrm(ks[12], (DEPTH, D_MODEL)),
        "w_in": D_MODEL ** -0.5 * nrm(ks[13], (DEPTH, D_MODEL, D_IN)),
        "b_ig": 0.1 * nrm(ks[14], (DEPTH, ML_HEADS)),
        "b_fg": 3.0 + 0.5 * nrm(ks[15], (DEPTH, ML_HEADS)),
        "ml_norm_w": 1.0 + 0.02 * nrm(ks[16], (DEPTH, ML_HEADS, ML_DIM)),
        "sb_q_norm_w": 1.0 + 0.02 * nrm(ks[17], (DEPTH, SB_DIM)),
        "sb_k_norm_w": 1.0 + 0.02 * nrm(ks[18], (DEPTH, SB_DIM)),
        "sb_out_norm_w": 1.0 + 0.02 * nrm(ks[19], (DEPTH, SB_WIDTH)),
        "w_out": D_MIX ** -0.5 * nrm(ks[20], (DEPTH, D_MIX, D_MODEL)),
        "norm2_w": 1.0 + 0.02 * nrm(ks[21], (DEPTH, D_MODEL)),
        "w_up": D_MODEL ** -0.5 * nrm(ks[22], (DEPTH, D_MODEL, 2 * D_FF)),
        "w_conv": CONV_W ** -0.5 * nrm(ks[23], (DEPTH, CONV_W, 2 * D_FF)),
        "b_conv": 0.01 * nrm(ks[24], (DEPTH, 2 * D_FF)),
        "w_down": D_FF ** -0.5 * nrm(ks[25], (DEPTH, D_FF, D_MODEL)),
    }

def reference(x_prompt, x_sample, c_prompt, c_sample, state_mlstm_c, state_mlstm_n, state_mlstm_m,
              cache_sb_k, cache_sb_v, state_ffn_conv, w_ada, b_ada, norm1_w, w_in, b_ig, b_fg,
              ml_norm_w, sb_q_norm_w, sb_k_norm_w, sb_out_norm_w, w_out, norm2_w, w_up, w_conv,
              b_conv, w_down):
    weights = {"w_ada": w_ada, "b_ada": b_ada, "norm1_w": norm1_w, "w_in": w_in, "b_ig": b_ig,
               "b_fg": b_fg, "ml_norm_w": ml_norm_w, "sb_q_norm_w": sb_q_norm_w,
               "sb_k_norm_w": sb_k_norm_w, "sb_out_norm_w": sb_out_norm_w, "w_out": w_out,
               "norm2_w": norm2_w, "w_up": w_up, "w_conv": w_conv, "b_conv": b_conv, "w_down": w_down}
    y_p, y_s = x_prompt, x_sample
    pc, pn, pm, pk, pv, pf = [], [], [], [], [], []
    sc, sn, sm, sk, sv, sf = [], [], [], [], [], []
    for l in range(DEPTH):
        p = {name: w[l] for name, w in weights.items()}
        y_p, (c_new, n_new, m_new), k_new, v_new, f_new = trunk_layer(y_p, c_prompt, p)
        pc.append(c_new); pn.append(n_new); pm.append(m_new); pk.append(k_new); pv.append(v_new); pf.append(f_new)
        y_s, (c_new, n_new, m_new), k_new, v_new, f_new = trunk_layer(
            y_s, c_sample, p, (state_mlstm_c[l], state_mlstm_n[l], state_mlstm_m[l]),
            cache_sb_k[l], cache_sb_v[l], state_ffn_conv[l])
        sc.append(c_new); sn.append(n_new); sm.append(m_new); sk.append(k_new); sv.append(v_new); sf.append(f_new)
    return (y_p, y_s,
            jnp.stack(pc), jnp.stack(pn), jnp.stack(pm), jnp.stack(pk), jnp.stack(pv), jnp.stack(pf),
            jnp.stack(sc), jnp.stack(sn), jnp.stack(sm), jnp.stack(sk), jnp.stack(sv), jnp.stack(sf))


_drawn_inputs = setup_inputs


def setup_inputs(seed=0):
    import zlib

    import numpy as np

    out = dict(_drawn_inputs(seed))
    spreads = {}
    factors = {'cache_sb_k': 4.362,
     'b_fg': 2.693,
     'ml_norm_w': 8.0,
     'sb_q_norm_w': 8.0,
     'sb_k_norm_w': 2.823,
     'sb_out_norm_w': 8.0,
     'norm2_w': 2.784,
     'b_conv': 8.0}
    for name, (base, spread) in spreads.items():
        noise = np.random.default_rng([zlib.crc32(name.encode()), seed]).standard_normal(out[name].shape)
        drawn = base * np.exp(spread * noise) if base else spread * noise
        out[name] = __import__('jax').numpy.asarray(drawn.astype(out[name].dtype))
    for name, factor in factors.items():
        out[name] = (out[name] * factor).astype(out[name].dtype)
    return out
```

```python
from contextlib import ExitStack

import numpy as np
import concourse.bass as bass
from concourse import mybir

F32 = mybir.dt.float32
F32R = mybir.dt.float32r
ACT = mybir.ActivationFunctionType
ALU = mybir.AluOpType
AX = mybir.AxisListType

P = 128
D = 1024
KD = D // P
SEQ, DEC, PAST = 2048, 32, 1024
NPT = SEQ // P
NT = NPT + 1
TOK = NT * P
MH, MD = 4, 128
SH, SD = 8, 64
W5 = 512
FF = 2816
NF = FF // P
EPS = 1e-6
FAR = -1e30
NPB = PAST // P


def tiles(eng, body):
    body(0, 0, 0, True)
    body(1, 1, 0, True)
    with eng.Fori(1, NPT // 2) as i:
        body(2 * i, 0, i, False)
        body(2 * i + 1, 1, i, False)
    body(NPT, 0, NPT // 2, False)


def at_least(eng, sem, value):
    if not (isinstance(value, int) and value <= 0):
        eng.wait_ge(sem, value)


def tok(t):
    return bass.ds(t * P, P)


class Kernel:
    def __init__(self, nc, ctx, dram):
        self.nc, self.ctx, self.d = nc, ctx, dram
        self.nsem, self.own = 0, []

    def sem(self, name):
        self.nsem += 1
        self.own.append(self.nc.alloc_semaphore(f"{name}_{self.nsem}"))
        return self.own[-1]

    def end_phase(self):
        self.nc.clear_and_free_semaphores(self.own)
        self.own = []
        self.nc.all_engine_barrier()

    def sems(self, *names):
        return [self.sem(n) for n in names]

    def scratch(self, name, shape, dt=F32):
        self.d[name] = self.nc.dram_tensor(name, shape, dt, kind="Internal").ap()
        return self.d[name]


def sbuf(nc, ctx, name, shape, dt=F32):
    return ctx.enter_context(nc.sbuf_tensor(name, shape, dt))


def psum(nc, ctx, name, shape):
    return ctx.enter_context(nc.psum_tensor(name, shape, F32))


def modulation(k, c):
    nc, d = k.nc, k.d
    loaded, bias_in, zero, ident_ready, sig_ready, silu_ready, mod_psum, mod_ready, mod_t, mod_row, stored, scale1, lead = k.sems(
        "c_loaded", "bias_loaded", "zeroed", "identity_ready", "sigmoid_ready", "silu_ready", "mod_summed", "mod_ready",
        "mod_transposed", "mod_row_ready", "mod_stored", "scale_ready", "scale_plus_one")
    NCH, NB = 12, 3
    w_in = [k.sem(f"w_ada_loaded{n}") for n in range(NB)]
    with ExitStack() as s:
        wa = sbuf(nc, s, "w_ada_sb", [P, NB, KD, W5])
        cT = sbuf(nc, s, "cT", [P, KD, 2])
        sg = sbuf(nc, s, "sg", [P, KD, 2])
        sc = sbuf(nc, s, "silu_c", [P, KD, 2])
        badd = sbuf(nc, s, "b_ada_sb", [P, 48])
        n1 = sbuf(nc, s, "n1", [P, KD])
        n2 = sbuf(nc, s, "n2", [P, KD])
        row = sbuf(nc, s, "modrow", [96, P])
        pm = psum(nc, s, "pm", [P, 512])
        pr = psum(nc, s, "pr", [P, 512])
        block = s.enter_context(nc.Block())

        @block.sync
        def _(sp):
            sp.dma_start(cT[:], d["c_T"]).then_inc(loaded, 16)
            src = d["w_ada"].rearrange("(k p) n -> p k n", p=P)

            def load(chunk, b):
                sp.dma_start(wa[:, b], src[:, :, bass.ds(chunk * W5, W5)]).then_inc(w_in[b], 16)

            for b in range(NB):
                load(b, b)
            with sp.Fori(1, NCH // NB) as i:
                for b in range(NB):
                    sp.wait_ge(mod_psum, i * NB + b - NB + 1)
                    load(i * NB + b, b)
            sp.wait_ge(mod_row, 1)
            sp.dma_start(d["mods"], row[:]).then_inc(stored, 16)
            sp.wait_ge(stored, 16)

        @block.gpsimd
        def _(pool):
            nc.gpsimd.memset(c["ident"][:], 0.0).then_inc(zero, 1)
            nc.gpsimd.memset(c["tri"][:], -1.0).then_inc(zero, 1)
            nc.gpsimd.memset(c["keep"][:], 1.0).then_inc(zero, 1)
            nc.gpsimd.memset(c["far"][:], 0.0).then_inc(zero, 1)
            nc.gpsimd.memset(c["farc"][:], 0.0).then_inc(zero, 1)
            nc.gpsimd.memset(c["nones"][:], -1.0).then_inc(zero, 1)
            nc.gpsimd.memset(c["eps"][:], EPS).then_inc(zero, 1)
            nc.gpsimd.memset(c["fold"][:], 0.0).then_inc(zero, 1)
            nc.gpsimd.memset(c["one"][:], 1.0).then_inc(ident_ready, 1)
            pool.wait_ge(zero, 8)
            sel = nc.gpsimd.affine_select
            sel(out=c["ident"][:], in_=c["ident"][:], compare_op=ALU.not_equal, fill=1.0, base=0,
                pattern=[[-1, P]], channel_multiplier=1).then_inc(zero, 1)
            sel(out=c["tri"][:], in_=c["tri"][:], compare_op=ALU.is_ge, fill=0.0, base=0,
                pattern=[[-1, P]], channel_multiplier=1).then_inc(zero, 1)
            sel(out=c["keep"][:], in_=c["keep"][:], compare_op=ALU.is_gt, fill=0.0, base=0,
                pattern=[[1, P]], channel_multiplier=-1).then_inc(zero, 1)
            sel(out=c["far"][:], in_=c["far"][:], compare_op=ALU.is_gt, fill=FAR, base=0,
                pattern=[[1, P]], channel_multiplier=-1).then_inc(zero, 1)
            sel(out=c["farc"][:], in_=c["farc"][:], compare_op=ALU.is_ge, fill=FAR, base=0,
                pattern=[[1, P]], channel_multiplier=-1).then_inc(zero, 1)
            for n in range(2):
                pool.wait_ge(zero, 13 + n)
                sel(out=c["fold"][:], in_=c["fold"][:], compare_op=ALU.not_equal, fill=1.0, base=-SD * n,
                    pattern=[[-1, SD]], channel_multiplier=1).then_inc(zero, 1)
            pool.wait_ge(zero, 15)
            nc.gpsimd.tensor_copy(c["tri_r"][:], c["tri"][:]).then_inc(ident_ready, 1)
            nc.gpsimd.tensor_copy(c["far_r"][:], c["far"][:]).then_inc(ident_ready, 1)
            nc.gpsimd.tensor_copy(c["ident_r"][:], c["ident"][:]).then_inc(ident_ready, 1)

        @block.scalar
        def _(act):
            act.dma_start(badd[:], d["b_ada_T"]).then_inc(bias_in, 16)
            act.dma_start(n1[:], d["norm1_T"]).then_inc(bias_in, 16)
            act.dma_start(n2[:], d["norm2_T"]).then_inc(bias_in, 16)
            act.wait_ge(loaded, 16)
            nc.scalar.activation(sg[:], cT[:], ACT.Sigmoid).then_inc(sig_ready, 1)

        @block.vector
        def _(dve):
            dve.wait_ge(sig_ready, 1)
            nc.vector.tensor_tensor(sc[:], cT[:], sg[:], ALU.mult).then_inc(silu_ready, 1)
            dve.wait_ge(bias_in, 48)
            dve.wait_ge(mod_psum, NCH)
            nc.vector.tensor_tensor(c["mod"][:], pm[:, 0:96].rearrange("p (j c) -> p j c", c=2),
                                    badd[:].unsqueeze(2).to_broadcast([P, 48, 2]), ALU.add).then_inc(mod_ready, 1)
            dve.wait_ge(mod_ready, 1)
            for n, (a, w, j) in enumerate(((c["A1"], n1, 8), (c["A2"], n2, 32))):
                nc.vector.tensor_scalar(a[:], c["mod"][:, j:j + 8, :], 1.0, None, ALU.add).then_inc(lead, 1)
                dve.wait_ge(lead, n + 1)
                nc.vector.tensor_tensor(a[:], a[:], w[:].unsqueeze(2).to_broadcast([P, KD, 2]),
                                        ALU.mult).then_inc(scale1, 1)
            dve.wait_ge(mod_t, 1)
            nc.vector.tensor_copy(row[:], pr[0:96, 0:P]).then_inc(mod_row, 1)

        @block.tensor
        def _(pe):
            pe.wait_ge(silu_ready, 1)
            with pe.Fori(0, NCH // NB) as i:
                for b in range(NB):
                    pe.wait_ge(w_in[b], 16 * i + 16)
                    for j in range(4):
                        for kk in range(KD):
                            mm = nc.tensor.matmul(pm[:, bass.ds((i * NB + b) * 8 + 2 * j, 2)],
                                                  wa[:, b, kk, j * P:(j + 1) * P], sc[:, kk, :],
                                                  start=(kk == 0), stop=(kk == KD - 1))
                    mm.then_inc(mod_psum, 1)
            pe.wait_ge(mod_ready, 1)
            pe.wait_ge(ident_ready, 4)
            nc.tensor.transpose(pr[0:96, 0:P], c["mod"][:].rearrange("p j c -> p (j c)"),
                                c["ident"][:]).then_inc(mod_t, 1)


def normalise(k, c, src, scale, shift0, hH, hL, name="a"):
    nc, d = k.nc, k.d
    x_in = [k.sem("x_loaded0"), k.sem("x_loaded1")]
    ssq_ready, std_ready, rstd_ready, x_scaled, x_turned, h_full, h_high, h_low = k.sems(
        "squares_summed", "std_ready", "rstd_ready", "x_scaled", "x_turned", "h_full", "h_high", "h_low")
    with ExitStack() as s:
        x = sbuf(nc, s, name + "nx", [P, 2, D])
        sq = sbuf(nc, s, name + "nsq", [P, D])
        tmp = sbuf(nc, s, name + "ntmp", [P, 2, KD, P])
        st = sbuf(nc, s, name + "nst", [P, 2, 3])
        pT = psum(nc, s, name + "npT", [P, 2, D])
        block = s.enter_context(nc.Block())
        eps = c["eps"]

        @block.sync
        def _(sp):
            def body(t, u, r, first):
                if not first:
                    sp.wait_ge(x_turned, t - 1)
                sp.dma_start(x[:, u], src[tok(t), :]).then_inc(x_in[u], 16)
            tiles(sp, body)

        @block.scalar
        def _(act):
            def high(t, u):
                act.wait_ge(h_full, t + 1)
                nc.scalar.activation(hH[:, :, tok(t)], tmp[:, u], ACT.Copy).then_inc(h_high, 1)

            def body(t, u, r, first):
                act.wait_ge(x_in[u], 16 * r + 16)
                if not first:
                    act.wait_ge(x_scaled, t - 1)
                nc.scalar.activation(sq[:], x[:, u], ACT.Square, accum_out=st[:, u, 0:1]).then_inc(ssq_ready, 1)
                act.wait_ge(ssq_ready, t + 1)
                nc.scalar.activation(st[:, u, 1:2], st[:, u, 0:1], ACT.Sqrt, bias=eps[:],
                                     scale=1.0 / D).then_inc(std_ready, 1)
                if not (first and u == 0):
                    high(t - 1, 1 - u)
            tiles(act, body)
            high(NPT, 0)

        @block.vector
        def _(dve):
            def scale_rows(t, u):
                dve.wait_ge(std_ready, t + 1)
                nc.vector.reciprocal(st[:, u, 2:3], st[:, u, 1:2]).then_inc(rstd_ready, 1)
                dve.wait_ge(rstd_ready, t + 1)
                nc.vector.tensor_scalar(x[:, u], x[:, u], st[:, u, 2:3], None, ALU.mult).then_inc(x_scaled, 1)

            def evacuate(t, u, which=0, first=False):
                dve.wait_ge(x_turned, t + 1)
                if not first:
                    dve.wait_ge(h_high, t - 1)
                    dve.wait_ge(h_low, t - 1)
                for kk in range(KD):
                    op = nc.vector.tensor_scalar(tmp[:, u, kk], pT[:, u, kk * P:(kk + 1) * P],
                                                 scale[:, kk, which:which + 1],
                                                 c["mod"][:, shift0 + kk, which:which + 1], ALU.mult, ALU.add)
                op.then_inc(h_full, 1)

            scale_rows(0, 0)
            scale_rows(1, 1)
            evacuate(0, 0, first=True)
            scale_rows(2, 0)
            evacuate(1, 1, first=True)
            scale_rows(3, 1)
            evacuate(2, 0)
            with dve.Fori(2, NPT // 2) as i:
                scale_rows(2 * i, 0)
                evacuate(2 * i - 1, 1)
                scale_rows(2 * i + 1, 1)
                evacuate(2 * i, 0)
            scale_rows(NPT, 0)
            evacuate(NPT - 1, 1)
            evacuate(NPT, 0, which=1)

        @block.gpsimd
        def _(pool):
            def body(t, u, r, first):
                pool.wait_ge(h_high, t + 1)
                nc.gpsimd.tensor_tensor(hL[:, :, tok(t)], tmp[:, u], hH[:, :, tok(t)].bitcast(F32),
                                        ALU.subtract).then_inc(h_low, 1)
            tiles(pool, body)

        @block.tensor
        def _(pe):
            def body(t, u, r, first):
                pe.wait_ge(x_scaled, t + 1)
                if not first:
                    pe.wait_ge(h_full, t - 1)
                for kk in range(KD):
                    mm = nc.tensor.transpose(pT[:, u, kk * P:(kk + 1) * P], x[:, u, kk * P:(kk + 1) * P],
                                             c["ident"][:])
                mm.then_inc(x_turned, 1)
            tiles(pe, body)


def project(k, c, hH, hL, w_dram, group0, n_groups, out_dram, normed):
    nc, d = k.nc, k.d
    NB, NS, NR, NW = 6, 4, 4, 12
    raw_in = [k.sem(f"w_raw_loaded{n}") for n in range(NR)]
    w_high, w_low, w_used, summed, taken = k.sems("w_high", "w_low", "w_used", "projected", "psum_taken")
    stored = [k.sem(f"proj_stored{n}") for n in range(NS)]
    if normed:
        squared, reduced, std_ready, rstd_ready, scaled, weighted, norm_in, q_scaled = k.sems(
            "squared", "reduced", "std_ready", "rstd_ready", "scaled", "weighted", "norm_w_loaded", "q_weight_scaled")
    done = weighted if normed else taken
    AHEAD = NW - KD
    with ExitStack() as s:
        raw = sbuf(nc, s, f"praw{group0}", [P, NR, W5])
        wH = sbuf(nc, s, f"pwH{group0}", [P, NW, W5], F32R)
        wL = sbuf(nc, s, f"pwL{group0}", [P, NW, W5], F32R)
        stage = sbuf(nc, s, f"pstage{group0}", [P, NS, W5])
        acc = psum(nc, s, f"pacc{group0}", [P, NB, W5])
        if normed:
            nst = sbuf(nc, s, "pnst", [P, 2, 3, SH])
            nw = sbuf(nc, s, "pnw", [P, 2, SD])
            sq = psum(nc, s, "psq", [P, 2, W5])
        block = s.enter_context(nc.Block())

        def slot(eng, g, kk):
            return bass.ds(eng.snap((g * KD + kk) % NW), 1)

        def stored_before(eng, g, t):
            rank, per = t // NS, len(range(t % NS, NT, NS))
            if not (isinstance(g, int) and g == 0 and rank == 0):
                eng.wait_ge(stored[t % NS], 16 * (g * per + rank))

        @block.sync
        def _(sp):
            def load(g, kk, first=False):
                if not (first and kk < NR):
                    sp.wait_ge(w_low, g * KD + kk - NR + 1)
                sp.dma_start(raw[:, kk % NR],
                             w_dram[bass.ds(group0 + g, 1), kk * P:(kk + 1) * P, :].rearrange("o p n -> (o p) n")
                             ).then_inc(raw_in[kk % NR], 16)

            def group(g, last):
                for t in range(NT):
                    if t % 2 == 0 and t // 2 < KD and not last:
                        load(g + 1, t // 2)
                    sp.wait_ge(done, g * NT + t + 1)
                    dst = out_dram[bass.ds(group0 + g, 1), t * P:(t + 1) * P, :].rearrange("o p n -> (o p) n")
                    sp.dma_start(dst, stage[:, t % NS]).then_inc(stored[t % NS], 16)
            for kk in range(KD):
                load(0, kk, True)
            if n_groups > 1:
                with sp.Fori(0, n_groups - 1) as g:
                    group(g, False)
            group(n_groups - 1, True)
            for n in range(NS):
                sp.wait_ge(stored[n], 16 * n_groups * len(range(n, NT, NS)))

        @block.scalar
        def _(act):
            def split(g, kk, free=False):
                act.wait_ge(raw_in[kk % NR], 16 * (g * (KD // NR) + kk // NR + 1))
                if not free and kk < AHEAD:
                    act.wait_ge(summed, (g - 1) * NT)
                elif not free:
                    act.wait_ge(w_used, (g - 1) * (KD - AHEAD) + kk - AHEAD + 1)
                nc.scalar.activation(wH[:, slot(act, g, kk), :], raw[:, kk % NR].unsqueeze(1),
                                     ACT.Copy).then_inc(w_high, 1)

            def take(g, t):
                stored_before(act, g, t)
                act.wait_ge(summed, g * NT + t + 1)
                nc.scalar.activation(stage[:, t % NS], acc[:, t % NB], ACT.Copy).then_inc(taken, 1)

            def std(g, t):
                act.wait_ge(reduced, g * NT + t + 1)
                nc.scalar.activation(nst[:, t % 2, 1], nst[:, t % 2, 0], ACT.Sqrt, bias=c["eps"][:],
                                     scale=1.0 / SD).then_inc(std_ready, 1)

            def group(g, last, first=False):
                for t in range(NT):
                    take(g, t)
                    if normed:
                        std(g, t)
                    if t % 2 == 1 and t // 2 < AHEAD and not last:
                        split(g + 1, t // 2, free=first)
                if not last:
                    for kk in range(AHEAD, KD):
                        split(g + 1, kk)
            for kk in range(KD):
                split(0, kk, free=True)
            group(0, n_groups == 1, first=True)
            if n_groups > 2:
                with act.Fori(1, n_groups - 1) as g:
                    group(g, False)
            if n_groups > 1:
                group(n_groups - 1, True)

        @block.gpsimd
        def _(pool):
            if normed:
                pool.dma_start(nw[:], d["sb_norms"]).then_inc(norm_in, 16)
            with pool.Fori(0, n_groups) as g:
                for kk in range(KD):
                    pool.wait_ge(w_high, g * KD + kk + 1)
                    at = slot(pool, g, kk)
                    nc.gpsimd.tensor_tensor(wL[:, at, :], raw[:, kk % NR].unsqueeze(1),
                                            wH[:, at, :].bitcast(F32), ALU.subtract).then_inc(w_low, 1)

        if normed:
            @block.vector
            def _(dve):
                dve.wait_ge(norm_in, 16)
                nc.vector.tensor_scalar(nw[:, 0], nw[:, 0], SD ** -0.5, None, ALU.mult).then_inc(q_scaled, 1)
                dve.wait_ge(q_scaled, 1)
                with dve.Fori(0, n_groups) as g:
                    for t in range(NT):
                        n = g * NT + t
                        st = stage[:, t % NS]
                        heads = st.rearrange("p (h e) -> p h e", e=SD)
                        dve.wait_ge(taken, n + 1)
                        nc.vector.tensor_tensor(sq[:, t % 2], st, st, ALU.mult).then_inc(squared, 1)
                        dve.wait_ge(squared, n + 1)
                        nc.vector.tensor_reduce(nst[:, t % 2, 0], sq[:, t % 2].rearrange("p (h e) -> p h e", e=SD),
                                                AX.X, ALU.add).then_inc(reduced, 1)
                        dve.wait_ge(std_ready, n + 1)
                        nc.vector.reciprocal(nst[:, t % 2, 2], nst[:, t % 2, 1]).then_inc(rstd_ready, 1)
                        dve.wait_ge(rstd_ready, n + 1)
                        nc.vector.tensor_tensor(heads, heads, nst[:, t % 2, 2].unsqueeze(2).to_broadcast([P, SH, SD]),
                                                ALU.mult).then_inc(scaled, 1)
                        dve.wait_ge(scaled, n + 1)
                        nc.vector.tensor_tensor(heads, heads, nw[:, bass.ds(g, 1), :].to_broadcast([P, SH, SD]),
                                                ALU.mult).then_inc(weighted, 1)

        @block.tensor
        def _(pe):
            def group(g, first):
                at = [slot(pe, g, kk) for kk in range(KD)]
                for t in range(NT):
                    if t >= NB:
                        pe.wait_ge(taken, g * NT + t - NB + 1)
                    elif t == 0 and not first:
                        pe.wait_ge(taken, g * NT)
                    for kk in range(KD):
                        if t == 0:
                            pe.wait_ge(w_high, g * KD + kk + 1)
                            pe.wait_ge(w_low, g * KD + kk + 1)
                        for n, (a, w) in enumerate(((hH, wH), (hL, wH), (hH, wL))):
                            mm = nc.tensor.matmul(acc[:, t % NB].unsqueeze(1), a[:, kk, t * P:(t + 1) * P],
                                                  w[:, at[kk], :], start=(kk == 0 and n == 0),
                                                  stop=(kk == KD - 1 and n == 2))
                        if t == NT - 1 and kk < KD - AHEAD:
                            mm.then_inc(w_used, 1)
                    mm.then_inc(summed, 1)
            group(0, True)
            if n_groups > 1:
                with pe.Fori(1, n_groups) as g:
                    group(g, False)


def project_gates(k, c, hH, hL):
    nc, d = k.nc, k.d
    raw_in, high, low, summed, taken, stored = k.sems("wg_loaded", "wg_high", "wg_low", "gates_summed", "gates_taken",
                                                      "gates_stored")
    spans = [(n * W5, W5) for n in range(SEQ // W5)] + [(SEQ, P)]
    with ExitStack() as s:
        raw = sbuf(nc, s, "graw", [P, KD, 8])
        wH = sbuf(nc, s, "gwH", [P, KD, 8], F32R)
        wL = sbuf(nc, s, "gwL", [P, KD, 8], F32R)
        out = sbuf(nc, s, "gout", [8, TOK])
        acc = psum(nc, s, "gacc", [8, 5, W5])
        block = s.enter_context(nc.Block())

        @block.sync
        def _(sp):
            sp.dma_start(raw[:], d["w_gate"].rearrange("(k p) n -> p k n", p=P)).then_inc(raw_in, 16)
            sp.wait_ge(taken, len(spans))
            sp.dma_start(d["gates_d"], out[:]).then_inc(stored, 16)
            sp.wait_ge(stored, 16)

        @block.vector
        def _(dve):
            dve.wait_ge(raw_in, 16)
            nc.vector.tensor_copy(wH[:], raw[:]).then_inc(high, 1)
            dve.wait_ge(high, 1)
            nc.vector.tensor_tensor(wL[:], raw[:], wH[:].bitcast(F32), ALU.subtract).then_inc(low, 1)
            for n, (a, w) in enumerate(spans):
                dve.wait_ge(summed, n + 1)
                nc.vector.tensor_copy(out[:, a:a + w], acc[:, n, 0:w]).then_inc(taken, 1)

        @block.tensor
        def _(pe):
            pe.wait_ge(low, 1)
            for n, (a, w) in enumerate(spans):
                for kk in range(KD):
                    for m, (wt, h) in enumerate(((wH, hH), (wH, hL), (wL, hH))):
                        mm = nc.tensor.matmul(acc[:, n, 0:w], wt[:, kk], h[:, kk, a:a + w],
                                              start=(kk == 0 and m == 0), stop=(kk == KD - 1 and m == 2))
                mm.then_inc(summed, 1)


def attention_operands(k, c):
    nc, d = k.nc, k.d
    NBLK = NT + NPB
    loaded = [k.sem("qkv_loaded0"), k.sem("qkv_loaded1")]
    q_stored = [k.sem("q_stored0"), k.sem("q_stored1")]
    kv_stored = [k.sem("kv_stored0"), k.sem("kv_stored1")]
    high, low, turned, taken_k, taken_q, qscaled = k.sems("qkv_high", "qkv_low", "qk_turned", "k_taken", "q_taken", "q_x")
    with ExitStack() as s:
        x = sbuf(nc, s, "ox", [P, 2, 3, W5])
        parts = sbuf(nc, s, "oparts", [P, 2, 3, SH, 3, SD], F32R)
        kT = sbuf(nc, s, "okT", [P, 2, SH, P], F32R)
        qT = sbuf(nc, s, "oqT", [P, 2, SH, 2, P], F32R)
        pT = psum(nc, s, "opT", [P, 3, SH * P])
        block = s.enter_context(nc.Block())

        def blocks(eng, body):
            body(0, 0, 0, True, False)
            body(1, 1, 0, True, False)
            with eng.Fori(1, NPT // 2) as i:
                body(2 * i, 0, i, False, False)
                body(2 * i + 1, 1, i, False, False)
            body(NPT, 0, NPT // 2, False, False)
            with eng.Fori(NPT // 2, NPT // 2 + NPB // 2) as i:
                body(2 * i + 1, 1, i, False, True)
                body(2 * i + 2, 0, i + 1, False, True)

        @block.sync
        def _(sp):
            def body(b, u, r, first, cache):
                if not first:
                    sp.wait_ge(low, b - 1)
                if cache:
                    rows = bass.ds((b - NT) * P, P)
                    sp.dma_start(x[:, u, 1], d["past_k"][rows, :]).then_inc(loaded[u], 16)
                    sp.dma_start(x[:, u, 2], d["past_v"][rows, :]).then_inc(loaded[u], 16)
                    sp.dma_start(x[:, u, 0], d["past_k"][rows, :]).then_inc(loaded[u], 16)
                else:
                    for n, g in enumerate((5, 6, 4)):
                        sp.dma_start(x[:, u, n], d["proj_out"][g, tok(b), :]).then_inc(loaded[u], 16)
            blocks(sp, body)

        @block.scalar
        def _(act):
            def body(b, u, r, first, cache):
                act.wait_ge(loaded[u], 48 * r + 48)
                if not first:
                    act.wait_ge(turned, b - 1)
                    at_least(act, q_stored[u], 16 * r)
                    at_least(act, kv_stored[u], 32 * r)
                nc.scalar.activation(parts[:, u, :, :, 0, :], x[:, u].rearrange("p n (h e) -> p n h e", e=SD),
                                     ACT.Copy).then_inc(high, 1)
                nc.scalar.activation(parts[:, u, 0, :, 2, :], x[:, u, 0].rearrange("p (h e) -> p h e", e=SD),
                                     ACT.Copy).then_inc(high, 1)
                act.wait_ge(turned, b + 1)
                for n in range(2):
                    op = nc.scalar.activation(qT[:, u, :, n, :], pT[:, 1 + n].rearrange("p (h e) -> p h e", e=P),
                                              ACT.Copy)
                op.then_inc(taken_q, 1)
                act.wait_ge(taken_q, b + 1)
                act.dma_start(d["q_d"][:, bass.ds(b, 1), :, :].rearrange("h o p n -> p (h o) n"),
                              qT[:, u].rearrange("p h n e -> p h (n e)").bitcast(F32)).then_inc(q_stored[u], 16)
            blocks(act, body)

        @block.vector
        def _(dve):
            def body(b, u, r, first, cache):
                dve.wait_ge(high, 2 * b + 2)
                nc.vector.tensor_tensor(parts[:, u, :, :, 1, :], x[:, u].rearrange("p n (h e) -> p n h e", e=SD),
                                        parts[:, u, :, :, 0, :].bitcast(F32), ALU.subtract).then_inc(low, 1)
                dve.wait_ge(turned, b + 1)
                if not first:
                    at_least(dve, kv_stored[u], 32 * r)
                nc.vector.tensor_copy(kT[:, u], pT[:, 0].rearrange("p (h e) -> p h e", e=P)).then_inc(taken_k, 1)
            blocks(dve, body)

        @block.gpsimd
        def _(pool):
            def body(b, u, r, first, cache):
                pool.wait_ge(low, b + 1)
                pool.dma_start(d["kv_d"][:, bass.ds(b, 1), :, P:2 * P].rearrange("h o p n -> p (h o) n"),
                               parts[:, u, 2, :, 0:2, :].rearrange("p h n e -> p h (n e)").bitcast(F32)).then_inc(kv_stored[u], 16)
                pool.wait_ge(taken_k, b + 1)
                pool.dma_start(d["kv_d"][:, bass.ds(b, 1), :, 0:P].rearrange("h o p n -> p (h o) n"),
                               kT[:, u].bitcast(F32)).then_inc(kv_stored[u], 16)
            blocks(pool, body)
            for u, n in enumerate((NBLK - NBLK // 2, NBLK // 2)):
                pool.wait_ge(q_stored[u], 16 * n)
                pool.wait_ge(kv_stored[u], 32 * n)

        @block.tensor
        def _(pe):
            def body(b, u, r, first, cache):
                pe.wait_ge(low, b + 1)
                if not (first and u == 0):
                    pe.wait_ge(taken_k, b)
                    pe.wait_ge(taken_q, b)
                for n, (which, a) in enumerate(((1, 0), (0, 0), (0, 1))):
                    for h in range(SH):
                        mm = nc.tensor.transpose(pT[:, n, h * P:(h + 1) * P],
                                                 parts[:, u, which, h, a:a + 2, :].rearrange("p n e -> p (n e)").bitcast(F32),
                                                 c["ident"][:])
                mm.then_inc(turned, 1)
            blocks(pe, body)


def attention(k, c):
    nc, d = k.nc, k.d
    NG = SEQ // W5
    steps = [(T, b) for T in reversed(range(NG)) for b in reversed(range(4 * T + 4))]
    N = len(steps)
    NZ = 5
    q_in = [k.sem(f"q_loaded{n}") for n in range(NG)]
    (z_ready, e_ready, l_ready, sp_ready, high, low, later_ready, zeroed, z_full, a_ready, ah_ready, al_ready, av_done,
     o_taken, folded, fold_taken, raw_sp, z_bound) = k.sems(
        "z_ready", "exp_ready", "ln_ready", "softplus_ready", "softplus_high", "softplus_low", "later_sum_ready",
        "later_sum_zeroed", "exponent_ready", "a_ready", "a_high", "a_low", "av_done",
        "o_taken", "o_folded", "fold_taken", "softplus_raw", "z_bounded")
    stored = [k.sem("o_stored0"), k.sem("o_stored1")]
    with ExitStack() as s:
        q = sbuf(nc, s, "aq", [P, SEQ // P, 2, P], F32R)
        kv = sbuf(nc, s, "akv", [P, SEQ // P, 2, P], F32R)
        ring = {n: sbuf(nc, s, f"a{n}", [P, 2, W5], dt) for n, dt in (
            ("E", F32), ("L", F32), ("SP", F32), ("SH", F32R), ("SL", F32R), ("A", F32), ("AH", F32R), ("AL", F32R),
            ("CA", F32), ("O", F32))}
        of = sbuf(nc, s, "aof", [P, 2, 4, SD])
        Z = psum(nc, s, "a_z", [P, NZ, W5])
        O = psum(nc, s, "a_out", [P, 2, W5])
        F = psum(nc, s, "a_fold", [P, 4, SD])
        block = s.enter_context(nc.Block())
        last = {m: T for m, (T, b) in enumerate(steps) if b == 0}
        first = {m: T for m, (T, b) in enumerate(steps) if b == 4 * T + 3}

        def cols(m):
            T, b = steps[m]
            return slice(max(0, b - 4 * T) * P, W5)

        def own(m):
            T, b = steps[m]
            return slice((b - 4 * T) * P, (b - 4 * T + 1) * P) if b >= 4 * T else None

        def freed(eng, sem, B, m, R):
            at_least(eng, sem, B + max(m - R + 1, 0))

        def run(eng, body):
            body(0)
            with eng.Fori(1, SH) as h:
                body(h)

        def pipeline(ops):
            most, least = max(a for _, a in ops), min(a for _, a in ops)
            for n in range(-most, N - least):
                for op, lead in ops:
                    if 0 <= n + lead < N:
                        op(n + lead)

        @block.sync
        def _(sp):
            def load(h, G):
                src = lambda x: x[bass.ds(h, 1), 4 * G:4 * G + 4, :, :].rearrange("o b p n -> p (o b) n")
                if not isinstance(h, int):
                    sp.wait_ge(av_done, (h - 1) * N + max(m for m in last if last[m] == G) + 1)
                sp.dma_start(q[:, 4 * G:4 * G + 4].rearrange("p b n e -> p b (n e)").bitcast(F32), src(d["q_d"])).then_inc(q_in[G], 16)
                sp.dma_start(kv[:, 4 * G:4 * G + 4].rearrange("p b n e -> p b (n e)").bitcast(F32), src(d["kv_d"])).then_inc(q_in[G], 16)
            for G in reversed(range(NG)):
                load(0, G)

            def body(h, more):
                for n, G in enumerate(reversed(range(NG))):
                    if more:
                        load(h + 1, G)
                    sp.wait_ge(fold_taken, h * NG + n + 1)
                    dst = d["o_d"][bass.ds(G * W5, W5), bass.ds(h * SD, SD)].rearrange("(j p) e -> p j e", p=P)
                    sp.dma_start(dst, of[:, n % 2]).then_inc(stored[n % 2], 16)
            with sp.Fori(0, SH - 1) as h:
                body(h, True)
            body(SH - 1, False)
            for n in range(2):
                sp.wait_ge(stored[n], 16 * SH * NG // 2)

        @block.scalar
        def _(act):
            def body(h):
                B = h * N

                def E(m):
                    act.wait_ge(z_bound, B + m + 1)
                    at = ring["E"][:, m % 2, cols(m)]
                    nc.scalar.activation(at, at, ACT.Exp).then_inc(e_ready, 1)

                def L(m):
                    act.wait_ge(e_ready, B + m + 1)
                    freed(act, raw_sp, B, m, 2)
                    nc.scalar.activation(ring["L"][:, m % 2, cols(m)], ring["E"][:, m % 2, cols(m)], ACT.Ln,
                                         bias=1.0).then_inc(l_ready, 1)

                def A(m):
                    act.wait_ge(z_full, B + m + 1)
                    freed(act, al_ready, B, m, 2)
                    nc.scalar.activation(ring["A"][:, m % 2, cols(m)], Z[:, m % NZ, cols(m)], ACT.Exp).then_inc(a_ready, 1)
                    freed(act, av_done, B, m, 2)
                    nc.scalar.activation(ring["AH"][:, m % 2, cols(m)], Z[:, m % NZ, cols(m)], ACT.Exp).then_inc(ah_ready, 1)
                pipeline([(E, 2), (L, 2), (A, 0)])
            act.preload_act_table_set("natural_log_exp_and_others")
            run(act, body)

        @block.vector
        def _(dve):
            def body(h):
                B = h * N

                def SP(m):
                    dve.wait_ge(l_ready, B + m + 1)
                    freed(dve, later_ready, B, m, 2)
                    freed(dve, low, B, m, 2)
                    freed(dve, high, B, m, 2)
                    at = ring["SP"][:, m % 2]
                    nc.vector.tensor_tensor(at[:, cols(m)], ring["L"][:, m % 2, cols(m)], Z[:, m % NZ, cols(m)],
                                            ALU.max).then_inc(raw_sp, 1)
                    if own(m):
                        dve.wait_ge(raw_sp, B + m + 1)
                        nc.vector.tensor_tensor(at[:, own(m)], at[:, own(m)], c["keep"][:], ALU.mult).then_inc(sp_ready, 1)

                def BOUND(m):
                    dve.wait_ge(z_ready, B + m + 1)
                    freed(dve, l_ready, B, m, 2)
                    nc.vector.tensor_scalar(ring["E"][:, m % 2, cols(m)], Z[:, m % NZ, cols(m)], 41.0, None,
                                            ALU.min).then_inc(z_bound, 1)

                def LO(m):
                    dve.wait_ge(high, B + m + 1)
                    freed(dve, z_full, B, m, 2)
                    nc.vector.tensor_tensor(ring["SL"][:, m % 2, cols(m)], ring["SP"][:, m % 2, cols(m)],
                                            ring["SH"][:, m % 2, cols(m)].bitcast(F32), ALU.subtract).then_inc(low, 1)

                def AL(m):
                    dve.wait_ge(a_ready, B + m + 1)
                    dve.wait_ge(ah_ready, B + m + 1)
                    freed(dve, av_done, B, m, 2)
                    nc.vector.tensor_tensor(ring["AL"][:, m % 2, cols(m)], ring["A"][:, m % 2, cols(m)],
                                            ring["AH"][:, m % 2, cols(m)].bitcast(F32), ALU.subtract).then_inc(al_ready, 1)

                def OUT(m):
                    if m in last:
                        n = NG - 1 - last[m]
                        g = h * NG + n
                        dve.wait_ge(av_done, B + m + 1)
                        if n >= 1:
                            dve.wait_ge(folded, g)
                        nc.vector.tensor_copy(ring["O"][:, n % 2], O[:, n % 2]).then_inc(o_taken, 1)
                        dve.wait_ge(folded, g + 1)
                        at_least(dve, stored[n % 2], 16 * (h * (NG // 2) + n // 2))
                        nc.vector.tensor_copy(of[:, n % 2], F[:]).then_inc(fold_taken, 1)
                pipeline([(SP, 1), (LO, 1), (AL, -1), (BOUND, 3), (OUT, -2)])
            run(dve, body)

        @block.gpsimd
        def _(pool):
            def body(h):
                B = h * N
                ones = lambda n: c["one"][:].to_broadcast([P, n])
                masked = [sum(own(x) is not None for x in range(m + 1)) for m in range(N)]

                def HI(m):
                    pool.wait_ge(raw_sp, B + m + 1)
                    at_least(pool, sp_ready, h * masked[-1] + masked[m])
                    freed(pool, z_full, B, m, 2)
                    sp = ring["SP"][:, m % 2]
                    nc.gpsimd.tensor_tensor(ring["SH"][:, m % 2, cols(m)], sp[:, cols(m)], ones(W5 - cols(m).start),
                                            ALU.mult).then_inc(high, 1)
                    if m > 0:
                        pool.wait_ge(later_ready, B + m)
                        freed(pool, z_full, B, m, 1)
                    sums = ring["CA"][:, (m + 1) % 2]
                    rest = slice(cols(m).start + (P if own(m) else 0), W5)
                    if own(m):
                        op = nc.gpsimd.tensor_tensor(sums[:, own(m)], sp[:, own(m)], ones(P), ALU.mult)
                    if rest.start < W5:
                        op = nc.gpsimd.tensor_tensor(sums[:, rest], ring["CA"][:, m % 2, rest], sp[:, rest], ALU.add)
                    op.then_inc(later_ready, 1)
                pipeline([(HI, 1)])
            run(pool, body)

        @block.tensor
        def _(pe):
            def body(h):
                B = h * N

                def z(m):
                    T, b = steps[m]
                    if m < N and T == NG - 1 and b % 4 == 3:
                        pe.wait_ge(q_in[b // 4], 32 * h + 32)
                    freed(pe, ah_ready, B, m, NZ)
                    span = slice(4 * T * P + cols(m).start, 4 * T * P + W5)
                    t0, n = span.start // P, (span.stop - span.start) // P
                    for part in range(2):
                        mm = nc.tensor.matmul(Z[:, m % NZ, cols(m)], kv[:, b, 0, :], q[:, t0:t0 + n, part, :],
                                              start=(part == 0), stop=(part == 1))
                    mm.then_inc(z_ready, 1)

                def sub(m):
                    go = dict(start=False, stop=True, skip_group_check=True)
                    at = Z[:, m % NZ]
                    pe.wait_ge(raw_sp, B + m + 1)
                    if m not in first:
                        rest = slice(cols(m).start + (P if own(m) else 0), W5)
                        pe.wait_ge(later_ready, B + m)
                        nc.tensor.matmul(at[:, rest], c["nones"][:], ring["CA"][:, m % 2, rest], **go)
                    if own(m):
                        nc.tensor.matmul(at[:, own(m)], c["ident_r"][:], c["far_r"][:], **go)
                    pe.wait_ge(high, B + m + 1)
                    nc.tensor.matmul(at[:, cols(m)], c["tri_r"][:], ring["SH"][:, m % 2, cols(m)], **go)
                    pe.wait_ge(low, B + m + 1)
                    nc.tensor.matmul(at[:, cols(m)], c["tri_r"][:], ring["SL"][:, m % 2, cols(m)], **go).then_inc(z_full, 1)

                def av(m):
                    T, b = steps[m]
                    n = NG - 1 - T
                    if m in first:
                        at_least(pe, o_taken, h * NG + max(n - 1, 0))
                    pe.wait_ge(ah_ready, B + m + 1)
                    go = dict(skip_group_check=True)
                    nc.tensor.matmul(O[:, n % 2, cols(m)], kv[:, b, 1, :], ring["AH"][:, m % 2, cols(m)],
                                     start=(m in first), stop=False, **go)
                    pe.wait_ge(al_ready, B + m + 1)
                    nc.tensor.matmul(O[:, n % 2, cols(m)], kv[:, b, 1, :], ring["AL"][:, m % 2, cols(m)],
                                     start=False, stop=(m in last), **go).then_inc(av_done, 1)

                def fold(m):
                    if m not in last:
                        return
                    n = NG - 1 - last[m]
                    pe.wait_ge(o_taken, h * NG + n + 1)
                    at_least(pe, fold_taken, h * NG + n)
                    for j in range(4):
                        mm = nc.tensor.matmul(F[:, j, :], ring["O"][:, n % 2, j * P:(j + 1) * P], c["fold"][:],
                                              start=(j == 0), stop=True, skip_group_check=True)
                    mm.then_inc(folded, 1)
                pipeline([(z, 4), (sub, 0), (av, -2), (fold, -3)])
            run(pe, body)


def attention_sample(k, c):
    nc, d = k.nc, k.d
    N, NZ, W = NPB + 1, 3, SH * DEC
    (q_in, kv_in, z_ready, z_bound, e_ready, l_ready, sp_raw, sp_ready, high, low, later_ready, z_full, a_ready, ah_ready,
     al_ready, av_done, zeroed, o_taken, folded, fold_taken, stored) = k.sems(
        "q_loaded", "kv_loaded", "z_ready", "z_bounded", "exp_ready", "ln_ready", "softplus_raw", "softplus_ready",
        "softplus_high", "softplus_low", "later_sum_ready", "exponent_ready", "a_ready", "a_high", "a_low", "av_done",
        "zeroed", "o_taken", "o_folded", "fold_taken", "o_stored")
    with ExitStack() as s:
        q = sbuf(nc, s, "bq", [P, SH, 2, P], F32R)
        kv = sbuf(nc, s, "bkv", [P, SH, N, 2, P], F32R)
        ring = {n: sbuf(nc, s, f"b{n}", [P, 2, W], dt) for n, dt in (
            ("E", F32), ("L", F32), ("SP", F32), ("SH", F32R), ("SL", F32R), ("A", F32), ("AH", F32R), ("AL", F32R),
            ("CA", F32))}
        Osb = sbuf(nc, s, "bO", [P, W])
        out = sbuf(nc, s, "bout", [P, W5])
        Z = psum(nc, s, "b_z", [P, NZ, W5])
        O = psum(nc, s, "b_out", [P, W5])
        F = psum(nc, s, "b_fold", [DEC, W5])
        block = s.enter_context(nc.Block())
        heads = lambda ap: ap.rearrange("p (h t) -> p h t", t=DEC)
        over_heads = lambda ap: ap[:, 0:DEC].unsqueeze(1).to_broadcast([P, SH, DEC])
        col = lambda h: slice(h * DEC, (h + 1) * DEC)

        @block.sync
        def _(sp):
            sp.dma_start(q[:].rearrange("p h n e -> p h (n e)").bitcast(F32),
                         d["q_d"][:, NPT].rearrange("h p n -> p h n")).then_inc(q_in, 16)
            for h in range(SH):
                sp.dma_start(kv[:, h].rearrange("p b n e -> p b (n e)").bitcast(F32),
                             d["kv_d"][h, NPT:].rearrange("b p n -> p b n")).then_inc(kv_in, 16)
            sp.wait_ge(fold_taken, 1)
            sp.dma_start(d["o_d"][SEQ:, :], out[:]).then_inc(stored, 16)
            sp.wait_ge(stored, 16)

        def blk(m):
            return 0 if m == 0 else NPB + 1 - m

        @block.scalar
        def _(act):
            act.preload_act_table_set("natural_log_exp_and_others")
            for m in range(N + 1):
                if m < N:
                    act.wait_ge(z_bound, m + 1)
                    at = ring["E"][:, m % 2]
                    nc.scalar.activation(at, at, ACT.Exp).then_inc(e_ready, 1)
                    act.wait_ge(e_ready, m + 1)
                    if m >= 2:
                        act.wait_ge(sp_raw, m - 1)
                    nc.scalar.activation(ring["L"][:, m % 2], at, ACT.Ln, bias=1.0).then_inc(l_ready, 1)
                n = m - 1
                if n >= 0:
                    act.wait_ge(z_full, n + 1)
                    if n >= 2:
                        act.wait_ge(al_ready, n - 1)
                        act.wait_ge(av_done, n - 1)
                    nc.scalar.activation(ring["A"][:, n % 2], Z[:, n % NZ, 0:W], ACT.Exp).then_inc(a_ready, 1)
                    nc.scalar.activation(ring["AH"][:, n % 2], Z[:, n % NZ, 0:W], ACT.Exp).then_inc(ah_ready, 1)

        @block.vector
        def _(dve):
            v = nc.vector

            def bound(m):
                dve.wait_ge(z_ready, m + 1)
                if m >= 2:
                    dve.wait_ge(l_ready, m - 1)
                v.tensor_scalar(ring["E"][:, m % 2], Z[:, m % NZ, 0:W], 41.0, None, ALU.min).then_inc(z_bound, 1)
            bound(0)
            for m in range(N):
                if m + 1 < N:
                    bound(m + 1)
                at = ring["SP"][:, m % 2]
                dve.wait_ge(l_ready, m + 1)
                if m >= 2:
                    dve.wait_ge(later_ready, m - 1)
                    dve.wait_ge(low, m - 1)
                    dve.wait_ge(high, m - 1)
                v.tensor_tensor(at, ring["L"][:, m % 2], Z[:, m % NZ, 0:W], ALU.max).then_inc(sp_raw, 1)
                if m == 0:
                    dve.wait_ge(sp_raw, 1)
                    v.tensor_tensor(heads(at), heads(at), over_heads(c["keep"]), ALU.mult).then_inc(sp_ready, 1)
                dve.wait_ge(high, m + 1)
                if m >= 2:
                    dve.wait_ge(z_full, m - 1)
                v.tensor_tensor(ring["SL"][:, m % 2], at, ring["SH"][:, m % 2].bitcast(F32), ALU.subtract).then_inc(low, 1)
                dve.wait_ge(ah_ready, m + 1)
                dve.wait_ge(a_ready, m + 1)
                if m >= 2:
                    dve.wait_ge(av_done, m - 1)
                v.tensor_tensor(ring["AL"][:, m % 2], ring["A"][:, m % 2], ring["AH"][:, m % 2].bitcast(F32),
                                ALU.subtract).then_inc(al_ready, 1)
            dve.wait_ge(av_done, N)
            v.tensor_copy(Osb[:], O[:, 0:W]).then_inc(o_taken, 1)
            dve.wait_ge(folded, 1)
            dve.wait_ge(zeroed, 2)
            v.tensor_copy(out[0:DEC, :], F[:]).then_inc(fold_taken, 1)

        @block.gpsimd
        def _(pool):
            g = nc.gpsimd
            g.memset(ring["CA"][:], 0.0).then_inc(zeroed, 1)
            g.memset(out[:], 0.0).then_inc(zeroed, 1)
            pool.wait_ge(zeroed, 2)
            for m in range(N):
                pool.wait_ge(sp_raw, m + 1)
                pool.wait_ge(sp_ready, 1)
                if m >= 2:
                    pool.wait_ge(z_full, m - 1)
                g.tensor_copy(ring["SH"][:, m % 2], ring["SP"][:, m % 2]).then_inc(high, 1)
                if m > 0:
                    pool.wait_ge(later_ready, m)
                    pool.wait_ge(z_full, m)
                g.tensor_tensor(ring["CA"][:, (m + 1) % 2], ring["CA"][:, m % 2], ring["SP"][:, m % 2],
                                ALU.add).then_inc(later_ready, 1)

        @block.tensor
        def _(pe):
            mm = nc.tensor.matmul
            go = dict(start=False, stop=True, skip_group_check=True)

            def z(m):
                if m >= NZ:
                    pe.wait_ge(ah_ready, m - NZ + 1)
                for h in range(SH):
                    for part in range(2):
                        op = mm(Z[:, m % NZ, col(h)], kv[:, h, blk(m), 0, :], q[:, h, part, 0:DEC],
                                start=(h == 0 and part == 0), stop=(part == 1), skip_group_check=True)
                op.then_inc(z_ready, 1)

            def av(m):
                for n, (src, sem) in enumerate((("AH", ah_ready), ("AL", al_ready))):
                    pe.wait_ge(sem, m + 1)
                    for h in range(SH):
                        op = mm(O[:, col(h)], kv[:, h, blk(m), 1, :], ring[src][:, m % 2, col(h)],
                                start=(m == 0 and n == 0 and h == 0), stop=(m == N - 1 and n == 1),
                                skip_group_check=True)
                op.then_inc(av_done, 1)
            pe.wait_ge(q_in, 16)
            pe.wait_ge(kv_in, 16 * SH)
            z(0)
            for m in range(N):
                if m + 1 < N:
                    z(m + 1)
                if m > 0:
                    av(m - 1)
                at = Z[:, m % NZ, 0:W]
                pe.wait_ge(sp_raw, m + 1)
                if m > 0:
                    pe.wait_ge(later_ready, m)
                    mm(at, c["nones"][:], ring["CA"][:, m % 2], **go)
                else:
                    for h in range(SH):
                        mm(Z[:, 0, col(h)], c["ident_r"][:], c["far_r"][:, 0:DEC], **go)
                pe.wait_ge(high, m + 1)
                mm(at, c["tri_r"][:], ring["SH"][:, m % 2], **go)
                pe.wait_ge(low, m + 1)
                mm(at, c["tri_r"][:], ring["SL"][:, m % 2], **go).then_inc(z_full, 1)
            av(N - 1)
            pe.wait_ge(o_taken, 1)
            for h in range(SH):
                op = mm(F[:, h * SD:(h + 1) * SD], Osb[:, col(h)], c["fold"][:], start=(h == 0), stop=True,
                        skip_group_check=True)
            op.then_inc(folded, 1)


def gate_rows(k, c, gc, dec):
    nc, d = k.nc, k.d
    (loaded, mask_ready, biased, abs_ready, e_ready, l_ready, lf_ready, padded, b_ready, m_ready, mp_ready, u_ready, args_ready,
     w_ready, stored, zeroed, turned, taken, dec_args, dec_sum) = k.sems(
        "gates_loaded", "chunk_mask_ready", "gates_biased", "abs_ready", "exp_ready", "ln_ready", "log_forget_ready",
        "padding_set", "b_ready", "m_ready", "m_before_ready", "u_ready", "arguments_ready", "weights_ready", "rows_stored",
        "rows_zeroed", "weights_turned", "weights_taken", "decay_rows", "decay_sum")
    with ExitStack() as s:
        def row(name):
            return sbuf(nc, s, name, [MH, NT, P])
        IG, FG, AB, LF, B, M, U, G, cm = map(row, ("rIG", "rFG", "rAB", "rLF", "rB", "rM", "rU", "rG", "rcm"))
        gb = sbuf(nc, s, "rgb", [MH, 2])
        m0 = sbuf(nc, s, "rm0", [MH, 1])
        mp = sbuf(nc, s, "rmp", [MH, NT])
        dl = sbuf(nc, s, "rdl", [MH, NT])
        W = sbuf(nc, s, "rW", [96, NT, P])
        dd = sbuf(nc, s, "rdd", [MH, NT, MH])
        pw = psum(nc, s, "rpw", [P, 4, W5])
        pd = psum(nc, s, "rpd", [P, W5])
        block = s.enter_context(nc.Block())
        flat = lambda x: x[:].rearrange("h n t -> h (n t)")
        bc = lambda x: x.unsqueeze(2).to_broadcast([MH, NT, P])

        @block.sync
        def _(sp):
            sp.dma_start(flat(IG), d["gates_d"][0:MH, :]).then_inc(loaded, 16)
            sp.dma_start(flat(FG), d["gates_d"][MH:2 * MH, :]).then_inc(loaded, 16)
            sp.dma_start(gb[:], d["b_gates"]).then_inc(loaded, 16)
            sp.dma_start(m0[:], d["m_init"]).then_inc(loaded, 16)
            sp.wait_ge(u_ready, 2)
            sp.dma_start(d["ug_d"][0], flat(G)).then_inc(stored, 16)
            sp.dma_start(d["ug_d"][1], flat(U)).then_inc(stored, 16)
            sp.dma_start(d["m_out"][0], M[:, NPT - 1, P - 1:P]).then_inc(stored, 16)
            sp.dma_start(d["m_out"][1], M[:, NT - 1, P - 1:P]).then_inc(stored, 16)
            sp.wait_ge(stored, 64)

        @block.gpsimd
        def _(pool):
            nc.gpsimd.memset(cm[:], 1.0).then_inc(mask_ready, 1)
            pool.wait_ge(mask_ready, 1)
            nc.gpsimd.memset(cm[:, :, 0:1], 0.0).then_inc(mask_ready, 1)
            nc.gpsimd.memset(W[:], 0.0).then_inc(zeroed, 1)

        @block.scalar
        def _(act):
            act.preload_act_table_set("natural_log_exp_and_others")
            act.wait_ge(abs_ready, 1)
            nc.scalar.activation(AB[:], AB[:], ACT.Exp, scale=-1.0).then_inc(e_ready, 1)
            act.wait_ge(e_ready, 1)
            nc.scalar.activation(AB[:], AB[:], ACT.Ln, bias=1.0).then_inc(l_ready, 1)
            act.wait_ge(zeroed, 1)
            act.wait_ge(m_ready, 2)
            nc.scalar.activation(W[64:64 + MH], M[:], ACT.Exp, scale=-1.0).then_inc(w_ready, 1)
            act.wait_ge(args_ready, 1)
            nc.scalar.activation(W[0:MH], IG[:], ACT.Exp).then_inc(w_ready, 1)
            act.wait_ge(args_ready, 2)
            nc.scalar.activation(W[32:32 + MH], FG[:], ACT.Exp).then_inc(w_ready, 1)

        @block.vector
        def _(dve):
            v = nc.vector
            dve.wait_ge(loaded, 64)
            v.tensor_scalar(IG[:], IG[:], gb[:, 0:1], None, ALU.add).then_inc(biased, 1)
            v.tensor_scalar(FG[:], FG[:], gb[:, 1:2], None, ALU.add).then_inc(biased, 1)
            dve.wait_ge(biased, 2)
            v.scalar_tensor_tensor(out=AB[:], in0=FG[:], scalar=-1.0, in1=FG[:], op0=ALU.mult,
                                   op1=ALU.max).then_inc(abs_ready, 1)
            dve.wait_ge(l_ready, 1)
            v.scalar_tensor_tensor(out=LF[:], in0=FG[:], scalar=0.0, in1=AB[:], op0=ALU.min,
                                   op1=ALU.subtract).then_inc(lf_ready, 1)
            dve.wait_ge(lf_ready, 1)
            v.memset(LF[:, NT - 1, DEC:], 0.0).then_inc(padded, 1)
            v.memset(IG[:, NT - 1, DEC:], FAR).then_inc(padded, 1)
            dve.wait_ge(padded, 2)
            dve.wait_ge(mask_ready, 2)
            v.tensor_tensor_scan(flat(B), flat(cm), flat(LF), 0.0, ALU.mult, ALU.add).then_inc(b_ready, 1)
            v.tensor_tensor_scan(flat(M)[:, 0:SEQ], flat(LF)[:, 0:SEQ], flat(IG)[:, 0:SEQ], 0.0, ALU.add,
                                 ALU.max).then_inc(m_ready, 1)
            v.tensor_tensor_scan(flat(M)[:, SEQ:], flat(LF)[:, SEQ:], flat(IG)[:, SEQ:], m0[:], ALU.add,
                                 ALU.max).then_inc(m_ready, 1)
            v.memset(mp[:, 0:1], 0.0).then_inc(mp_ready, 1)
            v.tensor_copy(mp[:, NT - 1:NT], m0[:]).then_inc(mp_ready, 1)
            dve.wait_ge(m_ready, 2)
            v.tensor_copy(mp[:, 1:NPT], M[:, 0:NPT - 1, P - 1]).then_inc(mp_ready, 1)
            dve.wait_ge(b_ready, 1)
            v.tensor_tensor(dl[:], B[:, :, P - 1], M[:, :, P - 1], ALU.subtract).then_inc(mp_ready, 1)
            v.tensor_tensor(U[:], B[:], M[:], ALU.subtract).then_inc(u_ready, 1)
            v.tensor_tensor(G[:], IG[:], B[:], ALU.subtract).then_inc(u_ready, 1)
            dve.wait_ge(u_ready, 2)
            dve.wait_ge(mp_ready, 4)
            v.tensor_tensor(IG[:], U[:], bc(mp[:]), ALU.add).then_inc(args_ready, 1)
            v.tensor_tensor(FG[:], G[:], bc(dl[:]), ALU.add).then_inc(args_ready, 1)
            dve.wait_ge(w_ready, 3)
            v.scalar_tensor_tensor(out=dd[:], in0=W[0:MH, :, P - 1].unsqueeze(2).to_broadcast([MH, NT, MH]), scalar=-1.0,
                                   in1=c["ident"][0:MH, 0:MH].unsqueeze(1).to_broadcast([MH, NT, MH]), op0=ALU.mult,
                                   op1=ALU.mult).then_inc(dec_args, 1)
            dve.wait_ge(turned, 1)
            for n in range(0, NT, 5):
                m = min(5, NT - n)
                src = pw[:, n // 5, 0:m * 96].rearrange("p (n q x) -> p n q x", q=3, x=32)[:, :, :, 0:MH]
                v.tensor_copy(gc[:, n:n + m], src).then_inc(taken, 1)
            dve.wait_ge(dec_sum, 1)
            v.tensor_copy(dec[:], pd[:, 0:NT * MH].rearrange("p (n h) -> p n h", h=MH)).then_inc(taken, 1)

        @block.tensor
        def _(pe):
            pe.wait_ge(w_ready, 3)
            for n in range(NT):
                mm = nc.tensor.transpose(pw[:, n // 5, (n % 5) * 96:(n % 5 + 1) * 96], W[:, n], c["ident"][0:96, 0:96])
            mm.then_inc(turned, 1)
            pe.wait_ge(dec_args, 1)
            nc.tensor.matmul(pd[:, 0:NT * MH], c["nones"][0:MH, :], dd[:].rearrange("h n g -> h (n g)"),
                             start=True, stop=True).then_inc(dec_sum, 1)


def mlstm(k, c, gc, dec):
    nc, d = k.nc, k.d
    MA = MD + 1
    qkv_in = [k.sem("qkv_loaded0"), k.sem("qkv_loaded1")]
    ug_in = [k.sem("ug_loaded0"), k.sem("ug_loaded1")]
    stored = [k.sem("h_stored0"), k.sem("h_stored1")]
    (ones_ready, state_in, k_scaled, q_weighted, v_ready, vw_ready, turned, q_taken, k_taken, qw_taken, d_ready, s_ready,
     dm_ready, w_ready, sw_ready, num_ready, u_ready, decayed, c_ready, dn_ready, ab_ready, fl_ready, rd_ready, h_ready,
     c_stored) = k.sems(
        "ones_ready", "state_loaded", "k_scaled", "q_weighted", "v_ready", "v_weighted", "qk_turned", "q_taken", "k_taken",
        "qw_taken", "exponent_ready", "scores_ready", "exponent_masked", "weights_ready", "scores_weighted",
        "numerator_ready", "update_ready", "memory_decayed", "memory_ready", "den_ready", "den_abs", "den_floored",
        "den_inverse", "h_ready", "memory_stored")
    with ExitStack() as s:
        x = sbuf(nc, s, "mx", [P, 2, 3, MH, MD])
        LG = sbuf(nc, s, "mLG", [2, 2, MH, P])
        RU = sbuf(nc, s, "mRU", [2, 2, MH, P])
        ks = sbuf(nc, s, "mks", [P, 2, MH, MD])
        qw = sbuf(nc, s, "mqw", [P, 2, MH, MD])
        VI = sbuf(nc, s, "mVI", [P, 2, MH, MA])
        VU = sbuf(nc, s, "mVU", [P, 2, MH, MA])
        T = sbuf(nc, s, "mT", [P, 3, MH, P])
        DM = sbuf(nc, s, "mDM", [P, MH, P])
        WX = sbuf(nc, s, "mWX", [P, MH, P])
        SW = sbuf(nc, s, "mSW", [P, MH, P])
        C = [sbuf(nc, s, "mC0", [P, MH, MA]), sbuf(nc, s, "mC1", [P, MH, MA])]
        dn = sbuf(nc, s, "mdn", [P, 4, MH])
        H = sbuf(nc, s, "mH", [P, 2, MH, MD])
        pT = psum(nc, s, "mpT", [P, 3, W5])
        pD = psum(nc, s, "mpD", [P, W5])
        pS = psum(nc, s, "mpS", [P, W5])
        pN = psum(nc, s, "mpN", [P, 2, W5])
        block = s.enter_context(nc.Block())
        pairs = lambda ap: ap[:, :, 0:2 * MA].rearrange("p b (h e) -> p b h e", e=MA)
        heads = lambda ap: ap.rearrange("p (b h) e -> p b h e", b=2)
        per_head = lambda col, n: col.unsqueeze(2).to_broadcast([P, MH, n])

        @block.sync
        def _(sp):
            sp.dma_start(C[1][:], d["c_init"]).then_inc(state_in, 16)

            def body(t, u, r, first):
                if not first:
                    sp.wait_ge(turned, t - 1)
                    sp.wait_ge(vw_ready, t - 1)
                    sp.wait_ge(d_ready, t - 1)
                for n in range(3):
                    sp.dma_start(x[:, u, n].rearrange("p h e -> p (h e)"), d["proj_out"][n, tok(t), :]).then_inc(qkv_in[u], 16)
                sp.wait_ge(ones_ready, 2)
                sp.dma_start(LG[0:1, u], d["ug_d"][0:1, :, tok(t)]).then_inc(ug_in[u], 16)
                sp.dma_start(RU[1:2, u], d["ug_d"][1:2, :, tok(t)]).then_inc(ug_in[u], 16)
            tiles(sp, body)
            sp.wait_ge(c_ready, NPT)
            sp.dma_start(d["c_out"][0], C[0][:]).then_inc(c_stored, 16)
            sp.wait_ge(c_ready, NT)
            sp.dma_start(d["c_out"][1], C[1][:]).then_inc(c_stored, 16)
            sp.wait_ge(c_stored, 32)
            for u in range(2):
                sp.wait_ge(stored[u], 16 * len(range(u, NT, 2)))

        @block.gpsimd
        def _(pool):
            nc.gpsimd.memset(LG[:], 1.0).then_inc(ones_ready, 1)
            nc.gpsimd.memset(RU[:], 1.0).then_inc(ones_ready, 1)
            nc.gpsimd.memset(VI[:], 1.0).then_inc(ones_ready, 1)
            nc.gpsimd.memset(C[0][:], 0.0).then_inc(ones_ready, 1)

            def body(t, u, r, first):
                pool.wait_ge(h_ready, t + 1)
                pool.dma_start(d["h_d"][tok(t), :], H[:, u].rearrange("p h e -> p (h e)")).then_inc(stored[u], 16)
            tiles(pool, body)

        @block.scalar
        def _(act):
            act.preload_act_table_set("natural_log_exp_and_others")
            act.wait_ge(ones_ready, 4)

            def body(t, u, r, first):
                act.wait_ge(qkv_in[u], 48 * r + 48)
                if not first:
                    act.wait_ge(turned, t - 1)
                    act.wait_ge(u_ready, t - 1)
                nc.scalar.activation(ks[:, u], x[:, u, 1], ACT.Copy, scale=MD ** -0.5).then_inc(k_scaled, 1)
                nc.scalar.activation(VI[:, u, :, 0:MD], x[:, u, 2], ACT.Copy).then_inc(v_ready, 1)
                act.wait_ge(turned, t + 1)
                nc.scalar.activation(T[:, 0], pT[:, 0].rearrange("p (h e) -> p h e", e=P), ACT.Copy).then_inc(q_taken, 1)
                act.wait_ge(dm_ready, t + 1)
                nc.scalar.activation(WX[:], DM[:], ACT.Exp).then_inc(w_ready, 1)
            tiles(act, body)

        @block.vector
        def _(dve):
            v = nc.vector

            def body(t, u, r, first):
                state = C[1] if isinstance(t, int) and t == NPT else C[0]
                g = gc[:, bass.ds(t, 1)].rearrange("p o q h -> p (o q) h")
                dve.wait_ge(qkv_in[u], 48 * r + 48)
                if not first:
                    dve.wait_ge(turned, t - 1)
                v.tensor_tensor(qw[:, u], x[:, u, 0], per_head(g[:, 0], MD), ALU.mult).then_inc(q_weighted, 1)
                dve.wait_ge(v_ready, t + 1)
                v.tensor_tensor(VU[:, u], VI[:, u], per_head(g[:, 1], MA), ALU.mult).then_inc(vw_ready, 1)
                dve.wait_ge(d_ready, t + 1)
                v.tensor_tensor(DM[:], pD[:].rearrange("p (h e) -> p h e", e=P),
                                c["farc"][:].unsqueeze(1).to_broadcast([P, MH, P]), ALU.add).then_inc(dm_ready, 1)
                dve.wait_ge(turned, t + 1)
                v.tensor_copy(T[:, 2], pT[:, 2].rearrange("p (h e) -> p h e", e=P)).then_inc(k_taken, 1)
                v.tensor_copy(T[:, 1], pT[:, 1].rearrange("p (h e) -> p h e", e=P)).then_inc(qw_taken, 1)
                dve.wait_ge(s_ready, t + 1)
                dve.wait_ge(w_ready, t + 1)
                v.tensor_tensor(SW[:], pS[:].rearrange("p (h e) -> p h e", e=P), WX[:], ALU.mult).then_inc(sw_ready, 1)
                dve.wait_ge(num_ready, t + 1)
                if isinstance(t, int) and t == NPT:
                    dve.wait_ge(state_in, 16)
                v.tensor_tensor(state[:], state[:], dec[:, bass.ds(t, 1)].rearrange("p o h -> p (o h)").unsqueeze(2)
                                .to_broadcast([P, MH, MA]), ALU.mult).then_inc(decayed, 1)
                dve.wait_ge(u_ready, t + 1)
                dve.wait_ge(decayed, t + 1)
                v.tensor_tensor(heads(state[:]), heads(state[:]), pairs(pT[:, 1:3]), ALU.add).then_inc(c_ready, 1)
                num = pairs(pN[:])
                v.tensor_copy(dn[:, 0].rearrange("p (b h) -> p b h", b=2), num[:, :, :, MD]).then_inc(dn_ready, 1)
                dve.wait_ge(dn_ready, t + 1)
                v.scalar_tensor_tensor(out=dn[:, 1], in0=dn[:, 0], scalar=-1.0, in1=dn[:, 0], op0=ALU.mult,
                                       op1=ALU.max).then_inc(ab_ready, 1)
                dve.wait_ge(ab_ready, t + 1)
                v.tensor_tensor(dn[:, 2], dn[:, 1], g[:, 2], ALU.max).then_inc(fl_ready, 1)
                dve.wait_ge(fl_ready, t + 1)
                v.reciprocal(dn[:, 3], dn[:, 2]).then_inc(rd_ready, 1)
                dve.wait_ge(rd_ready, t + 1)
                at_least(dve, stored[u], 16 * r)
                v.tensor_tensor(heads(H[:, u]), num[:, :, :, 0:MD],
                                dn[:, 3].rearrange("p (b h) -> p b h", b=2).unsqueeze(3).to_broadcast([P, 2, 2, MD]),
                                ALU.mult).then_inc(h_ready, 1)
            tiles(dve, body)

        @block.tensor
        def _(pe):
            t_ = nc.tensor

            def body(t, u, r, first):
                start = first and u == 0
                state = C[1] if isinstance(t, int) and t == NPT else C[0]
                pe.wait_ge(ug_in[u], 32 * r + 32)
                if not start:
                    pe.wait_ge(dm_ready, t)
                for h in range(MH):
                    mm = t_.matmul(pD[:, h * P:(h + 1) * P], LG[:, u, h], RU[:, u, h], start=(h == 0), stop=True,
                                   skip_group_check=True)
                mm.then_inc(d_ready, 1)
                pe.wait_ge(k_scaled, t + 1)
                pe.wait_ge(q_weighted, t + 1)
                if not start:
                    pe.wait_ge(c_ready, t)
                    pe.wait_ge(q_taken, t)
                for n, src in enumerate((x[:, u, 0], qw[:, u], ks[:, u])):
                    for h in range(MH):
                        mm = t_.transpose(pT[:, n, h * P:(h + 1) * P], src[:, h], c["ident"][:])
                mm.then_inc(turned, 1)
                pe.wait_ge(q_taken, t + 1)
                pe.wait_ge(k_taken, t + 1)
                if not start:
                    pe.wait_ge(sw_ready, t)
                for h in range(MH):
                    mm = t_.matmul(pS[:, h * P:(h + 1) * P], T[:, 2, h], T[:, 0, h], start=(h == 0), stop=True,
                                   skip_group_check=True)
                mm.then_inc(s_ready, 1)
                pe.wait_ge(qw_taken, t + 1)
                if not start:
                    pe.wait_ge(h_ready, t)
                if isinstance(t, int) and t == NPT:
                    pe.wait_ge(state_in, 16)
                elif start:
                    pe.wait_ge(ones_ready, 4)
                for h in range(MH):
                    t_.matmul(pN[:, h // 2, (h % 2) * MA:(h % 2 + 1) * MA], T[:, 1, h], state[:, h],
                              start=(h % 2 == 0), stop=False, skip_group_check=True)
                pe.wait_ge(sw_ready, t + 1)
                for h in range(MH):
                    mm = t_.matmul(pN[:, h // 2, (h % 2) * MA:(h % 2 + 1) * MA], SW[:, h], VI[:, u, h],
                                   start=False, stop=True, skip_group_check=True)
                mm.then_inc(num_ready, 1)
                pe.wait_ge(vw_ready, t + 1)
                for h in range(MH):
                    mm = t_.matmul(pT[:, 1 + h // 2, (h % 2) * MA:(h % 2 + 1) * MA], ks[:, u, h], VU[:, u, h],
                                   start=(h % 2 == 0), stop=True, skip_group_check=True)
                mm.then_inc(u_ready, 1)
            tiles(pe, body)


def output_projection(k, c):
    nc, d = k.nc, k.d
    x_in = [k.sem("tile_loaded0"), k.sem("tile_loaded1")]
    stored = [k.sem("x1_stored0"), k.sem("x1_stored1")]
    raw_in = [k.sem("w_raw_loaded0"), k.sem("w_raw_loaded1")]
    (w_high, w_low, rows_in, squared, summed_p, summed_o, std_ready, rstd_ready, sig_ready, normed, weighted, y_ready, turned,
     y_high, y_low, mix_ready, gated, x1_ready) = k.sems(
        "w_high", "w_low", "rows_loaded", "squared", "squares_summed", "o_squares_summed", "std_ready", "rstd_ready",
        "sigmoid_ready", "normed", "weighted", "y_ready", "y_turned", "y_high", "y_low", "mix_ready", "gated", "x1_ready")
    with ExitStack() as s:
        raw = sbuf(nc, s, "eraw", [P, 2, D])
        wH = sbuf(nc, s, "ewH", [P, KD, D], F32R)
        wL = sbuf(nc, s, "ewL", [P, KD, D], F32R)
        gate = sbuf(nc, s, "egate", [P, 2, D])
        wrow = sbuf(nc, s, "ewrow", [P, D])
        x = sbuf(nc, s, "ex", [P, 2, D])
        y = sbuf(nc, s, "ey", [P, 2, D])
        o = sbuf(nc, s, "eo", [P, 2, W5])
        st = sbuf(nc, s, "est", [P, 2, 4, 8])
        yH = sbuf(nc, s, "eyH", [P, 2, KD, P], F32R)
        yL = sbuf(nc, s, "eyL", [P, 2, KD, P], F32R)
        mix = sbuf(nc, s, "emix", [P, 2, D])
        sq = sbuf(nc, s, "esq", [P, D])
        pT = psum(nc, s, "epT", [P, 2, D])
        acc = psum(nc, s, "eacc", [P, 2, D])
        block = s.enter_context(nc.Block())

        @block.sync
        def _(sp):
            for n in range(2):
                src = d["mods"].rearrange("(j w) p -> w j p", w=2)[n:n + 1, 16:24, :]
                sp.dma_start(gate[:, n].rearrange("p (j e) -> p j e", e=P),
                             src.to_broadcast([P, KD, P])).then_inc(rows_in, 16)
            sp.dma_start(wrow[:], d["y_norms"]).then_inc(rows_in, 16)

            def body(t, u, r, first):
                if not first:
                    sp.wait_ge(x1_ready, t - 1)
                    sp.wait_ge(turned, t - 1)
                sp.dma_start(y[:, u, 0:W5], d["h_d"][tok(t), :]).then_inc(x_in[u], 16)
                sp.dma_start(y[:, u, W5:], d["o_d"][tok(t), :]).then_inc(x_in[u], 16)
                sp.dma_start(o[:, u], d["proj_out"][3, tok(t), :]).then_inc(x_in[u], 16)
                sp.dma_start(x[:, u], d["x_all"][tok(t), :]).then_inc(x_in[u], 16)
            tiles(sp, body)

        @block.gpsimd
        def _(pool):
            for kk in range(KD):
                pool.wait_ge(w_high, kk + 1)
                nc.gpsimd.tensor_tensor(wL[:, kk], raw[:, kk % 2], wH[:, kk].bitcast(F32), ALU.subtract).then_inc(w_low, 1)

            def body(t, u, r, first):
                pool.wait_ge(x1_ready, t + 1)
                pool.dma_start(d["x1_d"][tok(t), :], mix[:, u]).then_inc(stored[u], 16)
            tiles(pool, body)
            for u in range(2):
                pool.wait_ge(stored[u], 16 * len(range(u, NT, 2)))

        @block.scalar
        def _(act):
            for kk in range(KD):
                if kk >= 2:
                    act.wait_ge(w_low, kk - 1)
                act.dma_start(raw[:, kk % 2], d["w_out"][kk * P:(kk + 1) * P, :]).then_inc(raw_in[kk % 2], 16)
                act.wait_ge(raw_in[kk % 2], 16 * (kk // 2) + 16)
                nc.scalar.activation(wH[:, kk], raw[:, kk % 2], ACT.Copy).then_inc(w_high, 1)

            def body(t, u, r, first):
                act.wait_ge(x_in[u], 64 * r + 64)
                nc.scalar.activation(o[:, u], o[:, u], ACT.Sigmoid).then_inc(sig_ready, 1)
                act.wait_ge(summed_p, t + 1)
                act.wait_ge(summed_o, t + 1)
                if not first:
                    act.wait_ge(rstd_ready, t - 1)
                nc.scalar.activation(st[:, u, 2, 0:4], st[:, u, 0, 0:4], ACT.Sqrt, bias=c["eps"][:], scale=1.0 / MD)\
                    .then_inc(std_ready, 1)
                nc.scalar.activation(st[:, u, 2, 4:5], st[:, u, 1, 0:1], ACT.Sqrt, bias=c["eps"][:], scale=1.0 / W5)\
                    .then_inc(std_ready, 1)
                act.wait_ge(turned, t + 1)
                if not first:
                    act.wait_ge(mix_ready, t - 1)
                nc.scalar.activation(yH[:, u], pT[:, u].rearrange("p (j e) -> p j e", e=P), ACT.Copy).then_inc(y_high, 1)
            tiles(act, body)

        @block.vector
        def _(dve):
            v = nc.vector
            dve.wait_ge(rows_in, 48)

            def norm(t, u, r, first):
                dve.wait_ge(x_in[u], 64 * r + 64)
                v.tensor_tensor(sq[:], y[:, u], y[:, u], ALU.mult).then_inc(squared, 1)
                dve.wait_ge(squared, t + 1)
                v.tensor_reduce(st[:, u, 0], sq[:].rearrange("p (j e) -> p j e", e=P), AX.X, ALU.add).then_inc(summed_p, 1)
                dve.wait_ge(summed_p, t + 1)
                v.tensor_reduce(st[:, u, 1, 0:1], st[:, u, 0, 4:8], AX.X, ALU.add).then_inc(summed_o, 1)
                dve.wait_ge(std_ready, 2 * t + 2)
                v.reciprocal(st[:, u, 3, 0:5], st[:, u, 2, 0:5]).then_inc(rstd_ready, 1)
                dve.wait_ge(rstd_ready, t + 1)
                ya = y[:, u, 0:W5].rearrange("p (h e) -> p h e", e=MD)
                v.tensor_tensor(ya, ya, st[:, u, 3, 0:4].unsqueeze(2).to_broadcast([P, MH, MD]), ALU.mult).then_inc(normed, 1)
                dve.wait_ge(normed, t + 1)
                dve.wait_ge(sig_ready, t + 1)
                v.tensor_tensor(y[:, u, 0:W5], y[:, u, 0:W5], wrow[:, 0:W5], ALU.mult).then_inc(weighted, 1)
                v.scalar_tensor_tensor(out=y[:, u, W5:], in0=y[:, u, W5:], scalar=st[:, u, 3, 4:5], in1=wrow[:, W5:],
                                       op0=ALU.mult, op1=ALU.mult).then_inc(y_ready, 1)
                dve.wait_ge(weighted, t + 1)
                v.tensor_tensor(y[:, u, 0:W5], y[:, u, 0:W5], o[:, u], ALU.mult).then_inc(y_ready, 1)

            def low(t, u, r, first):
                dve.wait_ge(y_high, t + 1)
                if not first:
                    dve.wait_ge(mix_ready, t - 1)
                v.tensor_tensor(yL[:, u], pT[:, u].rearrange("p (j e) -> p j e", e=P), yH[:, u].bitcast(F32),
                                ALU.subtract).then_inc(y_low, 1)

            def finish(t, u, r, first):
                which = 1 if isinstance(t, int) and t == NPT else 0
                dve.wait_ge(mix_ready, t + 1)
                at_least(dve, stored[u], 16 * r)
                v.tensor_tensor(mix[:, u], acc[:, u], gate[:, which], ALU.mult).then_inc(gated, 1)
                dve.wait_ge(gated, t + 1)
                v.tensor_tensor(mix[:, u], mix[:, u], x[:, u], ALU.add).then_inc(x1_ready, 1)

            norm(0, 0, 0, True)
            low(0, 0, 0, True)
            norm(1, 1, 0, True)
            low(1, 1, 0, True)
            finish(0, 0, 0, True)
            with dve.Fori(1, NPT // 2) as i:
                norm(2 * i, 0, i, False)
                low(2 * i, 0, i, False)
                finish(2 * i - 1, 1, i - 1, False)
                norm(2 * i + 1, 1, i, False)
                low(2 * i + 1, 1, i, False)
                finish(2 * i, 0, i, False)
            norm(NPT, 0, NPT // 2, False)
            low(NPT, 0, NPT // 2, False)
            finish(NPT - 1, 1, NPT // 2 - 1, False)
            finish(NPT, 0, NPT // 2, False)

        @block.tensor
        def _(pe):
            def turn(t, u, r, first):
                pe.wait_ge(y_ready, 2 * t + 2)
                if not first:
                    pe.wait_ge(y_low, t - 1)
                for kk in range(KD):
                    mm = nc.tensor.transpose(pT[:, u, kk * P:(kk + 1) * P], y[:, u, kk * P:(kk + 1) * P], c["ident"][:])
                mm.then_inc(turned, 1)

            def multiply(t, u, r, first):
                pe.wait_ge(y_low, t + 1)
                if not first:
                    pe.wait_ge(gated, t - 1)
                for half in range(2):
                    cols = slice(half * W5, (half + 1) * W5)
                    for kk in range(KD):
                        for n, (a, w) in enumerate(((yH, wH), (yL, wH), (yH, wL))):
                            mm = nc.tensor.matmul(acc[:, u, cols], a[:, u, kk], w[:, kk, cols],
                                                  start=(kk == 0 and n == 0), stop=(kk == KD - 1 and n == 2))
                mm.then_inc(mix_ready, 1)
            pe.wait_ge(w_low, KD)
            turn(0, 0, 0, True)
            turn(1, 1, 0, True)
            multiply(0, 0, 0, True)
            turn(2, 0, 1, False)
            multiply(1, 1, 0, True)
            with pe.Fori(1, NPT // 2 - 1) as i:
                turn(2 * i + 1, 1, i, False)
                multiply(2 * i, 0, i, False)
                turn(2 * i + 2, 0, i + 1, False)
                multiply(2 * i + 1, 1, i, False)
            turn(NPT - 1, 1, NPT // 2 - 1, False)
            multiply(NPT - 2, 0, NPT // 2 - 1, False)
            turn(NPT, 0, NPT // 2, False)
            multiply(NPT - 1, 1, NPT // 2 - 1, False)
            multiply(NPT, 0, NPT // 2, False)


def ffn_up(k, c, hH, hL):
    nc, d = k.nc, k.d
    NW = SEQ // W5
    NV = NW + 1
    NU = 2 + SEQ + 2 + DEC
    S0 = 2 + SEQ + 2
    parts = ((0, 0, SEQ), (SEQ, S0 - 2, DEC))
    raw_in = [k.sem("w_raw_loaded0"), k.sem("w_raw_loaded1")]
    (w_high, w_low, up_done, up_taken, consts_in, zeroed, first_tap, second_tap, conv_done, silu_ready, act_ready, kept,
     turned, ends_taken, ends_stored, history_set, stored) = k.sems(
        "w_high", "w_low", "up_done", "up_taken", "constants_loaded", "zeroed", "first_tap", "second_tap", "conv_done",
        "silu_ready", "act_ready", "last_rows_kept", "last_rows_turned", "last_rows_taken", "last_rows_stored",
        "history_set", "act_stored")
    with ExitStack() as s:
        raw = sbuf(nc, s, "fraw", [P, 2, KD, P])
        wH = sbuf(nc, s, "fwH", [P, 2, KD, P], F32R)
        wL = sbuf(nc, s, "fwL", [P, 2, KD, P], F32R)
        U = sbuf(nc, s, "fU", [P, 2, NU])
        V = sbuf(nc, s, "fV", [P, 2, SEQ + DEC])
        cw = sbuf(nc, s, "fcw", [P, 2 * NF, 3])
        cb = sbuf(nc, s, "fcb", [P, 2 * NF])
        cs = sbuf(nc, s, "fcs", [P, 2 * NF, 2])
        ends = sbuf(nc, s, "fends", [P, 2, 2, 2 * NF])
        ends_t = sbuf(nc, s, "fends_t", [4 * NF, 2, P])
        acc = psum(nc, s, "facc", [P, 2, NW, W5])
        block = s.enter_context(nc.Block())

        def pairs(eng, body):
            body(0, True)
            with eng.Fori(1, NF) as i:
                body(i, False)

        @block.sync
        def _(sp):
            for t, n in ((cw, "w_conv_T"), (cb, "b_conv_T"), (cs, "conv_state_T")):
                sp.dma_start(t[:], d[n]).then_inc(consts_in, 16)

            def load(i, first):
                for j in range(2):
                    if not first:
                        sp.wait_ge(w_low, 2 * i + j - 1)
                    sp.dma_start(raw[:, j], d["w_up"].rearrange("(q p) n -> p q n", p=P)
                                 [:, :, bass.ds(j * FF + i * P, P)]).then_inc(raw_in[j], 16)

            def store(i):
                sp.wait_ge(act_ready, i + 1)
                sp.dma_start(d["act_d"][0:NPT, :, bass.ds(i, 1), :].rearrange("t p o e -> p t (o e)"),
                             V[:, 0, 0:SEQ].rearrange("p (t e) -> p t e", e=P)).then_inc(stored, 16)
                sp.dma_start(d["act_d"][NPT, :, bass.ds(i, 1), 0:DEC].rearrange("p o e -> p (o e)"),
                             V[:, 0, SEQ:]).then_inc(stored, 16)
            load(0, True)
            with sp.Fori(1, NF) as i:
                load(i, False)
                store(i - 1)
            store(NF - 1)
            sp.wait_ge(ends_taken, 1)
            for t in range(2):
                sp.dma_start(d["conv_out"][t], ends_t[:, t]).then_inc(ends_stored, 16)
            sp.wait_ge(ends_stored, 32)
            sp.wait_ge(stored, 32 * NF)

        @block.scalar
        def _(act):
            def split(i, j, free=False):
                act.wait_ge(raw_in[j], 16 * i + 16)
                if not free:
                    act.wait_ge(up_done, NV * (2 * i + j - 1))
                nc.scalar.activation(wH[:, j], raw[:, j], ACT.Copy).then_inc(w_high, 1)

            def take(i, j, first=False):
                n = 2 * i + j
                if not first:
                    act.wait_ge(conv_done, n - 1)
                    act.wait_ge(kept, n - 1)
                for w in range(NV):
                    act.wait_ge(up_done, NV * n + w + 1)
                    src, dst = ((acc[:, j, w], U[:, j, 2 + w * W5:2 + (w + 1) * W5]) if w < NW else
                                (acc[:, j, 0, 0:DEC], U[:, j, S0:]))
                    nc.scalar.activation(dst, src, ACT.Copy).then_inc(up_taken, 1)

            def silu(i):
                act.wait_ge(conv_done, 2 * i + 1)
                nc.scalar.activation(V[:, 0], V[:, 0], ACT.Silu).then_inc(silu_ready, 1)

            split(0, 0, free=True)
            split(0, 1, free=True)
            take(0, 0, first=True)
            split(1, 0)
            take(0, 1, first=True)
            silu(0)
            split(1, 1)
            with act.Fori(1, NF - 1) as i:
                take(i, 0)
                split(i + 1, 0)
                take(i, 1)
                silu(i)
                split(i + 1, 1)
            take(NF - 1, 0)
            take(NF - 1, 1)
            silu(NF - 1)

        @block.gpsimd
        def _(pool):
            def body(i, first):
                for j in range(2):
                    pool.wait_ge(w_high, 2 * i + j + 1)
                    if not first:
                        pool.wait_ge(up_done, NV * (2 * i + j - 1))
                    nc.gpsimd.tensor_tensor(wL[:, j], raw[:, j], wH[:, j].bitcast(F32), ALU.subtract).then_inc(w_low, 1)
            pairs(pool, body)

        @block.vector
        def _(dve):
            v = nc.vector
            v.memset(U[:, :, 0:2], 0.0).then_inc(zeroed, 1)
            dve.wait_ge(consts_in, 48)

            def conv(i, j, first):
                n = 2 * i + j
                ft = bass.ds(i + j * NF, 1)
                tap = lambda m: cw[:, ft, m:m + 1].rearrange("p o m -> p (o m)")
                if not first:
                    dve.wait_ge(conv_done, n - 1)
                v.tensor_copy(U[:, j:j + 1, S0 - 2:S0], cs[:, ft, :]).then_inc(history_set, 1)
                dve.wait_ge(up_taken, NV * (n + 1))
                dve.wait_ge(history_set, n + 1)
                if not first:
                    dve.wait_ge(act_ready, i)
                    dve.wait_ge(stored, 32 * i)
                for at, u0, width in parts:
                    v.tensor_scalar(V[:, j, at:at + width], U[:, j, u0:u0 + width], tap(0), cb[:, ft],
                                    ALU.mult, ALU.add).then_inc(first_tap, 1)
                for m, (at, u0, width) in enumerate(parts):
                    dve.wait_ge(first_tap, 2 * n + m + 1)
                    v.scalar_tensor_tensor(out=V[:, j, at:at + width], in0=U[:, j, u0 + 1:u0 + 1 + width],
                                           scalar=tap(1), in1=V[:, j, at:at + width], op0=ALU.mult,
                                           op1=ALU.add).then_inc(second_tap, 1)
                for m, (at, u0, width) in enumerate(parts):
                    dve.wait_ge(second_tap, 2 * n + m + 1)
                    op = v.scalar_tensor_tensor(out=V[:, j, at:at + width], in0=U[:, j, u0 + 2:u0 + 2 + width],
                                                scalar=tap(2), in1=V[:, j, at:at + width], op0=ALU.mult, op1=ALU.add)
                op.then_inc(conv_done, 1)
                for m, rows in enumerate((U[:, j, SEQ:SEQ + 2], U[:, j, NU - 2:NU])):
                    op = v.tensor_copy(ends[:, m, :, ft].rearrange("p r o -> p (r o)"), rows)
                op.then_inc(kept, 1)

            def body(i, first):
                if first:
                    dve.wait_ge(zeroed, 1)
                conv(i, 0, first)
                conv(i, 1, first)
                dve.wait_ge(silu_ready, i + 1)
                dve.wait_ge(conv_done, 2 * i + 2)
                v.tensor_tensor(V[:, 0], V[:, 0], V[:, 1], ALU.mult).then_inc(act_ready, 1)
            pairs(dve, body)
            dve.wait_ge(turned, 1)
            v.tensor_copy(ends_t[:], acc[0:4 * NF, 0, 0, 0:2 * P].rearrange("p (m e) -> p m e", e=P)).then_inc(ends_taken, 1)

        @block.tensor
        def _(pe):
            def body(i, first):
                for j in range(2):
                    n = 2 * i + j
                    pe.wait_ge(w_high, n + 1)
                    pe.wait_ge(w_low, n + 1)
                    if not first:
                        pe.wait_ge(up_taken, NV * (n - 1))
                    for w in range(NV):
                        if w < NW:
                            dst, cols = acc[:, j, w], slice(w * W5, (w + 1) * W5)
                        else:
                            pe.wait_ge(up_taken, NV * n + 1)
                            dst, cols = acc[:, j, 0, 0:DEC], slice(SEQ, SEQ + DEC)
                        for kk in range(KD):
                            for m, (a, h) in enumerate(((wH, hH), (wH, hL), (wL, hH))):
                                mm = nc.tensor.matmul(dst, a[:, j, kk], h[:, kk, cols],
                                                      start=(kk == 0 and m == 0), stop=(kk == KD - 1 and m == 2))
                        mm.then_inc(up_done, 1)
            pairs(pe, body)
            pe.wait_ge(kept, 2 * NF)
            pe.wait_ge(up_taken, NV * 2 * NF)
            for m in range(2):
                mm = nc.tensor.transpose(acc[0:4 * NF, 0, 0, m * P:(m + 1) * P],
                                         ends[:, m].rearrange("p r n -> p (r n)"), c["ident"][:])
            mm.then_inc(turned, 1)


def ffn_down(k, c, half):
    nc, d = k.nc, k.d
    cols = slice(half * W5, (half + 1) * W5)
    raw_in = [k.sem(f"w_raw_loaded{n}") for n in range(4)]
    act_in = [k.sem("act_loaded0"), k.sem("act_loaded1")]
    x_in = [k.sem("x1_loaded0"), k.sem("x1_loaded1")]
    stored = [k.sem("y_stored0"), k.sem("y_stored1")]
    gate_in, w_high, w_low, a_high, a_low, down_done, gated, y_ready = k.sems(
        "gate_loaded", "w_high", "w_low", "act_high", "act_low", "down_done", "gated", "y_ready")
    with ExitStack() as s:
        raw = sbuf(nc, s, f"draw{half}", [P, 4, W5])
        wH = sbuf(nc, s, f"dwH{half}", [P, NF, W5], F32R)
        wL = sbuf(nc, s, f"dwL{half}", [P, NF, W5], F32R)
        a = sbuf(nc, s, f"da{half}", [P, 2, NF, P])
        aH = sbuf(nc, s, f"daH{half}", [P, 2, NF, P], F32R)
        aL = sbuf(nc, s, f"daL{half}", [P, 2, NF, P], F32R)
        gate = sbuf(nc, s, f"dgate{half}", [P, 2, W5])
        x = sbuf(nc, s, f"dx{half}", [P, 2, W5])
        y = sbuf(nc, s, f"dy{half}", [P, 2, W5])
        acc = psum(nc, s, f"dacc{half}", [P, 2, W5])
        block = s.enter_context(nc.Block())
        width = lambda t: DEC if isinstance(t, int) and t == NPT else P

        @block.sync
        def _(sp):
            src = d["mods"].rearrange("(j w) p -> w j p", w=2)
            for n in range(2):
                sp.dma_start(gate[:, n].rearrange("p (j e) -> p j e", e=P),
                             src[n:n + 1, 40 + 4 * half:44 + 4 * half, :].to_broadcast([P, 4, P])).then_inc(gate_in, 16)

            def body(t, u, r, first):
                w = width(t)
                if not first:
                    sp.wait_ge(a_low, t - 1)
                sp.dma_start(a[:, u, :, 0:w], d["act_d"][bass.ds(t, 1), :, :, 0:w].rearrange("o p n e -> (o p) n e"))\
                    .then_inc(act_in[u], 16)
                if not first:
                    sp.wait_ge(y_ready, t - 1)
                sp.dma_start(x[:, u], d["x1_d"][tok(t), cols]).then_inc(x_in[u], 16)
            tiles(sp, body)

        @block.gpsimd
        def _(pool):
            for kk in range(NF):
                pool.wait_ge(w_high, kk + 1)
                nc.gpsimd.tensor_tensor(wL[:, kk], raw[:, kk % 4], wH[:, kk].bitcast(F32), ALU.subtract).then_inc(w_low, 1)

            def body(t, u, r, first):
                pool.wait_ge(y_ready, t + 1)
                pool.dma_start(d["y_out"][tok(t), cols], y[:, u]).then_inc(stored[u], 16)
            tiles(pool, body)
            for u in range(2):
                pool.wait_ge(stored[u], 16 * len(range(u, NT, 2)))

        @block.scalar
        def _(act):
            def load(kk):
                if kk >= 4:
                    act.wait_ge(w_low, kk - 3)
                act.dma_start(raw[:, kk % 4], d["w_down"][kk * P:(kk + 1) * P, cols]).then_inc(raw_in[kk % 4], 16)

            def split(kk):
                act.wait_ge(raw_in[kk % 4], 16 * (kk // 4) + 16)
                nc.scalar.activation(wH[:, kk], raw[:, kk % 4], ACT.Copy).then_inc(w_high, 1)

            def body(t, u, r, first):
                w = width(t)
                act.wait_ge(act_in[u], 16 * r + 16)
                if not first:
                    act.wait_ge(down_done, t - 1)
                nc.scalar.activation(aH[:, u, :, 0:w], a[:, u, :, 0:w], ACT.Copy).then_inc(a_high, 1)
            for kk in range(3):
                load(kk)
            for kk in range(NF):
                if kk + 3 < NF:
                    load(kk + 3)
                split(kk)
            tiles(act, body)

        @block.vector
        def _(dve):
            v = nc.vector

            def low(t, u, first):
                w = width(t)
                dve.wait_ge(a_high, t + 1)
                if not first:
                    dve.wait_ge(down_done, t - 1)
                v.tensor_tensor(aL[:, u, :, 0:w], a[:, u, :, 0:w], aH[:, u, :, 0:w].bitcast(F32),
                                ALU.subtract).then_inc(a_low, 1)

            def finish(t, u, r):
                which = 1 if isinstance(t, int) and t == NPT else 0
                w = width(t)
                dve.wait_ge(down_done, t + 1)
                at_least(dve, stored[u], 16 * r)
                v.tensor_tensor(y[0:w, u], acc[0:w, u], gate[0:w, which], ALU.mult).then_inc(gated, 1)
                dve.wait_ge(gated, t + 1)
                dve.wait_ge(x_in[u], 16 * r + 16)
                v.tensor_tensor(y[0:w, u], y[0:w, u], x[0:w, u], ALU.add).then_inc(y_ready, 1)
            dve.wait_ge(gate_in, 32)
            low(0, 0, True)
            low(1, 1, True)
            finish(0, 0, 0)
            with dve.Fori(1, NPT // 2) as i:
                low(2 * i, 0, False)
                finish(2 * i - 1, 1, i - 1)
                low(2 * i + 1, 1, False)
                finish(2 * i, 0, i)
            low(NPT, 0, False)
            finish(NPT - 1, 1, NPT // 2 - 1)
            finish(NPT, 0, NPT // 2)

        @block.tensor
        def _(pe):
            def body(t, u, r, first):
                w = width(t)
                pe.wait_ge(a_high, t + 1)
                pe.wait_ge(a_low, t + 1)
                if not first:
                    pe.wait_ge(gated, t - 1)
                for kk in range(NF):
                    if first and u == 0:
                        pe.wait_ge(w_low, kk + 1)
                    for n, (l, m) in enumerate(((aH, wH), (aL, wH), (aH, wL))):
                        mm = nc.tensor.matmul(acc[0:w, u], l[:, u, kk, 0:w], m[:, kk], start=(kk == 0 and n == 0),
                                              stop=(kk == NF - 1 and n == 2))
                mm.then_inc(down_done, 1)
            tiles(pe, body)


def build(nc, dram):
    with ExitStack() as ctx:
        k = Kernel(nc, ctx, dram)
        k.scratch("mods", [96, P])
        dram["q_d"] = k.scratch("q_blocks", [SH, 1 + NT + NPB, P, 2 * P])[:, 1:]
        dram["kv_d"] = k.scratch("kv_blocks", [SH, 1 + NT + NPB, P, 2 * P])[:, 1:]
        dram["o_d"] = k.scratch("o_rows", [P + TOK, W5])[P:, :]
        k.scratch("h_d", [TOK, W5])
        k.scratch("ug_d", [2, MH, TOK])
        k.scratch("x1_d", [TOK, D])
        k.scratch("act_d", [NT, P, NF, P])
        k.scratch("gates_d", [8, TOK])
        c = {}
        for name, shape, dt in (("ident", [P, P], F32), ("ident_r", [P, P], F32R), ("tri", [P, P], F32),
                                ("tri_r", [P, P], F32R), ("keep", [P, P], F32), ("far", [P, P], F32),
                                ("far_r", [P, P], F32R), ("farc", [P, P], F32), ("nones", [P, P], F32),
                                ("fold", [P, SD], F32), ("eps", [P, 1], F32), ("one", [P, 1], F32), ("mod", [P, 48, 2], F32),
                                ("A1", [P, KD, 2], F32), ("A2", [P, KD, 2], F32)):
            c[name] = sbuf(nc, ctx, name, shape, dt)
        modulation(k, c)
        k.end_phase()
        with ExitStack() as s:
            hH = sbuf(nc, s, "h1H", [P, KD, TOK], F32R)
            hL = sbuf(nc, s, "h1L", [P, KD, TOK], F32R)
            normalise(k, c, dram["x_all"], c["A1"], 0, hH, hL)
            k.end_phase()
            project_gates(k, c, hH, hL)
            k.end_phase()
            project(k, c, hH, hL, dram["w_in7"], 0, 5, dram["proj_out"], False)
            k.end_phase()
            project(k, c, hH, hL, dram["w_in7"], 5, 2, dram["proj_out"], True)
            k.end_phase()
        attention_operands(k, c)
        k.end_phase()
        attention(k, c)
        k.end_phase()
        with ExitStack() as s:
            gc = sbuf(nc, s, "gate_cols", [P, NT, 3, MH])
            dec = sbuf(nc, s, "decay", [P, NT, MH])
            gate_rows(k, c, gc, dec)
            k.end_phase()
            mlstm(k, c, gc, dec)
            k.end_phase()
        attention_sample(k, c)
        k.end_phase()
        output_projection(k, c)
        k.end_phase()
        with ExitStack() as s:
            hH = sbuf(nc, s, "h2H", [P, KD, TOK], F32R)
            hL = sbuf(nc, s, "h2L", [P, KD, TOK], F32R)
            normalise(k, c, dram["x1_d"], c["A2"], 24, hH, hL, "b")
            k.end_phase()
            ffn_up(k, c, hH, hL)
            k.end_phase()
        for half in range(2):
            ffn_down(k, c, half)
            k.end_phase()


OUTS = {
    "y_out": [TOK, D],
    "conv_out": [2, 4 * NF, P],
    "m_out": [2, MH, 1],
    "c_out": [2, P, MH, MD + 1],
    "proj_out": [7, TOK, W5],
}


def layout(i):
    f = lambda a: np.ascontiguousarray(np.asarray(a))
    x = np.concatenate([np.asarray(i["x_prompt"])[0], np.asarray(i["x_sample"])[0],
                        np.zeros((P - DEC, D), np.float32)])
    cols = lambda a, n: f(np.asarray(a).reshape(n, P).T)
    w_in = np.asarray(i["w_in"])[0]
    c = np.stack([np.asarray(i["c_prompt"])[0], np.asarray(i["c_sample"])[0]])
    g = 4 * W5
    parts = [w_in[:, n * W5:(n + 1) * W5] for n in range(4)]
    sb = w_in[:, g + 2 * MH:]
    parts += [sb[:, 2 * W5:], sb[:, :W5], sb[:, W5:2 * W5]]
    norms = np.stack([np.asarray(i["sb_q_norm_w"])[0], np.asarray(i["sb_k_norm_w"])[0]])
    return {
        "x_all": f(x),
        "c_T": f(c.reshape(2, KD, P).transpose(2, 1, 0)),
        "w_ada": f(np.asarray(i["w_ada"])[0]),
        "b_ada_T": cols(i["b_ada"], 48),
        "norm1_T": cols(i["norm1_w"], KD),
        "norm2_T": cols(i["norm2_w"], KD),
        "w_in7": f(np.stack(parts)),
        "w_gate": f(w_in[:, g:g + 2 * MH]),
        "y_norms": f(np.broadcast_to(np.concatenate([np.asarray(i["ml_norm_w"]).reshape(W5),
                                                     np.asarray(i["sb_out_norm_w"])[0]]), (P, D))),
        "w_out": f(np.asarray(i["w_out"])[0]),
        "w_up": f(np.asarray(i["w_up"])[0]),
        "w_down": f(np.asarray(i["w_down"])[0]),
        "w_conv_T": f(np.asarray(i["w_conv"])[0].reshape(3, 2 * NF, P).transpose(2, 1, 0)),
        "b_conv_T": cols(i["b_conv"], 2 * NF),
        "conv_state_T": f(np.asarray(i["state_ffn_conv"])[0, 0].reshape(2, 2 * NF, P).transpose(2, 1, 0)),
        "b_gates": f(np.stack([np.asarray(i["b_ig"])[0], np.asarray(i["b_fg"])[0]], axis=1)),
        "m_init": f(np.asarray(i["state_mlstm_m"]).reshape(MH, 1)),
        "c_init": f(np.concatenate([np.asarray(i["state_mlstm_c"])[0, 0],
                                    np.asarray(i["state_mlstm_n"])[0, 0][:, :, None]], axis=2).transpose(1, 0, 2)),
        "past_k": f(np.asarray(i["cache_sb_k"]).reshape(PAST, W5)),
        "past_v": f(np.asarray(i["cache_sb_v"]).reshape(PAST, W5)),
        "sb_norms": f(np.broadcast_to(norms, (P, 2, SD))),
    }


def results(r):
    y, pr, cm, m, u = (np.asarray(r[n]) for n in ("y_out", "proj_out", "c_out", "m_out", "conv_out"))
    out = [y[:SEQ].reshape(1, SEQ, D), y[SEQ:SEQ + DEC].reshape(1, DEC, D)]
    for n, rows in enumerate((slice(0, SEQ), slice(SEQ, SEQ + DEC))):
        mem = cm[n].transpose(1, 0, 2)
        out += [mem[None, None, :, :, :MD], mem[None, None, :, :, MD], m[n].reshape(1, 1, MH)]
        out += [pr[g, rows].reshape(1, 1, -1, SH, SD) for g in (6, 4)]
        out += [u[n].reshape(1, 1, 2, 2 * FF)]
    return tuple(np.ascontiguousarray(a) for a in out)


def kernel(**inputs):
    import concourse.bacc as bacc
    from concourse.bass_utils import run_bass_kernel_spmd

    nc = bacc.Bacc("TRN2", target_bir_lowering=False, num_devices=1)
    arrays = layout(inputs)
    dram = {n: nc.dram_tensor(n, a.shape, mybir.dt.from_np(a.dtype), kind="ExternalInput").ap() for n, a in arrays.items()}
    for n, shape in OUTS.items():
        dram[n] = nc.dram_tensor(n, shape, F32, kind="ExternalOutput").ap()
    build(nc, dram)
    r = run_bass_kernel_spmd(nc, [arrays], core_ids=[0])
    return results(r.results[0])
```

```python
from contextlib import ExitStack

import numpy as np
import concourse.bass as bass
from concourse import mybir

F32 = mybir.dt.float32
F32R = mybir.dt.float32r
ACT = mybir.ActivationFunctionType
ALU = mybir.AluOpType
AX = mybir.AxisListType

P = 128
D = 1024
KD = D // P
SEQ, DEC, PAST = 2048, 32, 1024
NPT = SEQ // P
NT = NPT + 1
TOK = NT * P
MH, MD = 4, 128
SH, SD = 8, 64
W5 = 512
FF = 2816
NF = FF // P
EPS = 1e-6
FAR = -1e30
NPB = PAST // P
NMOD = 2 * KD


def tiles(eng, body):
    body(0, 0, 0, True)
    body(1, 1, 0, True)
    with eng.Fori(1, NPT // 2) as i:
        body(2 * i, 0, i, False)
        body(2 * i + 1, 1, i, False)
    body(NPT, 0, NPT // 2, False)


def at_least(eng, sem, value):
    if not (isinstance(value, int) and value <= 0):
        eng.wait_ge(sem, value)


def tok(t):
    return bass.ds(t * P, P)


class Kernel:
    def __init__(self, nc, ctx, dram):
        self.nc, self.ctx, self.d = nc, ctx, dram
        self.nsem, self.own = 0, []

    def sem(self, name):
        self.nsem += 1
        self.own.append(self.nc.alloc_semaphore(f"{name}_{self.nsem}"))
        return self.own[-1]

    def end_phase(self):
        self.nc.clear_and_free_semaphores(self.own)
        self.own = []
        self.nc.all_engine_barrier()

    def sems(self, *names):
        return [self.sem(n) for n in names]

    def scratch(self, name, shape, dt=F32):
        self.d[name] = self.nc.dram_tensor(name, shape, dt, kind="Internal").ap()
        return self.d[name]


def sbuf(nc, ctx, name, shape, dt=F32):
    return ctx.enter_context(nc.sbuf_tensor(name, shape, dt))


def psum(nc, ctx, name, shape):
    return ctx.enter_context(nc.psum_tensor(name, shape, F32))


def modulation(k, c):
    nc, d = k.nc, k.d
    loaded, bias_in, zero, sig_ready, silu_ready, mod_psum, mod_ready, scale1, lead = k.sems(
        "c_loaded", "bias_loaded", "zeroed", "sigmoid_ready", "silu_ready", "mod_summed", "mod_ready", "scale_ready",
        "scale_plus_one")
    NCH = NMOD // 4
    w_in = [k.sem(f"w_ada_loaded{n}") for n in range(NCH)]
    with ExitStack() as s:
        wa = sbuf(nc, s, "w_ada_sb", [P, NCH, KD, W5])
        cT = sbuf(nc, s, "cT", [P, KD, 2])
        sg = sbuf(nc, s, "sg", [P, KD, 2])
        sc, badd, n2 = c["silu_c"], c["b_ada"], c["norm2"]
        n1 = sbuf(nc, s, "n1", [P, KD])
        pm = psum(nc, s, "pm", [P, 512])
        block = s.enter_context(nc.Block())

        @block.sync
        def _(sp):
            sp.dma_start(cT[:], d["c_T"]).then_inc(loaded, 16)
            src = d["w_ada"].rearrange("(k p) n -> p k n", p=P)

            for n in range(NCH):
                sp.dma_start(wa[:, n], src[:, :, n * W5:(n + 1) * W5]).then_inc(w_in[n], 16)

        @block.gpsimd
        def _(pool):
            nc.gpsimd.memset(c["ident"][:], 0.0).then_inc(zero, 1)
            nc.gpsimd.memset(c["tri"][:], -1.0).then_inc(zero, 1)
            nc.gpsimd.memset(c["keep"][:], 1.0).then_inc(zero, 1)
            nc.gpsimd.memset(c["far"][:], 0.0).then_inc(zero, 1)
            nc.gpsimd.memset(c["farc"][:], 0.0).then_inc(zero, 1)
            nc.gpsimd.memset(c["nones"][:], -1.0).then_inc(zero, 1)
            nc.gpsimd.memset(c["eps"][:], EPS).then_inc(zero, 1)
            nc.gpsimd.memset(c["fold"][:], 0.0).then_inc(zero, 1)
            nc.gpsimd.memset(c["one"][:], 1.0).then_inc(zero, 1)
            pool.wait_ge(zero, 9)
            sel = nc.gpsimd.affine_select
            sel(out=c["ident"][:], in_=c["ident"][:], compare_op=ALU.not_equal, fill=1.0, base=0,
                pattern=[[-1, P]], channel_multiplier=1).then_inc(zero, 1)
            sel(out=c["tri"][:], in_=c["tri"][:], compare_op=ALU.is_ge, fill=0.0, base=0,
                pattern=[[-1, P]], channel_multiplier=1).then_inc(zero, 1)
            sel(out=c["keep"][:], in_=c["keep"][:], compare_op=ALU.is_gt, fill=0.0, base=0,
                pattern=[[1, P]], channel_multiplier=-1).then_inc(zero, 1)
            sel(out=c["far"][:], in_=c["far"][:], compare_op=ALU.is_gt, fill=FAR, base=0,
                pattern=[[1, P]], channel_multiplier=-1).then_inc(zero, 1)
            sel(out=c["farc"][:], in_=c["farc"][:], compare_op=ALU.is_ge, fill=FAR, base=0,
                pattern=[[1, P]], channel_multiplier=-1).then_inc(zero, 1)
            for n in range(2):
                pool.wait_ge(zero, 14 + n)
                sel(out=c["fold"][:], in_=c["fold"][:], compare_op=ALU.not_equal, fill=1.0, base=-SD * n,
                    pattern=[[-1, SD]], channel_multiplier=1).then_inc(zero, 1)
            pool.wait_ge(zero, 16)
            nc.gpsimd.tensor_copy(c["tri_r"][:], c["tri"][:]).then_inc(zero, 1)
            nc.gpsimd.tensor_copy(c["far_r"][:], c["far"][:]).then_inc(zero, 1)
            nc.gpsimd.tensor_copy(c["ident_r"][:], c["ident"][:]).then_inc(zero, 1)

        @block.scalar
        def _(act):
            act.dma_start(badd[:], d["b_ada_T"]).then_inc(bias_in, 16)
            act.dma_start(n1[:], d["norm1_T"]).then_inc(bias_in, 16)
            act.dma_start(n2[:], d["norm2_T"]).then_inc(bias_in, 16)
            act.wait_ge(loaded, 16)
            nc.scalar.activation(sg[:], cT[:], ACT.Sigmoid).then_inc(sig_ready, 1)

        @block.vector
        def _(dve):
            dve.wait_ge(sig_ready, 1)
            nc.vector.tensor_tensor(sc[:], cT[:], sg[:], ALU.mult).then_inc(silu_ready, 1)
            dve.wait_ge(bias_in, 48)
            dve.wait_ge(mod_psum, NCH)
            nc.vector.tensor_tensor(c["mod"][:, 0:NMOD], pm[:, 0:2 * NMOD].rearrange("p (j c) -> p j c", c=2),
                                    badd[:, 0:NMOD].unsqueeze(2).to_broadcast([P, NMOD, 2]), ALU.add).then_inc(mod_ready, 1)
            dve.wait_ge(mod_ready, 1)
            nc.vector.tensor_scalar(c["A1"][:], c["mod"][:, KD:2 * KD, :], 1.0, None, ALU.add).then_inc(lead, 1)
            dve.wait_ge(lead, 1)
            nc.vector.tensor_tensor(c["A1"][:], c["A1"][:], n1[:].unsqueeze(2).to_broadcast([P, KD, 2]),
                                    ALU.mult).then_inc(scale1, 1)

        @block.tensor
        def _(pe):
            pe.wait_ge(silu_ready, 1)
            for n in range(NCH):
                pe.wait_ge(w_in[n], 16)
                for j in range(4):
                    for kk in range(KD):
                        mm = nc.tensor.matmul(pm[:, 2 * (4 * n + j):2 * (4 * n + j + 1)],
                                              wa[:, n, kk, j * P:(j + 1) * P], sc[:, kk, :],
                                              start=(kk == 0), stop=(kk == KD - 1))
                mm.then_inc(mod_psum, 1)


class Turn:
    def __init__(self, t, j, q):
        self.t, self.j, self.q, self.u = t, j, q, j % 2

    def ahead(self, n):
        return Turn(self.t + n, (self.j + n) % 4, self.q + (self.j + n) // 4)

    def within(self, n):
        return not isinstance(self.t, int) or self.t + n < NT


def turns_of_four(eng, body):
    for t in range(4):
        body(Turn(t, t, 0))
    with eng.Fori(1, NPT // 4 - 1) as q:
        for j in range(4):
            body(Turn(4 * q + j, j, q))
    for t in range(NPT - 4, NT):
        body(Turn(t, t % 4, t // 4))


def normalise(k, c, src, scale, shift0, hH, hL, name="a"):
    nc, d = k.nc, k.d
    NX = 4
    x_in = [k.sem(f"x_loaded{n}") for n in range(NX)]
    ssq_ready, std_ready, rstd_ready, x_scaled, x_turned, h_full, h_high, h_low = k.sems(
        "squares_summed", "std_ready", "rstd_ready", "x_scaled", "x_turned", "h_full", "h_high", "h_low")
    with ExitStack() as s:
        x = sbuf(nc, s, name + "nx", [P, NX, D])
        sq = sbuf(nc, s, name + "nsq", [P, D])
        tmp = sbuf(nc, s, name + "ntmp", [P, 2, KD, P])
        st = sbuf(nc, s, name + "nst", [P, NX, 3])
        pT = psum(nc, s, name + "npT", [P, 2, D])
        block = s.enter_context(nc.Block())
        eps = c["eps"]

        @block.sync
        def _(sp):
            def load(i):
                at_least(sp, x_turned, i.t - NX + 1)
                sp.dma_start(x[:, i.j], src[tok(i.t), :]).then_inc(x_in[i.j], 16)
            turns_of_four(sp, load)

        @block.scalar
        def _(act):
            def spread(i):
                act.wait_ge(x_in[i.j], 16 * i.q + 16)
                at_least(act, x_scaled, i.t - NX + 1)
                nc.scalar.activation(sq[:], x[:, i.j], ACT.Square, accum_out=st[:, i.j, 0:1]).then_inc(ssq_ready, 1)
                act.wait_ge(ssq_ready, i.t + 1)
                nc.scalar.activation(st[:, i.j, 1:2], st[:, i.j, 0:1], ACT.Sqrt, bias=eps[:],
                                     scale=1.0 / D).then_inc(std_ready, 1)

            def slot(i):
                if i.within(3):
                    spread(i.ahead(3))
                act.wait_ge(h_full, i.t + 1)
                nc.scalar.activation(hH[:, :, tok(i.t)], tmp[:, i.u], ACT.Copy).then_inc(h_high, 1)
            for t in range(3):
                spread(Turn(t, t, 0))
            turns_of_four(act, slot)

        @block.vector
        def _(dve):
            def scale_rows(i):
                dve.wait_ge(std_ready, i.t + 1)
                nc.vector.reciprocal(st[:, i.j, 2:3], st[:, i.j, 1:2]).then_inc(rstd_ready, 1)
                dve.wait_ge(rstd_ready, i.t + 1)
                nc.vector.tensor_scalar(x[:, i.j], x[:, i.j], st[:, i.j, 2:3], None, ALU.mult).then_inc(x_scaled, 1)

            def slot(i):
                if i.within(2):
                    scale_rows(i.ahead(2))
                which = 1 if isinstance(i.t, int) and i.t == NPT else 0
                dve.wait_ge(x_turned, i.t + 1)
                at_least(dve, h_high, i.t - 1)
                at_least(dve, h_low, i.t - 1)
                for kk in range(KD):
                    op = nc.vector.tensor_scalar(tmp[:, i.u, kk], pT[:, i.u, kk * P:(kk + 1) * P],
                                                 scale[:, kk, which:which + 1],
                                                 c["mod"][:, shift0 + kk, which:which + 1], ALU.mult, ALU.add)
                op.then_inc(h_full, 1)
            for t in range(2):
                scale_rows(Turn(t, t, 0))
            turns_of_four(dve, slot)

        @block.gpsimd
        def _(pool):
            def low(i):
                pool.wait_ge(h_high, i.t + 1)
                nc.gpsimd.tensor_tensor(hL[:, :, tok(i.t)], tmp[:, i.u], hH[:, :, tok(i.t)].bitcast(F32),
                                        ALU.subtract).then_inc(h_low, 1)
            turns_of_four(pool, low)

        @block.tensor
        def _(pe):
            def turn(i):
                pe.wait_ge(x_scaled, i.t + 1)
                at_least(pe, h_full, i.t - 1)
                for kk in range(KD):
                    mm = nc.tensor.transpose(pT[:, i.u, kk * P:(kk + 1) * P], x[:, i.j, kk * P:(kk + 1) * P],
                                             c["ident"][:])
                mm.then_inc(x_turned, 1)
            turns_of_four(pe, turn)


def project(k, c, hH, hL, w_dram, group0, n_groups, out_dram, normed):
    nc, d = k.nc, k.d
    NB, NS, NR, NW = 5 if normed else 6, 4, 4, 11 if normed else 12
    raw_in = [k.sem(f"w_raw_loaded{n}") for n in range(NR)]
    w_high, w_low, w_used, summed, taken = k.sems("w_high", "w_low", "w_used", "projected", "psum_taken")
    stored = [k.sem(f"proj_stored{n}") for n in range(NS)]
    if normed:
        squared, reduced, std_ready, rstd_ready, scaled, weighted, norm_in, q_scaled, turned, turn_taken = k.sems(
            "squared", "reduced", "std_ready", "rstd_ready", "scaled", "weighted", "norm_w_loaded", "q_weight_scaled",
            "qk_turned", "turn_taken")
        turn_stored = [k.sem("turn_stored0"), k.sem("turn_stored1")]
    done = weighted if normed else taken
    AHEAD = NW - KD
    with ExitStack() as s:
        raw = sbuf(nc, s, f"praw{group0}", [P, NR, W5])
        wH = sbuf(nc, s, f"pwH{group0}", [P, NW, W5], F32R)
        wL = sbuf(nc, s, f"pwL{group0}", [P, NW, W5], F32R)
        stage = sbuf(nc, s, f"pstage{group0}", [P, NS, W5])
        acc = psum(nc, s, f"pacc{group0}", [P, NB, W5])
        if normed:
            nst = sbuf(nc, s, "pnst", [P, 2, 3, SH])
            nw = sbuf(nc, s, "pnw", [P, 2, SD])
            sq = psum(nc, s, "psq", [P, 2, W5])
            pT = psum(nc, s, "ppT", [P, 4, P])
            xT = sbuf(nc, s, "pxT", [P, 2, 4, P])
        block = s.enter_context(nc.Block())

        def slot(eng, g, kk):
            return bass.ds(eng.snap((g * KD + kk) % NW), 1)

        def stored_before(eng, g, t):
            rank, per = t // NS, len(range(t % NS, NT, NS))
            if not (isinstance(g, int) and g == 0 and rank == 0):
                eng.wait_ge(stored[t % NS], 16 * (g * per + rank))

        @block.sync
        def _(sp):
            def load(g, kk, first=False):
                if not (first and kk < NR):
                    sp.wait_ge(w_low, g * KD + kk - NR + 1)
                sp.dma_start(raw[:, kk % NR],
                             w_dram[bass.ds(group0 + g, 1), kk * P:(kk + 1) * P, :].rearrange("o p n -> (o p) n")
                             ).then_inc(raw_in[kk % NR], 16)

            def group(g, last):
                for t in range(NT):
                    if t % 2 == 0 and t // 2 < KD and not last:
                        load(g + 1, t // 2)
                    sp.wait_ge(done, g * NT + t + 1)
                    dst = out_dram[bass.ds(group0 + g, 1), t * P:(t + 1) * P, :].rearrange("o p n -> (o p) n")
                    sp.dma_start(dst, stage[:, t % NS]).then_inc(stored[t % NS], 16)
            for kk in range(KD):
                load(0, kk, True)
            if n_groups > 1:
                with sp.Fori(0, n_groups - 1) as g:
                    group(g, False)
            group(n_groups - 1, True)
            for n in range(NS):
                sp.wait_ge(stored[n], 16 * n_groups * len(range(n, NT, NS)))

        @block.scalar
        def _(act):
            def split(g, kk, free=False):
                act.wait_ge(raw_in[kk % NR], 16 * (g * (KD // NR) + kk // NR + 1))
                if not free and kk < AHEAD:
                    act.wait_ge(summed, (g - 1) * NT)
                elif not free:
                    act.wait_ge(w_used, (g - 1) * (KD - AHEAD) + kk - AHEAD + 1)
                nc.scalar.activation(wH[:, slot(act, g, kk), :], raw[:, kk % NR].unsqueeze(1),
                                     ACT.Copy).then_inc(w_high, 1)

            def take(g, t):
                stored_before(act, g, t)
                if normed:
                    rank = t // NS
                    at_least(act, turned, g * NT + t - NS + 1 if rank else (g - 1) * NT + max(range(t % NS, NT, NS)) + 1)
                act.wait_ge(summed, g * NT + t + 1)
                nc.scalar.activation(stage[:, t % NS], acc[:, t % NB], ACT.Copy).then_inc(taken, 1)

            def std(g, t):
                act.wait_ge(reduced, g * NT + t + 1)
                nc.scalar.activation(nst[:, t % 2, 1], nst[:, t % 2, 0], ACT.Sqrt, bias=c["eps"][:],
                                     scale=1.0 / SD).then_inc(std_ready, 1)

            def take_turned(n):
                act.wait_ge(turned, n + 1)
                at_least(act, turn_stored[n % 2], 16 * (n // 2))
                nc.scalar.activation(xT[:, n % 2], pT[:], ACT.Copy).then_inc(turn_taken, 1)

            def group(g, last, first=False):
                for t in range(NT):
                    if normed and g * NT + t >= 2:
                        take_turned(g * NT + t - 2)
                    take(g, t)
                    if normed:
                        std(g, t)
                    if t % 2 == 1 and t // 2 < AHEAD and not last:
                        split(g + 1, t // 2, free=first)
                if not last:
                    for kk in range(AHEAD, KD):
                        split(g + 1, kk)
            for kk in range(KD):
                split(0, kk, free=True)
            group(0, n_groups == 1, first=True)
            if n_groups > 2:
                with act.Fori(1, n_groups - 1) as g:
                    group(g, False)
            if n_groups > 1:
                group(n_groups - 1, True)
            for n in range(n_groups * NT - 2, n_groups * NT) if normed else ():
                take_turned(n)

        @block.gpsimd
        def _(pool):
            if normed:
                pool.dma_start(nw[:], d["sb_norms"]).then_inc(norm_in, 16)

            def store_turned(n):
                g, t = n // NT, n % NT
                pool.wait_ge(turn_taken, n + 1)
                dst = d["qk_T"][g, :, :, t * P:(t + 1) * P].rearrange("(j a) e t -> (a e) j t", a=2)
                pool.dma_start(dst, xT[:, n % 2]).then_inc(turn_stored[n % 2], 16)

            def split_low(g, kk):
                pool.wait_ge(w_high, g * KD + kk + 1)
                at = slot(pool, g, kk)
                nc.gpsimd.tensor_tensor(wL[:, at, :], raw[:, kk % NR].unsqueeze(1),
                                        wH[:, at, :].bitcast(F32), ALU.subtract).then_inc(w_low, 1)
            if normed:
                for kk in range(KD):
                    split_low(0, kk)
                for g in range(n_groups):
                    for t in range(NT):
                        if t % 2 == 1 and t // 2 < AHEAD and g + 1 < n_groups:
                            split_low(g + 1, t // 2)
                        if g * NT + t >= 2:
                            store_turned(g * NT + t - 2)
                    for kk in range(AHEAD, KD):
                        if g + 1 < n_groups:
                            split_low(g + 1, kk)
                for n in range(n_groups * NT - 2, n_groups * NT):
                    store_turned(n)
                for u in range(2):
                    pool.wait_ge(turn_stored[u], 16 * n_groups * NT // 2)
            else:
                with pool.Fori(0, n_groups) as g:
                    for kk in range(KD):
                        split_low(g, kk)

        if normed:
            @block.vector
            def _(dve):
                dve.wait_ge(norm_in, 16)
                nc.vector.tensor_scalar(nw[:, 0], nw[:, 0], SD ** -0.5, None, ALU.mult).then_inc(q_scaled, 1)
                dve.wait_ge(q_scaled, 1)
                with dve.Fori(0, n_groups) as g:
                    for t in range(NT):
                        n = g * NT + t
                        st = stage[:, t % NS]
                        heads = st.rearrange("p (h e) -> p h e", e=SD)
                        dve.wait_ge(taken, n + 1)
                        nc.vector.tensor_tensor(sq[:, t % 2], st, st, ALU.mult).then_inc(squared, 1)
                        dve.wait_ge(squared, n + 1)
                        nc.vector.tensor_reduce(nst[:, t % 2, 0], sq[:, t % 2].rearrange("p (h e) -> p h e", e=SD),
                                                AX.X, ALU.add).then_inc(reduced, 1)
                        dve.wait_ge(std_ready, n + 1)
                        nc.vector.reciprocal(nst[:, t % 2, 2], nst[:, t % 2, 1]).then_inc(rstd_ready, 1)
                        dve.wait_ge(rstd_ready, n + 1)
                        nc.vector.tensor_tensor(heads, heads, nst[:, t % 2, 2].unsqueeze(2).to_broadcast([P, SH, SD]),
                                                ALU.mult).then_inc(scaled, 1)
                        dve.wait_ge(scaled, n + 1)
                        nc.vector.tensor_tensor(heads, heads, nw[:, bass.ds(g, 1), :].to_broadcast([P, SH, SD]),
                                                ALU.mult).then_inc(weighted, 1)

        @block.tensor
        def _(pe):
            def group(g, first):
                at = [slot(pe, g, kk) for kk in range(KD)]
                for t in range(NT):
                    if t >= NB:
                        pe.wait_ge(taken, g * NT + t - NB + 1)
                    elif t == 0 and not first:
                        pe.wait_ge(taken, g * NT)
                    for kk in range(KD):
                        if t == 0:
                            pe.wait_ge(w_high, g * KD + kk + 1)
                            pe.wait_ge(w_low, g * KD + kk + 1)
                        for n, (a, w) in enumerate(((hH, wH), (hL, wH), (hH, wL))):
                            mm = nc.tensor.matmul(acc[:, t % NB].unsqueeze(1), a[:, kk, t * P:(t + 1) * P],
                                                  w[:, at[kk], :], start=(kk == 0 and n == 0),
                                                  stop=(kk == KD - 1 and n == 2))
                        if t == NT - 1 and kk < KD - AHEAD:
                            mm.then_inc(w_used, 1)
                    mm.then_inc(summed, 1)
                    if normed and g * NT + t >= 2:
                        turn(g * NT + t - 2)

            def turn(n):
                pe.wait_ge(weighted, n + 1)
                at_least(pe, turn_taken, n)
                for j in range(4):
                    mm = nc.tensor.transpose(pT[:, j], stage[:, n % NT % NS, j * P:(j + 1) * P], c["ident"][:])
                mm.then_inc(turned, 1)
            group(0, True)
            if normed:
                group(1, False)
                turn(2 * NT - 2)
                turn(2 * NT - 1)
            elif n_groups > 1:
                with pe.Fori(1, n_groups) as g:
                    group(g, False)


def project_gates(k, c, hH, hL):
    nc, d = k.nc, k.d
    raw_in, high, low, summed, taken, stored = k.sems("wg_loaded", "wg_high", "wg_low", "gates_summed", "gates_taken",
                                                      "gates_stored")
    spans = [(n * W5, W5) for n in range(SEQ // W5)] + [(SEQ, P)]
    with ExitStack() as s:
        raw = sbuf(nc, s, "graw", [P, KD, 8])
        wH = sbuf(nc, s, "gwH", [P, KD, 8], F32R)
        wL = sbuf(nc, s, "gwL", [P, KD, 8], F32R)
        out = sbuf(nc, s, "gout", [8, TOK])
        acc = psum(nc, s, "gacc", [8, 5, W5])
        block = s.enter_context(nc.Block())

        @block.sync
        def _(sp):
            sp.dma_start(raw[:], d["w_gate"].rearrange("(k p) n -> p k n", p=P)).then_inc(raw_in, 16)
            sp.wait_ge(taken, len(spans))
            sp.dma_start(d["gates_d"], out[:]).then_inc(stored, 16)
            sp.wait_ge(stored, 16)

        @block.vector
        def _(dve):
            dve.wait_ge(raw_in, 16)
            nc.vector.tensor_copy(wH[:], raw[:]).then_inc(high, 1)
            dve.wait_ge(high, 1)
            nc.vector.tensor_tensor(wL[:], raw[:], wH[:].bitcast(F32), ALU.subtract).then_inc(low, 1)
            for n, (a, w) in enumerate(spans):
                dve.wait_ge(summed, n + 1)
                nc.vector.tensor_copy(out[:, a:a + w], acc[:, n, 0:w]).then_inc(taken, 1)

        @block.tensor
        def _(pe):
            pe.wait_ge(low, 1)
            for n, (a, w) in enumerate(spans):
                for kk in range(KD):
                    for m, (wt, h) in enumerate(((wH, hH), (wH, hL), (wL, hH))):
                        mm = nc.tensor.matmul(acc[:, n, 0:w], wt[:, kk], h[:, kk, a:a + w],
                                              start=(kk == 0 and m == 0), stop=(kk == KD - 1 and m == 2))
                mm.then_inc(summed, 1)


LEADS = dict(A=-1, E=2, L=2, LO=0, SP=1, B=3, AL=-2, z=4, av=-3)


def attention(k, c):
    nc, d = k.nc, k.d
    NG = SEQ // W5
    steps = [(T, b) for T in reversed(range(NG)) for b in reversed(range(4 * T + 4))]
    N = len(steps)
    NZ, R = 5, 4
    x_in = [k.sem("qkv_loaded0"), k.sem("qkv_loaded1")]
    (z_ready, e_ready, l_ready, sp_ready, high, low, later_ready, z_full, a_ready, ah_ready, al_ready, av_done,
     o_taken, folded, fold_taken, raw_sp, z_bound, ops_high, ops_ready) = k.sems(
        "z_ready", "exp_ready", "ln_ready", "softplus_ready", "softplus_high", "softplus_low", "later_sum_ready",
        "exponent_ready", "a_ready", "a_high", "a_low", "av_done", "o_taken", "o_folded", "fold_taken", "softplus_raw",
        "z_bounded", "operands_high", "operands_ready")
    stored = [k.sem("o_stored0"), k.sem("o_stored1")]
    with ExitStack() as s:
        Q = sbuf(nc, s, "aq", [P, 2, SEQ], F32R)
        K = sbuf(nc, s, "ak", [P, SEQ], F32R)
        V = sbuf(nc, s, "av", [P, NPT, 2, SD], F32R)
        xq = sbuf(nc, s, "axq", [P, 2, W5])
        xk = sbuf(nc, s, "axk", [P, 2, W5])
        xv = sbuf(nc, s, "axv", [P, 2, 4, SD])
        ring = {n: sbuf(nc, s, f"a{n}", [P, R, W5], dt) for n, dt in (
            ("E", F32), ("L", F32), ("SP", F32), ("SH", F32R), ("SL", F32R), ("A", F32), ("AH", F32R), ("AL", F32R),
            ("CA", F32))}
        Osb = sbuf(nc, s, "aO", [P, 2, W5])
        of = sbuf(nc, s, "aof", [P, 2, 4, SD])
        Z = psum(nc, s, "a_z", [P, NZ, W5])
        O = psum(nc, s, "a_out", [P, 2, W5])
        F = psum(nc, s, "a_fold", [P, 4, SD])
        block = s.enter_context(nc.Block())
        last = {m: T for m, (T, b) in enumerate(steps) if b == 0}
        first = {m: T for m, (T, b) in enumerate(steps) if b == 4 * T + 3}

        def cols(m):
            T, b = steps[m]
            return slice(max(0, b - 4 * T) * P, W5)

        def own(m):
            T, b = steps[m]
            return slice((b - 4 * T) * P, (b - 4 * T + 1) * P) if b >= 4 * T else None

        def at(name, m, span=None):
            return ring[name][:, m % R, span or cols(m)]

        def freed(eng, sem, h, m, depth=R):
            at_least(eng, sem, h * N + m - depth + 1)

        def pipeline(eng, ops):
            def slots(h, span, back, ahead):
                for n in span:
                    for op, lead in ops:
                        m = n + lead
                        if 0 <= m < N:
                            op(h, m)
                        elif m < 0 and back:
                            op(h - 1, m + N)
                        elif m >= N and ahead:
                            op(h + 1, m - N)
            most, least = max(0, *(a for _, a in ops)), min(0, *(a for _, a in ops))
            slots(0, range(-most, N), False, True)
            with eng.Fori(1, SH - 1) as h:
                slots(h, range(N), True, True)
            slots(SH - 1, range(N - least), True, False)

        def next_group(body):
            def op(h, m):
                if m in last and not (isinstance(h, int) and h == SH - 1):
                    body(h + 1, NG - 1 - last[m], m)
            return op

        @block.sync
        def _(sp):
            def load(h, n):
                G = NG - 1 - n
                at_least(sp, ops_ready, h * NG + n - 1)
                for x, which in ((xq, 0), (xk, 1)):
                    src = d["qk_T"][which, bass.ds(h, 1), :, G * W5:(G + 1) * W5].rearrange("o e t -> (o e) t")
                    for half in range(2):
                        sp.dma_start(x[half * SD:(half + 1) * SD, n % 2], src).then_inc(x_in[n % 2], 16)
                sp.dma_start(xv[:, n % 2], d["proj_out"][4, G * W5:(G + 1) * W5, bass.ds(h * SD, SD)]
                             .rearrange("(b p) e -> p b e", p=P)).then_inc(x_in[n % 2], 16)

            def store(h, n):
                G = NG - 1 - n
                sp.wait_ge(fold_taken, h * NG + n + 1)
                dst = d["o_d"][bass.ds(G * W5, W5), bass.ds(h * SD, SD)].rearrange("(j p) e -> p j e", p=P)
                sp.dma_start(dst, of[:, n % 2]).then_inc(stored[n % 2], 16)
            for n in range(NG):
                load(0, n)
            with sp.Fori(0, SH - 1) as h:
                for n in range(NG):
                    load(h + 1, n)
                    store(h, n)
            for n in range(NG):
                store(SH - 1, n)
            for n in range(2):
                sp.wait_ge(stored[n], 16 * SH * NG // 2)

        @block.scalar
        def _(act):
            def E(h, m):
                act.wait_ge(z_bound, h * N + m + 1)
                nc.scalar.activation(at("E", m), at("E", m), ACT.Exp).then_inc(e_ready, 1)

            def L(h, m):
                act.wait_ge(e_ready, h * N + m + 1)
                freed(act, raw_sp, h, m)
                nc.scalar.activation(at("L", m), at("E", m), ACT.Ln, bias=1.0).then_inc(l_ready, 1)

            def A(h, m):
                act.wait_ge(z_full, h * N + m + 1)
                freed(act, al_ready, h, m)
                nc.scalar.activation(at("A", m), Z[:, m % NZ, cols(m)], ACT.Exp).then_inc(a_ready, 1)
                freed(act, av_done, h, m)
                nc.scalar.activation(at("AH", m), Z[:, m % NZ, cols(m)], ACT.Exp).then_inc(ah_ready, 1)

            def split(h, n, m=None):
                G = NG - 1 - n
                span = slice(G * W5, (G + 1) * W5)
                act.wait_ge(x_in[n % 2], 80 * (h * (NG // 2) + n // 2 + 1))
                if m is not None:
                    act.wait_ge(av_done, (h - 1) * N + m + 1)
                cp = nc.scalar.activation
                cp(K[:, span], xk[:, n % 2], ACT.Copy)
                cp(Q[:, 0, span], xq[:, n % 2], ACT.Copy)
                cp(Q[:, 1, span], xq[:, n % 2], ACT.Copy)
                cp(V[:, 4 * G:4 * G + 4, 0, :], xv[:, n % 2], ACT.Copy).then_inc(ops_high, 1)
            act.preload_act_table_set("natural_log_exp_and_others")
            for n in range(NG):
                split(0, n)
            pipeline(act, [(A, LEADS["A"]), (E, LEADS["E"]), (L, LEADS["L"]), (next_group(split), -4)])

        @block.vector
        def _(dve):
            v = nc.vector

            def SP(h, m):
                dve.wait_ge(l_ready, h * N + m + 1)
                freed(dve, later_ready, h, m)
                freed(dve, low, h, m)
                v.tensor_tensor(at("SP", m), at("L", m), Z[:, m % NZ, cols(m)], ALU.max).then_inc(raw_sp, 1)
                if own(m):
                    dve.wait_ge(raw_sp, h * N + m + 1)
                    v.tensor_tensor(at("SP", m, own(m)), at("SP", m, own(m)), c["keep"][:], ALU.mult).then_inc(sp_ready, 1)

            def BOUND(h, m):
                dve.wait_ge(z_ready, h * N + m + 1)
                freed(dve, l_ready, h, m)
                v.tensor_scalar(at("E", m), Z[:, m % NZ, cols(m)], 41.0, None, ALU.min).then_inc(z_bound, 1)

            def LO(h, m):
                dve.wait_ge(high, h * N + m + 1)
                freed(dve, z_full, h, m)
                v.tensor_tensor(at("SL", m), at("SP", m), at("SH", m).bitcast(F32), ALU.subtract).then_inc(low, 1)

            def AL(h, m):
                dve.wait_ge(a_ready, h * N + m + 1)
                dve.wait_ge(ah_ready, h * N + m + 1)
                freed(dve, av_done, h, m)
                v.tensor_tensor(at("AL", m), at("A", m), at("AH", m).bitcast(F32), ALU.subtract).then_inc(al_ready, 1)

            def OUT(h, m):
                if m in last:
                    n = NG - 1 - last[m]
                    dve.wait_ge(av_done, h * N + m + 1)
                    at_least(dve, folded, h * NG + n - 1)
                    v.tensor_copy(Osb[:, n % 2], O[:, n % 2]).then_inc(o_taken, 1)

            def FOLDED(h, m):
                if m in last:
                    n = NG - 1 - last[m]
                    dve.wait_ge(folded, h * NG + n + 1)
                    at_least(dve, stored[n % 2], 16 * (h * (NG // 2) + n // 2))
                    v.tensor_copy(of[:, n % 2], F[:]).then_inc(fold_taken, 1)

            def split(h, n, m=None):
                G = NG - 1 - n
                span = slice(G * W5, (G + 1) * W5)
                top, bottom = slice(0, SD), slice(SD, P)
                dve.wait_ge(ops_high, h * NG + n + 1)
                for dst, x, rows in ((K[:, span], xk[:, n % 2], bottom), (Q[:, 0, span], xq[:, n % 2], bottom),
                                     (Q[:, 1, span], xq[:, n % 2], top)):
                    v.tensor_tensor(dst[rows], x[rows], dst[rows].bitcast(F32), ALU.subtract)
                blocks = slice(4 * G, 4 * G + 4)
                v.tensor_tensor(V[:, blocks, 1, :], xv[:, n % 2], V[:, blocks, 0, :].bitcast(F32),
                                ALU.subtract).then_inc(ops_ready, 1)
            for n in range(NG):
                split(0, n)
            pipeline(dve, [(LO, LEADS["LO"]), (SP, LEADS["SP"]), (BOUND, LEADS["B"]), (AL, LEADS["AL"]), (OUT, -4),
                           (FOLDED, -6), (next_group(split), -5)])

        @block.gpsimd
        def _(pool):
            ones = lambda n: c["one"][:].to_broadcast([P, n])
            masked = [sum(own(x) is not None for x in range(m + 1)) for m in range(N)]
            tt = nc.gpsimd.tensor_tensor

            def HI(h, m):
                pool.wait_ge(raw_sp, h * N + m + 1)
                at_least(pool, sp_ready, h * masked[-1] + masked[m])
                freed(pool, z_full, h, m)
                tt(at("SH", m), at("SP", m), ones(W5 - cols(m).start), ALU.mult).then_inc(high, 1)

            def SUM(h, m):
                at_least(pool, later_ready, h * N + m)
                freed(pool, z_full, h, m + 1)
                rest = slice(cols(m).start + (P if own(m) else 0), W5)
                if own(m):
                    op = tt(at("CA", m + 1, own(m)), at("SP", m, own(m)), ones(P), ALU.mult)
                if rest.start < W5:
                    op = tt(at("CA", m + 1, rest), at("CA", m, rest), at("SP", m, rest), ALU.add)
                op.then_inc(later_ready, 1)
            pipeline(pool, [(HI, 1), (SUM, 1)])

        @block.tensor
        def _(pe):
            go = dict(start=False, stop=True, skip_group_check=True)

            def z(h, m):
                T, b = steps[m]
                if T == NG - 1 and b % 4 == 3:
                    pe.wait_ge(ops_ready, h * NG + NG - b // 4)
                freed(pe, ah_ready, h, m, NZ)
                span = slice(4 * T * P + cols(m).start, 4 * T * P + W5)
                for part in range(2):
                    mm = nc.tensor.matmul(Z[:, m % NZ, cols(m)], K[:, b * P:(b + 1) * P], Q[:, part, span],
                                          start=(part == 0), stop=(part == 1))
                mm.then_inc(z_ready, 1)

            def sub(h, m):
                to = Z[:, m % NZ]
                pe.wait_ge(raw_sp, h * N + m + 1)
                if m not in first:
                    rest = slice(cols(m).start + (P if own(m) else 0), W5)
                    pe.wait_ge(later_ready, h * N + m)
                    nc.tensor.matmul(to[:, rest], c["nones"][:], at("CA", m, rest), **go)
                if own(m):
                    nc.tensor.matmul(to[:, own(m)], c["ident_r"][:], c["far_r"][:], **go)
                pe.wait_ge(high, h * N + m + 1)
                nc.tensor.matmul(to[:, cols(m)], c["tri_r"][:], at("SH", m), **go)
                pe.wait_ge(low, h * N + m + 1)
                nc.tensor.matmul(to[:, cols(m)], c["tri_r"][:], at("SL", m), **go).then_inc(z_full, 1)

            def av(h, m):
                T, b = steps[m]
                n = NG - 1 - T
                if m in first:
                    at_least(pe, o_taken, h * NG + n - 1)
                vb = V[:, b].rearrange("p n e -> p (n e)")
                pe.wait_ge(ah_ready, h * N + m + 1)
                nc.tensor.matmul(O[:, n % 2, cols(m)], vb, at("AH", m), start=(m in first), stop=False,
                                 skip_group_check=True)
                pe.wait_ge(al_ready, h * N + m + 1)
                nc.tensor.matmul(O[:, n % 2, cols(m)], vb, at("AL", m), start=False, stop=(m in last),
                                 skip_group_check=True).then_inc(av_done, 1)

            def fold(h, m):
                if m in last:
                    n = NG - 1 - last[m]
                    pe.wait_ge(o_taken, h * NG + n + 1)
                    at_least(pe, fold_taken, h * NG + n)
                    for j in range(4):
                        mm = nc.tensor.matmul(F[:, j, :], Osb[:, n % 2, j * P:(j + 1) * P], c["fold"][:],
                                              start=(j == 0), stop=True, skip_group_check=True)
                    mm.then_inc(folded, 1)
            pipeline(pe, [(sub, 0), (z, LEADS["z"]), (av, LEADS["av"]), (fold, -5)])


def attention_sample(k, c):
    nc, d = k.nc, k.d
    N, NZ, W = NPB + 1, 3, SH * DEC
    qk_high, qk_low, qk_turned, qk_taken, v_in, v_high, v_low = k.sems(
        "qk_high", "qk_low", "qk_turned", "qk_taken", "v_loaded", "v_high", "v_low")
    (q_in, k_in, z_ready, z_bound, e_ready, l_ready, sp_raw, sp_ready, high, low, later_ready, z_full, a_ready, ah_ready,
     al_ready, av_done, zeroed, o_taken, folded, fold_taken, stored) = k.sems(
        "q_loaded", "k_loaded", "z_ready", "z_bounded", "exp_ready", "ln_ready", "softplus_raw", "softplus_ready",
        "softplus_high", "softplus_low", "later_sum_ready", "exponent_ready", "a_ready", "a_high", "a_low", "av_done",
        "zeroed", "o_taken", "o_folded", "fold_taken", "o_stored")
    with ExitStack() as s:
        q = sbuf(nc, s, "bq", [P, 2, SH, P], F32R)
        K = sbuf(nc, s, "bK", [P, N, SH, P], F32R)
        V = sbuf(nc, s, "bV", [P, N, SH, 2, SD], F32R)
        xq = sbuf(nc, s, "bxq", [P, SH, SD])
        xk = sbuf(nc, s, "bxk", [P, N, W5])
        xv = sbuf(nc, s, "bxv", [P, N, W5])
        parts = sbuf(nc, s, "bparts", [P, 2, SH, 3, SD], F32R)
        ring = {n: sbuf(nc, s, f"b{n}", [P, 2, W], dt) for n, dt in (
            ("E", F32), ("L", F32), ("SP", F32), ("SH", F32R), ("SL", F32R), ("A", F32), ("AH", F32R), ("AL", F32R),
            ("CA", F32))}
        Osb = sbuf(nc, s, "bO", [P, W])
        out = sbuf(nc, s, "bout", [P, W5])
        Z = psum(nc, s, "b_z", [P, NZ, W5])
        O = psum(nc, s, "b_out", [P, W5])
        F = psum(nc, s, "b_fold", [DEC, W5])
        pT = psum(nc, s, "b_turn", [P, 2, 4, P])
        block = s.enter_context(nc.Block())
        heads = lambda ap: ap.rearrange("p (h t) -> p h t", t=DEC)
        over_heads = lambda ap: ap[:, 0:DEC].unsqueeze(1).to_broadcast([P, SH, DEC])
        col = lambda h: slice(h * DEC, (h + 1) * DEC)

        @block.sync
        def _(sp):
            own = tok(NPT)
            sp.dma_start(xq[:].rearrange("p h e -> p (h e)"), d["proj_out"][5, own, :]).then_inc(q_in, 16)
            for x, g, cache, sem in ((xk, 6, "past_k", k_in), (xv, 4, "past_v", v_in)):
                sp.dma_start(x[:, 0], d["proj_out"][g, own, :]).then_inc(sem, 16)
                sp.dma_start(x[:, 1:], d[cache].rearrange("(b p) n -> p b n", p=P)).then_inc(sem, 16)
            sp.wait_ge(fold_taken, 1)
            sp.dma_start(d["o_d"][SEQ:, :], out[:]).then_inc(stored, 16)
            sp.wait_ge(stored, 16)

        def blk(m):
            return 0 if m == 0 else NPB + 1 - m

        turns = [(None, half, form, q[:, form, 4 * half:4 * half + 4]) for form in range(2) for half in range(2)]
        turns += [(n, half, 0, K[:, n, 4 * half:4 * half + 4]) for n in range(N) for half in range(2)]
        turns_of = lambda i: range(0, 4) if i == 0 else range(2 * i + 2, 2 * i + 4)

        @block.scalar
        def _(act):
            def parts_high(i):
                if i > 0:
                    act.wait_ge(k_in, 32)
                else:
                    act.wait_ge(q_in, 16)
                if i >= 2:
                    act.wait_ge(qk_turned, turns_of(i - 2)[-1] + 1)
                src = xq[:] if i == 0 else xk[:, i - 1].rearrange("p (h e) -> p h e", e=SD)
                for part in (0, 2) if i == 0 else (0,):
                    op = nc.scalar.activation(parts[:, i % 2, :, part], src, ACT.Copy)
                op.then_inc(qk_high, 1)
            parts_high(0)
            for i in range(N + 1):
                if i < N:
                    parts_high(i + 1)
                for n in turns_of(i):
                    act.wait_ge(qk_turned, n + 1)
                    nc.scalar.activation(turns[n][3], pT[:, n % 2], ACT.Copy).then_inc(qk_taken, 1)
            act.preload_act_table_set("natural_log_exp_and_others")
            for m in range(N + 1):
                if m < N:
                    act.wait_ge(z_bound, m + 1)
                    at = ring["E"][:, m % 2]
                    nc.scalar.activation(at, at, ACT.Exp).then_inc(e_ready, 1)
                    act.wait_ge(e_ready, m + 1)
                    if m >= 2:
                        act.wait_ge(sp_raw, m - 1)
                    nc.scalar.activation(ring["L"][:, m % 2], at, ACT.Ln, bias=1.0).then_inc(l_ready, 1)
                n = m - 1
                if n >= 0:
                    act.wait_ge(z_full, n + 1)
                    if n >= 2:
                        act.wait_ge(al_ready, n - 1)
                        act.wait_ge(av_done, n - 1)
                    nc.scalar.activation(ring["A"][:, n % 2], Z[:, n % NZ, 0:W], ACT.Exp).then_inc(a_ready, 1)
                    nc.scalar.activation(ring["AH"][:, n % 2], Z[:, n % NZ, 0:W], ACT.Exp).then_inc(ah_ready, 1)

        @block.vector
        def _(dve):
            v = nc.vector

            def bound(m):
                dve.wait_ge(z_ready, m + 1)
                if m >= 2:
                    dve.wait_ge(l_ready, m - 1)
                v.tensor_scalar(ring["E"][:, m % 2], Z[:, m % NZ, 0:W], 41.0, None, ALU.min).then_inc(z_bound, 1)
            for i in range(N + 1):
                src = xq[:] if i == 0 else xk[:, i - 1].rearrange("p (h e) -> p h e", e=SD)
                dve.wait_ge(qk_high, i + 1)
                v.tensor_tensor(parts[:, i % 2, :, 1], src, parts[:, i % 2, :, 0].bitcast(F32),
                                ALU.subtract).then_inc(qk_low, 1)
            dve.wait_ge(v_high, 1)
            v.tensor_tensor(V[:, :, :, 1], xv[:].rearrange("p b (h e) -> p b h e", e=SD), V[:, :, :, 0].bitcast(F32),
                            ALU.subtract).then_inc(v_low, 1)
            bound(0)
            for m in range(N):
                if m + 1 < N:
                    bound(m + 1)
                at = ring["SP"][:, m % 2]
                dve.wait_ge(l_ready, m + 1)
                if m >= 2:
                    dve.wait_ge(later_ready, m - 1)
                    dve.wait_ge(low, m - 1)
                    dve.wait_ge(high, m - 1)
                v.tensor_tensor(at, ring["L"][:, m % 2], Z[:, m % NZ, 0:W], ALU.max).then_inc(sp_raw, 1)
                if m == 0:
                    dve.wait_ge(sp_raw, 1)
                    v.tensor_tensor(heads(at), heads(at), over_heads(c["keep"]), ALU.mult).then_inc(sp_ready, 1)
                dve.wait_ge(high, m + 1)
                if m >= 2:
                    dve.wait_ge(z_full, m - 1)
                v.tensor_tensor(ring["SL"][:, m % 2], at, ring["SH"][:, m % 2].bitcast(F32), ALU.subtract).then_inc(low, 1)
                dve.wait_ge(ah_ready, m + 1)
                dve.wait_ge(a_ready, m + 1)
                if m >= 2:
                    dve.wait_ge(av_done, m - 1)
                v.tensor_tensor(ring["AL"][:, m % 2], ring["A"][:, m % 2], ring["AH"][:, m % 2].bitcast(F32),
                                ALU.subtract).then_inc(al_ready, 1)
            dve.wait_ge(av_done, N)
            v.tensor_copy(Osb[:], O[:, 0:W]).then_inc(o_taken, 1)
            dve.wait_ge(folded, 1)
            dve.wait_ge(zeroed, 2)
            v.tensor_copy(out[0:DEC, :], F[:]).then_inc(fold_taken, 1)

        @block.gpsimd
        def _(pool):
            g = nc.gpsimd
            pool.wait_ge(v_in, 32)
            g.tensor_copy(V[:, :, :, 0], xv[:].rearrange("p b (h e) -> p b h e", e=SD)).then_inc(v_high, 1)
            g.memset(ring["CA"][:], 0.0).then_inc(zeroed, 1)
            g.memset(out[:], 0.0).then_inc(zeroed, 1)
            pool.wait_ge(zeroed, 2)
            for m in range(N):
                pool.wait_ge(sp_raw, m + 1)
                pool.wait_ge(sp_ready, 1)
                if m >= 2:
                    pool.wait_ge(z_full, m - 1)
                g.tensor_copy(ring["SH"][:, m % 2], ring["SP"][:, m % 2]).then_inc(high, 1)
                if m > 0:
                    pool.wait_ge(later_ready, m)
                    pool.wait_ge(z_full, m)
                g.tensor_tensor(ring["CA"][:, (m + 1) % 2], ring["CA"][:, m % 2], ring["SP"][:, m % 2],
                                ALU.add).then_inc(later_ready, 1)

        @block.tensor
        def _(pe):
            mm = nc.tensor.matmul
            go = dict(start=False, stop=True, skip_group_check=True)

            def z(m):
                if m >= NZ:
                    pe.wait_ge(ah_ready, m - NZ + 1)
                for h in range(SH):
                    for part in range(2):
                        op = mm(Z[:, m % NZ, col(h)], K[:, blk(m), h], q[:, part, h, 0:DEC],
                                start=(h == 0 and part == 0), stop=(part == 1), skip_group_check=True)
                op.then_inc(z_ready, 1)

            def av(m):
                for n, (src, sem) in enumerate((("AH", ah_ready), ("AL", al_ready))):
                    pe.wait_ge(sem, m + 1)
                    for h in range(SH):
                        op = mm(O[:, col(h)], V[:, blk(m), h].rearrange("p n e -> p (n e)"), ring[src][:, m % 2, col(h)],
                                start=(m == 0 and n == 0 and h == 0), stop=(m == N - 1 and n == 1),
                                skip_group_check=True)
                op.then_inc(av_done, 1)
            for n, (blk_n, half, form, _) in enumerate(turns):
                i = 0 if blk_n is None else blk_n + 1
                pe.wait_ge(qk_low, i + 1)
                if n >= 2:
                    pe.wait_ge(qk_taken, n - 1)
                for h in range(4):
                    op = nc.tensor.transpose(pT[:, n % 2, h], parts[:, i % 2, 4 * half + h, form:form + 2]
                                             .rearrange("p n e -> p (n e)").bitcast(F32), c["ident"][:])
                op.then_inc(qk_turned, 1)
            pe.wait_ge(v_low, 1)
            pe.wait_ge(qk_taken, len(turns))
            z(0)
            for m in range(N):
                if m + 1 < N:
                    z(m + 1)
                if m > 0:
                    av(m - 1)
                at = Z[:, m % NZ, 0:W]
                pe.wait_ge(sp_raw, m + 1)
                if m > 0:
                    pe.wait_ge(later_ready, m)
                    mm(at, c["nones"][:], ring["CA"][:, m % 2], **go)
                else:
                    for h in range(SH):
                        mm(Z[:, 0, col(h)], c["ident_r"][:], c["far_r"][:, 0:DEC], **go)
                pe.wait_ge(high, m + 1)
                mm(at, c["tri_r"][:], ring["SH"][:, m % 2], **go)
                pe.wait_ge(low, m + 1)
                mm(at, c["tri_r"][:], ring["SL"][:, m % 2], **go).then_inc(z_full, 1)
            av(N - 1)
            pe.wait_ge(o_taken, 1)
            for h in range(SH):
                op = mm(F[:, h * SD:(h + 1) * SD], Osb[:, col(h)], c["fold"][:], start=(h == 0), stop=True,
                        skip_group_check=True)
            op.then_inc(folded, 1)


def gate_rows(k, c, gc, dec):
    nc, d = k.nc, k.d
    (loaded, mask_ready, biased, abs_ready, e_ready, l_ready, lf_ready, padded, b_ready, m_ready, mp_ready, u_ready, args_ready,
     w_ready, stored, zeroed, turned, taken, dec_args, dec_sum) = k.sems(
        "gates_loaded", "chunk_mask_ready", "gates_biased", "abs_ready", "exp_ready", "ln_ready", "log_forget_ready",
        "padding_set", "b_ready", "m_ready", "m_before_ready", "u_ready", "arguments_ready", "weights_ready", "rows_stored",
        "rows_zeroed", "weights_turned", "weights_taken", "decay_rows", "decay_sum")
    with ExitStack() as s:
        def row(name):
            return sbuf(nc, s, name, [MH, NT, P])
        IG, FG, AB, LF, B, M, U, G, cm = map(row, ("rIG", "rFG", "rAB", "rLF", "rB", "rM", "rU", "rG", "rcm"))
        gb = sbuf(nc, s, "rgb", [MH, 2])
        m0 = sbuf(nc, s, "rm0", [MH, 1])
        mp = sbuf(nc, s, "rmp", [MH, NT])
        dl = sbuf(nc, s, "rdl", [MH, NT])
        W = sbuf(nc, s, "rW", [96, NT, P])
        dd = sbuf(nc, s, "rdd", [MH, NT, MH])
        pw = psum(nc, s, "rpw", [P, 4, W5])
        pd = psum(nc, s, "rpd", [P, W5])
        block = s.enter_context(nc.Block())
        flat = lambda x: x[:].rearrange("h n t -> h (n t)")
        bc = lambda x: x.unsqueeze(2).to_broadcast([MH, NT, P])

        @block.sync
        def _(sp):
            sp.dma_start(flat(IG), d["gates_d"][0:MH, :]).then_inc(loaded, 16)
            sp.dma_start(flat(FG), d["gates_d"][MH:2 * MH, :]).then_inc(loaded, 16)
            sp.dma_start(gb[:], d["b_gates"]).then_inc(loaded, 16)
            sp.dma_start(m0[:], d["m_init"]).then_inc(loaded, 16)
            sp.wait_ge(u_ready, 2)
            sp.dma_start(d["ug_d"][0], flat(G)).then_inc(stored, 16)
            sp.dma_start(d["ug_d"][1], flat(U)).then_inc(stored, 16)
            sp.dma_start(d["m_out"][0], M[:, NPT - 1, P - 1:P]).then_inc(stored, 16)
            sp.dma_start(d["m_out"][1], M[:, NT - 1, P - 1:P]).then_inc(stored, 16)
            sp.wait_ge(stored, 64)

        @block.gpsimd
        def _(pool):
            nc.gpsimd.memset(cm[:], 1.0).then_inc(mask_ready, 1)
            pool.wait_ge(mask_ready, 1)
            nc.gpsimd.memset(cm[:, :, 0:1], 0.0).then_inc(mask_ready, 1)
            nc.gpsimd.memset(W[:], 0.0).then_inc(zeroed, 1)

        @block.scalar
        def _(act):
            act.preload_act_table_set("natural_log_exp_and_others")
            act.wait_ge(abs_ready, 1)
            nc.scalar.activation(AB[:], AB[:], ACT.Exp, scale=-1.0).then_inc(e_ready, 1)
            act.wait_ge(e_ready, 1)
            nc.scalar.activation(AB[:], AB[:], ACT.Ln, bias=1.0).then_inc(l_ready, 1)
            act.wait_ge(zeroed, 1)
            act.wait_ge(m_ready, 2)
            nc.scalar.activation(W[64:64 + MH], M[:], ACT.Exp, scale=-1.0).then_inc(w_ready, 1)
            act.wait_ge(args_ready, 1)
            nc.scalar.activation(W[0:MH], IG[:], ACT.Exp).then_inc(w_ready, 1)
            act.wait_ge(args_ready, 2)
            nc.scalar.activation(W[32:32 + MH], FG[:], ACT.Exp).then_inc(w_ready, 1)

        @block.vector
        def _(dve):
            v = nc.vector
            dve.wait_ge(loaded, 64)
            v.tensor_scalar(IG[:], IG[:], gb[:, 0:1], None, ALU.add).then_inc(biased, 1)
            v.tensor_scalar(FG[:], FG[:], gb[:, 1:2], None, ALU.add).then_inc(biased, 1)
            dve.wait_ge(biased, 2)
            v.scalar_tensor_tensor(out=AB[:], in0=FG[:], scalar=-1.0, in1=FG[:], op0=ALU.mult,
                                   op1=ALU.max).then_inc(abs_ready, 1)
            dve.wait_ge(l_ready, 1)
            v.scalar_tensor_tensor(out=LF[:], in0=FG[:], scalar=0.0, in1=AB[:], op0=ALU.min,
                                   op1=ALU.subtract).then_inc(lf_ready, 1)
            dve.wait_ge(lf_ready, 1)
            v.memset(LF[:, NT - 1, DEC:], 0.0).then_inc(padded, 1)
            v.memset(IG[:, NT - 1, DEC:], FAR).then_inc(padded, 1)
            dve.wait_ge(padded, 2)
            dve.wait_ge(mask_ready, 2)
            v.tensor_tensor_scan(flat(B), flat(cm), flat(LF), 0.0, ALU.mult, ALU.add).then_inc(b_ready, 1)
            v.tensor_tensor_scan(flat(M)[:, 0:SEQ], flat(LF)[:, 0:SEQ], flat(IG)[:, 0:SEQ], 0.0, ALU.add,
                                 ALU.max).then_inc(m_ready, 1)
            v.tensor_tensor_scan(flat(M)[:, SEQ:], flat(LF)[:, SEQ:], flat(IG)[:, SEQ:], m0[:], ALU.add,
                                 ALU.max).then_inc(m_ready, 1)
            v.memset(mp[:, 0:1], 0.0).then_inc(mp_ready, 1)
            v.tensor_copy(mp[:, NT - 1:NT], m0[:]).then_inc(mp_ready, 1)
            dve.wait_ge(m_ready, 2)
            v.tensor_copy(mp[:, 1:NPT], M[:, 0:NPT - 1, P - 1]).then_inc(mp_ready, 1)
            dve.wait_ge(b_ready, 1)
            v.tensor_tensor(dl[:], B[:, :, P - 1], M[:, :, P - 1], ALU.subtract).then_inc(mp_ready, 1)
            v.tensor_tensor(U[:], B[:], M[:], ALU.subtract).then_inc(u_ready, 1)
            v.tensor_tensor(G[:], IG[:], B[:], ALU.subtract).then_inc(u_ready, 1)
            dve.wait_ge(u_ready, 2)
            dve.wait_ge(mp_ready, 4)
            v.tensor_tensor(IG[:], U[:], bc(mp[:]), ALU.add).then_inc(args_ready, 1)
            v.tensor_tensor(FG[:], G[:], bc(dl[:]), ALU.add).then_inc(args_ready, 1)
            dve.wait_ge(w_ready, 3)
            v.scalar_tensor_tensor(out=dd[:], in0=W[0:MH, :, P - 1].unsqueeze(2).to_broadcast([MH, NT, MH]), scalar=-1.0,
                                   in1=c["ident"][0:MH, 0:MH].unsqueeze(1).to_broadcast([MH, NT, MH]), op0=ALU.mult,
                                   op1=ALU.mult).then_inc(dec_args, 1)
            dve.wait_ge(turned, 1)
            for n in range(0, NT, 5):
                m = min(5, NT - n)
                src = pw[:, n // 5, 0:m * 96].rearrange("p (n q x) -> p n q x", q=3, x=32)[:, :, :, 0:MH]
                v.tensor_copy(gc[:, n:n + m], src).then_inc(taken, 1)
            dve.wait_ge(dec_sum, 1)
            v.tensor_copy(dec[:], pd[:, 0:NT * MH].rearrange("p (n h) -> p n h", h=MH)).then_inc(taken, 1)

        @block.tensor
        def _(pe):
            pe.wait_ge(w_ready, 3)
            for n in range(NT):
                mm = nc.tensor.transpose(pw[:, n // 5, (n % 5) * 96:(n % 5 + 1) * 96], W[:, n], c["ident"][0:96, 0:96])
            mm.then_inc(turned, 1)
            pe.wait_ge(dec_args, 1)
            nc.tensor.matmul(pd[:, 0:NT * MH], c["nones"][0:MH, :], dd[:].rearrange("h n g -> h (n g)"),
                             start=True, stop=True).then_inc(dec_sum, 1)


def mlstm(k, c, gc, dec):
    nc, d = k.nc, k.d
    MA = MD + 1
    qkv_in = [k.sem("qkv_loaded0"), k.sem("qkv_loaded1")]
    ug_in = [k.sem("ug_loaded0"), k.sem("ug_loaded1")]
    stored = [k.sem("h_stored0"), k.sem("h_stored1")]
    (ones_ready, state_in, k_scaled, q_weighted, v_ready, vw_ready, turned, q_taken, k_taken, qw_taken, d_ready, s_ready,
     dm_ready, w_ready, sw_ready, num_ready, u_ready, decayed, c_ready, dn_ready, ab_ready, fl_ready, rd_ready, h_ready,
     c_stored) = k.sems(
        "ones_ready", "state_loaded", "k_scaled", "q_weighted", "v_ready", "v_weighted", "qk_turned", "q_taken", "k_taken",
        "qw_taken", "exponent_ready", "scores_ready", "exponent_masked", "weights_ready", "scores_weighted",
        "numerator_ready", "update_ready", "memory_decayed", "memory_ready", "den_ready", "den_abs", "den_floored",
        "den_inverse", "h_ready", "memory_stored")
    w_in = [k.sem("w_ada_loaded0"), k.sem("w_ada_loaded1")]
    mod_psum, mod_ready, mod_turned, mod_row, mod_stored, plus_one, scale_ready = k.sems(
        "mod_summed", "mod_ready", "mod_turned", "mod_row_ready", "mod_stored", "scale_plus_one", "scale_ready")
    NM = 6 * KD - NMOD
    with ExitStack() as s:
        wa = sbuf(nc, s, "mwa", [P, 2, KD, 2 * P])
        mod_rows = sbuf(nc, s, "mmod_rows", [2 * NM, P])
        pm = psum(nc, s, "mpm", [P, W5])
        x = sbuf(nc, s, "mx", [P, 2, 3, MH, MD])
        LG = sbuf(nc, s, "mLG", [2, 2, MH, P])
        RU = sbuf(nc, s, "mRU", [2, 2, MH, P])
        ks = sbuf(nc, s, "mks", [P, 2, MH, MD])
        qw = sbuf(nc, s, "mqw", [P, 2, MH, MD])
        VI = sbuf(nc, s, "mVI", [P, 2, MH, MA])
        VU = sbuf(nc, s, "mVU", [P, 2, MH, MA])
        T = sbuf(nc, s, "mT", [P, 2, 3, MH, P])
        DM = sbuf(nc, s, "mDM", [P, MH, P])
        WX = sbuf(nc, s, "mWX", [P, MH, P])
        SW = sbuf(nc, s, "mSW", [P, 2, MH, P])
        C = [sbuf(nc, s, "mC0", [P, MH, MA]), sbuf(nc, s, "mC1", [P, MH, MA])]
        dn = sbuf(nc, s, "mdn", [P, 4, MH])
        H = sbuf(nc, s, "mH", [P, 2, MH, MD])
        pT = psum(nc, s, "mpT", [P, 3, W5])
        pD = psum(nc, s, "mpD", [P, W5])
        pS = psum(nc, s, "mpS", [P, W5])
        pN = psum(nc, s, "mpN", [P, 2, W5])
        block = s.enter_context(nc.Block())
        pairs = lambda ap: ap[:, :, 0:2 * MA].rearrange("p b (h e) -> p b h e", e=MA)
        heads = lambda ap: ap.rearrange("p (b h) e -> p b h e", b=2)
        per_head = lambda col, n: col.unsqueeze(2).to_broadcast([P, MH, n])

        def chunks(eng, before, slot, after):
            before((0, 0, 0))
            for t in range(2):
                slot((t, t, 0), (t + 1, 1 - t, t))
            with eng.Fori(1, NPT // 2 - 1) as i:
                slot((2 * i, 0, i), (2 * i + 1, 1, i))
                slot((2 * i + 1, 1, i), (2 * i + 2, 0, i + 1))
            for t in range(NPT - 2, NPT):
                slot((t, t % 2, t // 2), (t + 1, (t + 1) % 2, (t + 1) // 2))
            after((NPT, 0, NPT // 2))

        @block.sync
        def _(sp):
            sp.dma_start(C[1][:], d["c_init"]).then_inc(state_in, 16)

            def body(t, u, r, first):
                if not first:
                    sp.wait_ge(turned, t - 1)
                    sp.wait_ge(vw_ready, t - 1)
                    sp.wait_ge(d_ready, t - 1)
                for n in range(3):
                    sp.dma_start(x[:, u, n].rearrange("p h e -> p (h e)"), d["proj_out"][n, tok(t), :]).then_inc(qkv_in[u], 16)
                sp.wait_ge(ones_ready, 2)
                sp.dma_start(LG[0:1, u], d["ug_d"][0:1, :, tok(t)]).then_inc(ug_in[u], 16)
                sp.dma_start(RU[1:2, u], d["ug_d"][1:2, :, tok(t)]).then_inc(ug_in[u], 16)
                if not (isinstance(t, int) and t == NPT):
                    if not first:
                        sp.wait_ge(mod_psum, t - 1)
                    sp.dma_start(wa[:, u], d["w_ada"].rearrange("(k p) n -> p k n", p=P)
                                 [:, :, bass.ds(t * 2 * P + NMOD * P, 2 * P)]).then_inc(w_in[u], 16)
            tiles(sp, body)
            sp.wait_ge(mod_row, 1)
            sp.dma_start(d["mods"], mod_rows[:]).then_inc(mod_stored, 16)
            sp.wait_ge(mod_stored, 16)
            sp.wait_ge(c_ready, NPT)
            sp.dma_start(d["c_out"][0], C[0][:]).then_inc(c_stored, 16)
            sp.wait_ge(c_ready, NT)
            sp.dma_start(d["c_out"][1], C[1][:]).then_inc(c_stored, 16)
            sp.wait_ge(c_stored, 32)
            for u in range(2):
                sp.wait_ge(stored[u], 16 * len(range(u, NT, 2)))

        @block.gpsimd
        def _(pool):
            nc.gpsimd.memset(LG[:], 1.0).then_inc(ones_ready, 1)
            nc.gpsimd.memset(RU[:], 1.0).then_inc(ones_ready, 1)
            nc.gpsimd.memset(VI[:], 1.0).then_inc(ones_ready, 1)
            nc.gpsimd.memset(C[0][:], 0.0).then_inc(ones_ready, 1)

            def body(t, u, r, first):
                pool.wait_ge(h_ready, t + 1)
                pool.dma_start(d["h_d"][tok(t), :], H[:, u].rearrange("p h e -> p (h e)")).then_inc(stored[u], 16)
            tiles(pool, body)

        @block.scalar
        def _(act):
            act.preload_act_table_set("natural_log_exp_and_others")
            act.wait_ge(ones_ready, 4)

            def body(t, u, r, first):
                act.wait_ge(qkv_in[u], 48 * r + 48)
                if not first:
                    act.wait_ge(turned, t - 1)
                    act.wait_ge(u_ready, t - 1)
                nc.scalar.activation(ks[:, u], x[:, u, 1], ACT.Copy, scale=MD ** -0.5).then_inc(k_scaled, 1)
                nc.scalar.activation(VI[:, u, :, 0:MD], x[:, u, 2], ACT.Copy).then_inc(v_ready, 1)
                act.wait_ge(turned, t + 1)
                nc.scalar.activation(T[:, u, 0], pT[:, 0].rearrange("p (h e) -> p h e", e=P), ACT.Copy).then_inc(q_taken, 1)
                act.wait_ge(dm_ready, t + 1)
                at_least(act, sw_ready, t)
                nc.scalar.activation(WX[:], DM[:], ACT.Exp).then_inc(w_ready, 1)
            tiles(act, body)

        @block.vector
        def _(dve):
            v = nc.vector

            gates = lambda t: gc[:, bass.ds(t, 1)].rearrange("p o q h -> p (o q) h")

            def prepare(chunk):
                t, u, r = chunk
                g = gates(t)
                dve.wait_ge(qkv_in[u], 48 * r + 48)
                at_least(dve, turned, t - 1)
                v.tensor_tensor(qw[:, u], x[:, u, 0], per_head(g[:, 0], MD), ALU.mult).then_inc(q_weighted, 1)
                dve.wait_ge(v_ready, t + 1)
                v.tensor_tensor(VU[:, u], VI[:, u], per_head(g[:, 1], MA), ALU.mult).then_inc(vw_ready, 1)
                dve.wait_ge(d_ready, t + 1)
                v.tensor_tensor(DM[:], pD[:].rearrange("p (h e) -> p h e", e=P),
                                c["farc"][:].unsqueeze(1).to_broadcast([P, MH, P]), ALU.add).then_inc(dm_ready, 1)
                dve.wait_ge(turned, t + 1)
                v.tensor_copy(T[:, u, 2], pT[:, 2].rearrange("p (h e) -> p h e", e=P)).then_inc(k_taken, 1)
                v.tensor_copy(T[:, u, 1], pT[:, 1].rearrange("p (h e) -> p h e", e=P)).then_inc(qw_taken, 1)

            def weigh(chunk):
                t, u, r = chunk
                dve.wait_ge(s_ready, t + 1)
                dve.wait_ge(w_ready, t + 1)
                v.tensor_tensor(SW[:, u], pS[:].rearrange("p (h e) -> p h e", e=P), WX[:], ALU.mult).then_inc(sw_ready, 1)

            def memory(t):
                return C[1] if isinstance(t, int) and t == NPT else C[0]

            def decay(chunk):
                t, u, r = chunk
                state = memory(t)
                dve.wait_ge(num_ready, t + 1)
                if isinstance(t, int) and t == NPT:
                    dve.wait_ge(state_in, 16)
                v.tensor_tensor(state[:], state[:], dec[:, bass.ds(t, 1)].rearrange("p o h -> p (o h)").unsqueeze(2)
                                .to_broadcast([P, MH, MA]), ALU.mult).then_inc(decayed, 1)

            def finish(chunk):
                t, u, r = chunk
                g, state = gates(t), memory(t)
                dve.wait_ge(u_ready, t + 1)
                dve.wait_ge(decayed, t + 1)
                v.tensor_tensor(heads(state[:]), heads(state[:]), pairs(pT[:, 1:3]), ALU.add).then_inc(c_ready, 1)
                num = pairs(pN[:])
                v.tensor_copy(dn[:, 0].rearrange("p (b h) -> p b h", b=2), num[:, :, :, MD]).then_inc(dn_ready, 1)
                dve.wait_ge(dn_ready, t + 1)
                v.scalar_tensor_tensor(out=dn[:, 1], in0=dn[:, 0], scalar=-1.0, in1=dn[:, 0], op0=ALU.mult,
                                       op1=ALU.max).then_inc(ab_ready, 1)
                dve.wait_ge(ab_ready, t + 1)
                v.tensor_tensor(dn[:, 2], dn[:, 1], g[:, 2], ALU.max).then_inc(fl_ready, 1)
                dve.wait_ge(fl_ready, t + 1)
                v.reciprocal(dn[:, 3], dn[:, 2]).then_inc(rd_ready, 1)
                dve.wait_ge(rd_ready, t + 1)
                at_least(dve, stored[u], 16 * r)
                v.tensor_tensor(heads(H[:, u]), num[:, :, :, 0:MD],
                                dn[:, 3].rearrange("p (b h) -> p b h", b=2).unsqueeze(3).to_broadcast([P, 2, 2, MD]),
                                ALU.mult).then_inc(h_ready, 1)

            def slot(chunk, nxt):
                prepare(nxt)
                decay(chunk)
                weigh(nxt)
                finish(chunk)
            chunks(dve, lambda i: (prepare(i), weigh(i)), slot, lambda i: (decay(i), finish(i)))
            dve.wait_ge(mod_psum, NPT)
            v.tensor_tensor(c["mod"][:, NMOD:], pm[:, 0:2 * NM].rearrange("p (j c) -> p j c", c=2),
                            c["b_ada"][:, NMOD:].unsqueeze(2).to_broadcast([P, NM, 2]), ALU.add).then_inc(mod_ready, 1)
            dve.wait_ge(mod_ready, 1)
            v.tensor_scalar(c["A2"][:], c["mod"][:, 4 * KD:5 * KD, :], 1.0, None, ALU.add).then_inc(plus_one, 1)
            dve.wait_ge(plus_one, 1)
            v.tensor_tensor(c["A2"][:], c["A2"][:], c["norm2"][:].unsqueeze(2).to_broadcast([P, KD, 2]),
                            ALU.mult).then_inc(scale_ready, 1)
            dve.wait_ge(mod_turned, 1)
            v.tensor_copy(mod_rows[:], pm[0:2 * NM, P:2 * P]).then_inc(mod_row, 1)

        @block.tensor
        def _(pe):
            t_ = nc.tensor

            def turn(chunk):
                t, u, r = chunk
                pe.wait_ge(ug_in[u], 32 * r + 32)
                at_least(pe, dm_ready, t)
                for h in range(MH):
                    mm = t_.matmul(pD[:, h * P:(h + 1) * P], LG[:, u, h], RU[:, u, h], start=(h == 0), stop=True,
                                   skip_group_check=True)
                mm.then_inc(d_ready, 1)
                pe.wait_ge(k_scaled, t + 1)
                pe.wait_ge(q_weighted, t + 1)
                at_least(pe, c_ready, t - 1)
                at_least(pe, q_taken, t)
                for n, src in enumerate((x[:, u, 0], qw[:, u], ks[:, u])):
                    for h in range(MH):
                        mm = t_.transpose(pT[:, n, h * P:(h + 1) * P], src[:, h], c["ident"][:])
                mm.then_inc(turned, 1)

            def modulate(chunk):
                t, u, r = chunk
                pe.wait_ge(w_in[u], 16 * r + 16)
                for j in range(2):
                    for kk in range(KD):
                        mm = t_.matmul(pm[:, bass.ds(t * 4 + 2 * j, 2)], wa[:, u, kk, j * P:(j + 1) * P],
                                       c["silu_c"][:, kk, :], start=(kk == 0), stop=(kk == KD - 1))
                mm.then_inc(mod_psum, 1)

            def scores(chunk):
                t, u, r = chunk
                pe.wait_ge(q_taken, t + 1)
                pe.wait_ge(k_taken, t + 1)
                at_least(pe, sw_ready, t)
                for h in range(MH):
                    mm = t_.matmul(pS[:, h * P:(h + 1) * P], T[:, u, 2, h], T[:, u, 0, h], start=(h == 0), stop=True,
                                   skip_group_check=True)
                mm.then_inc(s_ready, 1)

            def numerator(chunk):
                t, u, r = chunk
                last = isinstance(t, int) and t == NPT
                state = C[1] if last else C[0]
                pe.wait_ge(qw_taken, t + 1)
                at_least(pe, h_ready, t)
                if last:
                    pe.wait_ge(state_in, 16)
                elif isinstance(t, int) and t == 0:
                    pe.wait_ge(ones_ready, 4)
                at_least(pe, c_ready, t)
                for h in range(MH):
                    t_.matmul(pN[:, h // 2, (h % 2) * MA:(h % 2 + 1) * MA], T[:, u, 1, h], state[:, h],
                              start=(h % 2 == 0), stop=False, skip_group_check=True)
                pe.wait_ge(sw_ready, t + 1)
                for h in range(MH):
                    mm = t_.matmul(pN[:, h // 2, (h % 2) * MA:(h % 2 + 1) * MA], SW[:, u, h], VI[:, u, h],
                                   start=False, stop=True, skip_group_check=True)
                mm.then_inc(num_ready, 1)

            def update(chunk):
                t, u, r = chunk
                pe.wait_ge(vw_ready, t + 1)
                if not (isinstance(t, int) and t == NPT):
                    pe.wait_ge(qw_taken, t + 2)
                    pe.wait_ge(k_taken, t + 2)
                for h in range(MH):
                    mm = t_.matmul(pT[:, 1 + h // 2, (h % 2) * MA:(h % 2 + 1) * MA], ks[:, u, h], VU[:, u, h],
                                   start=(h % 2 == 0), stop=True, skip_group_check=True)
                mm.then_inc(u_ready, 1)

            def slot(chunk, nxt):
                turn(nxt)
                numerator(chunk)
                scores(nxt)
                update(chunk)
                modulate(chunk)
            chunks(pe, lambda i: (turn(i), scores(i)), slot, lambda i: (numerator(i), update(i)))
            pe.wait_ge(mod_ready, 1)
            t_.transpose(pm[0:2 * NM, P:2 * P], c["mod"][:, NMOD:].rearrange("p j c -> p (j c)"),
                         c["ident"][:]).then_inc(mod_turned, 1)


def output_projection(k, c):
    nc, d = k.nc, k.d
    x_in = [k.sem("tile_loaded0"), k.sem("tile_loaded1")]
    res_in = [k.sem("residual_loaded0"), k.sem("residual_loaded1")]
    stored = [k.sem("x1_stored0"), k.sem("x1_stored1")]
    NR = 4
    raw_in = [k.sem(f"w_raw_loaded{n}") for n in range(NR)]
    (w_high, w_low, rows_in, squared, summed_p, summed_o, std_ready, rstd_ready, sig_ready, normed, weighted, y_ready, turned,
     y_high, y_low, mix_ready, gated, x1_ready) = k.sems(
        "w_high", "w_low", "rows_loaded", "squared", "squares_summed", "o_squares_summed", "std_ready", "rstd_ready",
        "sigmoid_ready", "normed", "weighted", "y_ready", "y_turned", "y_high", "y_low", "mix_ready", "gated", "x1_ready")
    with ExitStack() as s:
        raw = sbuf(nc, s, "eraw", [P, NR, D])
        wH = sbuf(nc, s, "ewH", [P, KD, D], F32R)
        wL = sbuf(nc, s, "ewL", [P, KD, D], F32R)
        gate = sbuf(nc, s, "egate", [P, 2, D])
        wrow = sbuf(nc, s, "ewrow", [P, D])
        x = sbuf(nc, s, "ex", [P, 2, D])
        y = sbuf(nc, s, "ey", [P, 2, D])
        o = sbuf(nc, s, "eo", [P, 2, W5])
        st = sbuf(nc, s, "est", [P, 2, 4, 8])
        yH = sbuf(nc, s, "eyH", [P, 2, KD, P], F32R)
        yL = sbuf(nc, s, "eyL", [P, 2, KD, P], F32R)
        mix = sbuf(nc, s, "emix", [P, 2, D])
        sq = sbuf(nc, s, "esq", [P, D])
        pT = psum(nc, s, "epT", [P, 2, D])
        acc = psum(nc, s, "eacc", [P, 2, D])
        block = s.enter_context(nc.Block())

        @block.sync
        def _(sp):
            for n in range(2):
                src = d["mods"].rearrange("(j w) p -> w j p", w=2)[n:n + 1, 2 * KD - NMOD:3 * KD - NMOD, :]
                sp.dma_start(gate[:, n].rearrange("p (j e) -> p j e", e=P),
                             src.to_broadcast([P, KD, P])).then_inc(rows_in, 16)
            sp.dma_start(wrow[:], d["y_norms"]).then_inc(rows_in, 16)

            def body(t, u, r, first):
                if not first:
                    sp.wait_ge(turned, t - 1)
                sp.dma_start(y[:, u, 0:W5], d["h_d"][tok(t), :]).then_inc(x_in[u], 16)
                sp.dma_start(y[:, u, W5:], d["o_d"][tok(t), :]).then_inc(x_in[u], 16)
                sp.dma_start(o[:, u], d["proj_out"][3, tok(t), :]).then_inc(x_in[u], 16)
                if not first:
                    sp.wait_ge(x1_ready, t - 1)
                sp.dma_start(x[:, u], d["x_all"][tok(t), :]).then_inc(res_in[u], 16)
            tiles(sp, body)

        @block.gpsimd
        def _(pool):
            for kk in range(KD):
                pool.wait_ge(w_high, kk + 1)
                nc.gpsimd.tensor_tensor(wL[:, kk], raw[:, kk % NR], wH[:, kk].bitcast(F32), ALU.subtract).then_inc(w_low, 1)

            def body(t, u, r, first):
                pool.wait_ge(x1_ready, t + 1)
                pool.dma_start(d["x1_d"][tok(t), :], mix[:, u]).then_inc(stored[u], 16)
            tiles(pool, body)
            for u in range(2):
                pool.wait_ge(stored[u], 16 * len(range(u, NT, 2)))

        @block.scalar
        def _(act):
            def load(kk):
                if kk >= NR:
                    act.wait_ge(w_low, kk - NR + 1)
                act.dma_start(raw[:, kk % NR], d["w_out"][kk * P:(kk + 1) * P, :]).then_inc(raw_in[kk % NR], 16)
            for kk in range(NR):
                load(kk)
            for kk in range(KD):
                if 0 < kk and kk + NR - 1 < KD:
                    load(kk + NR - 1)
                act.wait_ge(raw_in[kk % NR], 16 * (kk // NR) + 16)
                nc.scalar.activation(wH[:, kk], raw[:, kk % NR], ACT.Copy).then_inc(w_high, 1)

            def body(t, u, r, first):
                act.wait_ge(x_in[u], 48 * r + 48)
                nc.scalar.activation(o[:, u], o[:, u], ACT.Sigmoid).then_inc(sig_ready, 1)
                act.wait_ge(summed_p, t + 1)
                act.wait_ge(summed_o, t + 1)
                if not first:
                    act.wait_ge(rstd_ready, t - 1)
                nc.scalar.activation(st[:, u, 2, 0:4], st[:, u, 0, 0:4], ACT.Sqrt, bias=c["eps"][:], scale=1.0 / MD)\
                    .then_inc(std_ready, 1)
                nc.scalar.activation(st[:, u, 2, 4:5], st[:, u, 1, 0:1], ACT.Sqrt, bias=c["eps"][:], scale=1.0 / W5)\
                    .then_inc(std_ready, 1)
                act.wait_ge(turned, t + 1)
                if not first:
                    act.wait_ge(mix_ready, t - 1)
                nc.scalar.activation(yH[:, u], pT[:, u].rearrange("p (j e) -> p j e", e=P), ACT.Copy).then_inc(y_high, 1)
            tiles(act, body)

        @block.vector
        def _(dve):
            v = nc.vector
            dve.wait_ge(rows_in, 48)

            def norm(t, u, r, first):
                dve.wait_ge(x_in[u], 48 * r + 48)
                v.tensor_tensor(sq[:], y[:, u], y[:, u], ALU.mult).then_inc(squared, 1)
                dve.wait_ge(squared, t + 1)
                v.tensor_reduce(st[:, u, 0], sq[:].rearrange("p (j e) -> p j e", e=P), AX.X, ALU.add).then_inc(summed_p, 1)
                dve.wait_ge(summed_p, t + 1)
                v.tensor_reduce(st[:, u, 1, 0:1], st[:, u, 0, 4:8], AX.X, ALU.add).then_inc(summed_o, 1)
                dve.wait_ge(std_ready, 2 * t + 2)
                v.reciprocal(st[:, u, 3, 0:5], st[:, u, 2, 0:5]).then_inc(rstd_ready, 1)
                dve.wait_ge(rstd_ready, t + 1)
                ya = y[:, u, 0:W5].rearrange("p (h e) -> p h e", e=MD)
                v.tensor_tensor(ya, ya, st[:, u, 3, 0:4].unsqueeze(2).to_broadcast([P, MH, MD]), ALU.mult).then_inc(normed, 1)
                dve.wait_ge(normed, t + 1)
                dve.wait_ge(sig_ready, t + 1)
                v.tensor_tensor(y[:, u, 0:W5], y[:, u, 0:W5], wrow[:, 0:W5], ALU.mult).then_inc(weighted, 1)
                v.scalar_tensor_tensor(out=y[:, u, W5:], in0=y[:, u, W5:], scalar=st[:, u, 3, 4:5], in1=wrow[:, W5:],
                                       op0=ALU.mult, op1=ALU.mult).then_inc(y_ready, 1)
                dve.wait_ge(weighted, t + 1)
                v.tensor_tensor(y[:, u, 0:W5], y[:, u, 0:W5], o[:, u], ALU.mult).then_inc(y_ready, 1)

            def low(t, u, r, first):
                dve.wait_ge(y_high, t + 1)
                if not first:
                    dve.wait_ge(mix_ready, t - 1)
                v.tensor_tensor(yL[:, u], pT[:, u].rearrange("p (j e) -> p j e", e=P), yH[:, u].bitcast(F32),
                                ALU.subtract).then_inc(y_low, 1)

            def finish(t, u, r, first):
                which = 1 if isinstance(t, int) and t == NPT else 0
                dve.wait_ge(mix_ready, t + 1)
                at_least(dve, stored[u], 16 * r)
                dve.wait_ge(res_in[u], 16 * r + 16)
                v.tensor_tensor(mix[:, u], acc[:, u], gate[:, which], ALU.mult).then_inc(gated, 1)
                dve.wait_ge(gated, t + 1)
                v.tensor_tensor(mix[:, u], mix[:, u], x[:, u], ALU.add).then_inc(x1_ready, 1)

            norm(0, 0, 0, True)
            low(0, 0, 0, True)
            norm(1, 1, 0, True)
            low(1, 1, 0, True)

            def step(t, u, r, before):
                norm(t, u, r, False)
                finish(t - 2, u, before, False)
                low(t, u, r, False)
            step(2, 0, 1, 0)
            step(3, 1, 1, 0)
            with dve.Fori(2, NPT // 2) as i:
                step(2 * i, 0, i, i - 1)
                step(2 * i + 1, 1, i, i - 1)
            step(NPT, 0, NPT // 2, NPT // 2 - 1)
            finish(NPT - 1, 1, NPT // 2 - 1, False)
            finish(NPT, 0, NPT // 2, False)

        @block.tensor
        def _(pe):
            def turn(t, u, r, first):
                pe.wait_ge(y_ready, 2 * t + 2)
                if not first:
                    pe.wait_ge(y_low, t - 1)
                for kk in range(KD):
                    mm = nc.tensor.transpose(pT[:, u, kk * P:(kk + 1) * P], y[:, u, kk * P:(kk + 1) * P], c["ident"][:])
                mm.then_inc(turned, 1)

            def multiply(t, u, r, first):
                pe.wait_ge(y_low, t + 1)
                if not first:
                    pe.wait_ge(gated, t - 1)
                for half in range(2):
                    cols = slice(half * W5, (half + 1) * W5)
                    for kk in range(KD):
                        for n, (a, w) in enumerate(((yH, wH), (yL, wH), (yH, wL))):
                            mm = nc.tensor.matmul(acc[:, u, cols], a[:, u, kk], w[:, kk, cols],
                                                  start=(kk == 0 and n == 0), stop=(kk == KD - 1 and n == 2))
                mm.then_inc(mix_ready, 1)
            pe.wait_ge(w_low, KD)
            turn(0, 0, 0, True)
            turn(1, 1, 0, True)
            multiply(0, 0, 0, True)
            turn(2, 0, 1, False)
            multiply(1, 1, 0, True)
            with pe.Fori(1, NPT // 2 - 1) as i:
                turn(2 * i + 1, 1, i, False)
                multiply(2 * i, 0, i, False)
                turn(2 * i + 2, 0, i + 1, False)
                multiply(2 * i + 1, 1, i, False)
            turn(NPT - 1, 1, NPT // 2 - 1, False)
            multiply(NPT - 2, 0, NPT // 2 - 1, False)
            turn(NPT, 0, NPT // 2, False)
            multiply(NPT - 1, 1, NPT // 2 - 1, False)
            multiply(NPT, 0, NPT // 2, False)


def ffn_up(k, c, hH, hL):
    nc, d = k.nc, k.d
    NW = SEQ // W5
    NV = NW + 1
    NU = 2 + SEQ + 2 + DEC
    S0 = 2 + SEQ + 2
    parts = ((0, 0, SEQ), (SEQ, S0 - 2, DEC))
    raw_in = [k.sem("w_raw_loaded0"), k.sem("w_raw_loaded1")]
    (w_high, w_low, up_done, up_taken, consts_in, zeroed, first_tap, second_tap, conv_done, silu_ready, act_ready, kept,
     turned, ends_taken, ends_stored, history_set, stored) = k.sems(
        "w_high", "w_low", "up_done", "up_taken", "constants_loaded", "zeroed", "first_tap", "second_tap", "conv_done",
        "silu_ready", "act_ready", "last_rows_kept", "last_rows_turned", "last_rows_taken", "last_rows_stored",
        "history_set", "act_stored")
    with ExitStack() as s:
        raw = sbuf(nc, s, "fraw", [P, 2, KD, P])
        wH = sbuf(nc, s, "fwH", [P, 2, KD, P], F32R)
        wL = sbuf(nc, s, "fwL", [P, 2, KD, P], F32R)
        U = sbuf(nc, s, "fU", [P, 2, NU])
        V = sbuf(nc, s, "fV", [P, 2, SEQ + DEC])
        cw = sbuf(nc, s, "fcw", [P, 2 * NF, 3])
        cb = sbuf(nc, s, "fcb", [P, 2 * NF])
        cs = sbuf(nc, s, "fcs", [P, 2 * NF, 2])
        ends = sbuf(nc, s, "fends", [P, 2, 2, 2 * NF])
        ends_t = sbuf(nc, s, "fends_t", [4 * NF, 2, P])
        acc = psum(nc, s, "facc", [P, 2, NW, W5])
        block = s.enter_context(nc.Block())

        def pairs(eng, body):
            body(0, True)
            with eng.Fori(1, NF) as i:
                body(i, False)

        @block.sync
        def _(sp):
            for t, n in ((cw, "w_conv_T"), (cb, "b_conv_T"), (cs, "conv_state_T")):
                sp.dma_start(t[:], d[n]).then_inc(consts_in, 16)

            def load(i, first):
                for j in range(2):
                    if not first:
                        sp.wait_ge(w_low, 2 * i + j - 1)
                    sp.dma_start(raw[:, j], d["w_up"].rearrange("(q p) n -> p q n", p=P)
                                 [:, :, bass.ds(j * FF + i * P, P)]).then_inc(raw_in[j], 16)

            def store(i):
                sp.wait_ge(act_ready, i + 1)
                sp.dma_start(d["act_d"][0:NPT, :, bass.ds(i, 1), :].rearrange("t p o e -> p t (o e)"),
                             V[:, 0, 0:SEQ].rearrange("p (t e) -> p t e", e=P)).then_inc(stored, 16)
                sp.dma_start(d["act_d"][NPT, :, bass.ds(i, 1), 0:DEC].rearrange("p o e -> p (o e)"),
                             V[:, 0, SEQ:]).then_inc(stored, 16)
            load(0, True)
            with sp.Fori(1, NF) as i:
                load(i, False)
                store(i - 1)
            store(NF - 1)
            sp.wait_ge(ends_taken, 1)
            for t in range(2):
                sp.dma_start(d["conv_out"][t], ends_t[:, t]).then_inc(ends_stored, 16)
            sp.wait_ge(ends_stored, 32)
            sp.wait_ge(stored, 32 * NF)

        @block.scalar
        def _(act):
            def split(i, j, free=False):
                act.wait_ge(raw_in[j], 16 * i + 16)
                if not free:
                    act.wait_ge(up_done, NV * (2 * i + j - 1))
                nc.scalar.activation(wH[:, j], raw[:, j], ACT.Copy).then_inc(w_high, 1)

            def take(i, j, first=False):
                n = 2 * i + j
                if not first:
                    act.wait_ge(conv_done, n - 1)
                    act.wait_ge(kept, n - 1)
                for w in range(NV):
                    act.wait_ge(up_done, NV * n + w + 1)
                    src, dst = ((acc[:, j, w], U[:, j, 2 + w * W5:2 + (w + 1) * W5]) if w < NW else
                                (acc[:, j, 0, 0:DEC], U[:, j, S0:]))
                    nc.scalar.activation(dst, src, ACT.Copy).then_inc(up_taken, 1)

            def silu(i):
                act.wait_ge(conv_done, 2 * i + 1)
                nc.scalar.activation(V[:, 0], V[:, 0], ACT.Silu).then_inc(silu_ready, 1)

            split(0, 0, free=True)
            split(0, 1, free=True)
            take(0, 0, first=True)
            split(1, 0)
            take(0, 1, first=True)
            silu(0)
            split(1, 1)
            with act.Fori(1, NF - 1) as i:
                take(i, 0)
                split(i + 1, 0)
                take(i, 1)
                silu(i)
                split(i + 1, 1)
            take(NF - 1, 0)
            take(NF - 1, 1)
            silu(NF - 1)

        @block.gpsimd
        def _(pool):
            def body(i, first):
                for j in range(2):
                    pool.wait_ge(w_high, 2 * i + j + 1)
                    if not first:
                        pool.wait_ge(up_done, NV * (2 * i + j - 1))
                    nc.gpsimd.tensor_tensor(wL[:, j], raw[:, j], wH[:, j].bitcast(F32), ALU.subtract).then_inc(w_low, 1)
            pairs(pool, body)

        @block.vector
        def _(dve):
            v = nc.vector
            v.memset(U[:, :, 0:2], 0.0).then_inc(zeroed, 1)
            dve.wait_ge(consts_in, 48)

            def conv(i, j, first):
                n = 2 * i + j
                ft = bass.ds(i + j * NF, 1)
                tap = lambda m: cw[:, ft, m:m + 1].rearrange("p o m -> p (o m)")
                if not first:
                    dve.wait_ge(conv_done, n - 1)
                v.tensor_copy(U[:, j:j + 1, S0 - 2:S0], cs[:, ft, :]).then_inc(history_set, 1)
                dve.wait_ge(up_taken, NV * (n + 1))
                dve.wait_ge(history_set, n + 1)
                if not first:
                    dve.wait_ge(act_ready, i)
                    dve.wait_ge(stored, 32 * i)
                for at, u0, width in parts:
                    v.tensor_scalar(V[:, j, at:at + width], U[:, j, u0:u0 + width], tap(0), cb[:, ft],
                                    ALU.mult, ALU.add).then_inc(first_tap, 1)
                for m, (at, u0, width) in enumerate(parts):
                    dve.wait_ge(first_tap, 2 * n + m + 1)
                    v.scalar_tensor_tensor(out=V[:, j, at:at + width], in0=U[:, j, u0 + 1:u0 + 1 + width],
                                           scalar=tap(1), in1=V[:, j, at:at + width], op0=ALU.mult,
                                           op1=ALU.add).then_inc(second_tap, 1)
                for m, (at, u0, width) in enumerate(parts):
                    dve.wait_ge(second_tap, 2 * n + m + 1)
                    op = v.scalar_tensor_tensor(out=V[:, j, at:at + width], in0=U[:, j, u0 + 2:u0 + 2 + width],
                                                scalar=tap(2), in1=V[:, j, at:at + width], op0=ALU.mult, op1=ALU.add)
                op.then_inc(conv_done, 1)
                for m, rows in enumerate((U[:, j, SEQ:SEQ + 2], U[:, j, NU - 2:NU])):
                    op = v.tensor_copy(ends[:, m, :, ft].rearrange("p r o -> p (r o)"), rows)
                op.then_inc(kept, 1)

            def body(i, first):
                if first:
                    dve.wait_ge(zeroed, 1)
                conv(i, 0, first)
                conv(i, 1, first)
                dve.wait_ge(silu_ready, i + 1)
                dve.wait_ge(conv_done, 2 * i + 2)
                v.tensor_tensor(V[:, 0], V[:, 0], V[:, 1], ALU.mult).then_inc(act_ready, 1)
            pairs(dve, body)
            dve.wait_ge(turned, 1)
            v.tensor_copy(ends_t[:], acc[0:4 * NF, 0, 0, 0:2 * P].rearrange("p (m e) -> p m e", e=P)).then_inc(ends_taken, 1)

        @block.tensor
        def _(pe):
            def body(i, first):
                for j in range(2):
                    n = 2 * i + j
                    pe.wait_ge(w_high, n + 1)
                    pe.wait_ge(w_low, n + 1)
                    if not first:
                        pe.wait_ge(up_taken, NV * (n - 1))
                    for w in range(NV):
                        if w < NW:
                            dst, cols = acc[:, j, w], slice(w * W5, (w + 1) * W5)
                        else:
                            pe.wait_ge(up_taken, NV * n + 1)
                            dst, cols = acc[:, j, 0, 0:DEC], slice(SEQ, SEQ + DEC)
                        for kk in range(KD):
                            for m, (a, h) in enumerate(((wH, hH), (wH, hL), (wL, hH))):
                                mm = nc.tensor.matmul(dst, a[:, j, kk], h[:, kk, cols],
                                                      start=(kk == 0 and m == 0), stop=(kk == KD - 1 and m == 2))
                        mm.then_inc(up_done, 1)
            pairs(pe, body)
            pe.wait_ge(kept, 2 * NF)
            pe.wait_ge(up_taken, NV * 2 * NF)
            for m in range(2):
                mm = nc.tensor.transpose(acc[0:4 * NF, 0, 0, m * P:(m + 1) * P],
                                         ends[:, m].rearrange("p r n -> p (r n)"), c["ident"][:])
            mm.then_inc(turned, 1)


def ffn_down(k, c):
    nc, d = k.nc, k.d
    NR = 8
    raw_in = [k.sem(f"w_raw_loaded{n}") for n in range(NR)]
    act_in = [k.sem("act_loaded0"), k.sem("act_loaded1")]
    x_in = [k.sem("x1_loaded0"), k.sem("x1_loaded1")]
    stored = [k.sem("y_stored0"), k.sem("y_stored1")]
    w_low = [k.sem("w_low_even"), k.sem("w_low_odd")]
    gate_in, w_high, w_used, a_high, a_low, down_done, gated, y_ready = k.sems(
        "gate_loaded", "w_high", "w_used", "act_high", "act_low", "down_done", "gated", "y_ready")
    with ExitStack() as s:
        raw = sbuf(nc, s, "draw", [P, NR, W5])
        wH = sbuf(nc, s, "dwH", [P, NF, W5], F32R)
        wL = sbuf(nc, s, "dwL", [P, NF, W5], F32R)
        a = sbuf(nc, s, "da", [P, 2, NF, P])
        aH = sbuf(nc, s, "daH", [P, 2, NF, P], F32R)
        aL = sbuf(nc, s, "daL", [P, 2, NF, P], F32R)
        gate = sbuf(nc, s, "dgate", [P, 2, D])
        x = sbuf(nc, s, "dx", [P, 2, W5])
        y = sbuf(nc, s, "dy", [P, 2, W5])
        acc = psum(nc, s, "dacc", [P, 2, W5])
        block = s.enter_context(nc.Block())

        class Tile:
            def __init__(self, half, t, u, r):
                self.half, self.t, self.n, self.b = half, t, half * NT + t, u ^ half
                self.r = half * (NT // 2) + r + (half & u)
                self.sample = isinstance(t, int) and t == NPT
                self.width = DEC if self.sample else P
                self.cols = slice(half * W5, (half + 1) * W5)
                self.first = isinstance(t, int) and self.n < 2

        def half_tiles(eng, half, body, start=0):
            for t in range(start, 2):
                body(Tile(half, t, t, 0))
            with eng.Fori(1, NPT // 2 - 1) as i:
                body(Tile(half, 2 * i, 0, i))
                body(Tile(half, 2 * i + 1, 1, i))
            for t in range(NPT - 2, NT):
                body(Tile(half, t, t % 2, t // 2))

        def weights_split(eng, half, kk):
            q = half * NF + kk
            eng.wait_ge(w_high, q + 1)
            (nc.gpsimd if kk % 2 == 0 else nc.vector).tensor_tensor(
                wL[:, kk], raw[:, q % NR], wH[:, kk].bitcast(F32), ALU.subtract).then_inc(w_low[kk % 2], 1)

        @block.sync
        def _(sp):
            def weights(half, kk):
                q = half * NF + kk
                if q >= NR:
                    sp.wait_ge(w_low[kk % 2], (q - NR) // 2 + 1)
                sp.dma_start(raw[:, q % NR], d["w_down"][kk * P:(kk + 1) * P, half * W5:(half + 1) * W5])\
                    .then_inc(raw_in[q % NR], 16)

            def load(i):
                if not i.first:
                    sp.wait_ge(a_low, i.n - 1)
                sp.dma_start(a[:, i.b, :, 0:i.width],
                             d["act_d"][bass.ds(i.t, 1), :, :, 0:i.width].rearrange("o p n e -> (o p) n e"))\
                    .then_inc(act_in[i.b], 16)
                if not i.first:
                    sp.wait_ge(y_ready, i.n - 1)
                sp.dma_start(x[:, i.b], d["x1_d"][tok(i.t), i.cols]).then_inc(x_in[i.b], 16)
            for kk in range(2):
                weights(0, kk)
            load(Tile(0, 0, 0, 0))
            for kk in range(2, NF):
                weights(0, kk)
            src = d["mods"].rearrange("(j w) p -> w j p", w=2)
            for n in range(2):
                sp.dma_start(gate[:, n].rearrange("p (j e) -> p j e", e=P),
                             src[n:n + 1, 5 * KD - NMOD:6 * KD - NMOD, :].to_broadcast([P, KD, P])).then_inc(gate_in, 16)
            half_tiles(sp, 0, load, start=1)
            for kk in range(NR):
                weights(1, kk)
            load(Tile(1, 0, 0, 0))
            for kk in range(NR, NF):
                weights(1, kk)
            half_tiles(sp, 1, load, start=1)

        @block.gpsimd
        def _(pool):
            def store(i):
                pool.wait_ge(y_ready, i.n + 1)
                pool.dma_start(d["y_out"][tok(i.t), i.cols], y[:, i.b]).then_inc(stored[i.b], 16)
            for kk in range(0, NF, 2):
                weights_split(pool, 0, kk)
            for t in range(2):
                store(Tile(0, t, t, 0))
            with pool.Fori(1, NPT // 2) as i:
                store(Tile(0, 2 * i, 0, i))
                store(Tile(0, 2 * i + 1, 1, i))
            for kk in range(0, NF, 2):
                weights_split(pool, 1, kk)
            store(Tile(0, NPT, 0, NPT // 2))
            half_tiles(pool, 1, store)
            for u in range(2):
                pool.wait_ge(stored[u], 16 * NT)

        @block.scalar
        def _(act):
            def split(half):
                for kk in range(NF):
                    q = half * NF + kk
                    act.wait_ge(raw_in[q % NR], 16 * (q // NR) + 16)
                    if half and kk < NF - 1:
                        act.wait_ge(w_used, kk + 1)
                    elif half:
                        act.wait_ge(down_done, NT)
                    nc.scalar.activation(wH[:, kk], raw[:, q % NR], ACT.Copy).then_inc(w_high, 1)

            def high(i):
                act.wait_ge(act_in[i.b], 16 * i.r + 16)
                if not i.first:
                    act.wait_ge(down_done, i.n - 1)
                nc.scalar.activation(aH[:, i.b, :, 0:i.width], a[:, i.b, :, 0:i.width], ACT.Copy).then_inc(a_high, 1)
            for half in range(2):
                high(Tile(half, 0, 0, 0))
                split(half)
                half_tiles(act, half, high, start=1)

        @block.vector
        def _(dve):
            v = nc.vector

            def low(i):
                dve.wait_ge(a_high, i.n + 1)
                if not i.first:
                    dve.wait_ge(down_done, i.n - 1)
                v.tensor_tensor(aL[:, i.b, :, 0:i.width], a[:, i.b, :, 0:i.width], aH[:, i.b, :, 0:i.width].bitcast(F32),
                                ALU.subtract).then_inc(a_low, 1)

            def finish(i):
                w, b = i.width, i.b
                dve.wait_ge(down_done, i.n + 1)
                at_least(dve, stored[b], 16 * i.r)
                v.tensor_tensor(y[0:w, b], acc[0:w, b], gate[0:w, int(i.sample), i.cols], ALU.mult).then_inc(gated, 1)
                dve.wait_ge(gated, i.n + 1)
                dve.wait_ge(x_in[b], 16 * i.r + 16)
                v.tensor_tensor(y[0:w, b], y[0:w, b], x[0:w, b], ALU.add).then_inc(y_ready, 1)

            for half in range(2):
                low(Tile(half, 0, 0, 0))
                for kk in range(1, NF, 2):
                    weights_split(dve, half, kk)
                if half:
                    finish(Tile(0, NPT, 0, NPT // 2))
                else:
                    dve.wait_ge(gate_in, 32)
                for t in range(2):
                    low(Tile(half, t + 1, (t + 1) % 2, (t + 1) // 2))
                    finish(Tile(half, t, t, 0))
                with dve.Fori(1, NPT // 2 - 1) as i:
                    low(Tile(half, 2 * i + 1, 1, i))
                    finish(Tile(half, 2 * i, 0, i))
                    low(Tile(half, 2 * i + 2, 0, i + 1))
                    finish(Tile(half, 2 * i + 1, 1, i))
                for t in range(NPT - 2, NPT):
                    low(Tile(half, t + 1, (t + 1) % 2, (t + 1) // 2))
                    finish(Tile(half, t, t % 2, t // 2))
            finish(Tile(1, NPT, 0, NPT // 2))

        @block.tensor
        def _(pe):
            def body(i):
                w, start = i.width, isinstance(i.t, int) and i.t == 0
                pe.wait_ge(a_high, i.n + 1)
                pe.wait_ge(a_low, i.n + 1)
                if not i.first:
                    pe.wait_ge(gated, i.n - 1)
                for kk in range(NF):
                    if start:
                        pe.wait_ge(w_low[kk % 2], i.half * (NF // 2) + kk // 2 + 1)
                    for n, (l, m) in enumerate(((aH, wH), (aL, wH), (aH, wL))):
                        mm = nc.tensor.matmul(acc[0:w, i.b], l[:, i.b, kk, 0:w], m[:, kk], start=(kk == 0 and n == 0),
                                              stop=(kk == NF - 1 and n == 2))
                    if i.sample and i.half == 0:
                        mm.then_inc(w_used if kk < NF - 1 else down_done, 1)
                if not (i.sample and i.half == 0):
                    mm.then_inc(down_done, 1)
            for half in range(2):
                half_tiles(pe, half, body)


def build(nc, dram):
    with ExitStack() as ctx:
        k = Kernel(nc, ctx, dram)
        k.scratch("mods", [2 * (6 * KD - NMOD), P])
        dram["qk_T"] = k.scratch("qk_rows", [2, SH, SD, P + TOK])[:, :, :, P:]
        dram["o_d"] = k.scratch("o_rows", [P + TOK, W5])[P:, :]
        k.scratch("h_d", [TOK, W5])
        k.scratch("ug_d", [2, MH, TOK])
        k.scratch("x1_d", [TOK, D])
        k.scratch("act_d", [NT, P, NF, P])
        k.scratch("gates_d", [8, TOK])
        c = {}
        for name, shape, dt in (("ident", [P, P], F32), ("ident_r", [P, P], F32R), ("tri", [P, P], F32),
                                ("tri_r", [P, P], F32R), ("keep", [P, P], F32), ("far", [P, P], F32),
                                ("far_r", [P, P], F32R), ("farc", [P, P], F32), ("nones", [P, P], F32),
                                ("fold", [P, SD], F32), ("eps", [P, 1], F32), ("one", [P, 1], F32), ("mod", [P, 48, 2], F32),
                                ("A1", [P, KD, 2], F32), ("A2", [P, KD, 2], F32), ("silu_c", [P, KD, 2], F32),
                                ("b_ada", [P, 6 * KD], F32), ("norm2", [P, KD], F32)):
            c[name] = sbuf(nc, ctx, name, shape, dt)
        modulation(k, c)
        k.end_phase()
        with ExitStack() as s:
            hH = sbuf(nc, s, "h1H", [P, KD, TOK], F32R)
            hL = sbuf(nc, s, "h1L", [P, KD, TOK], F32R)
            normalise(k, c, dram["x_all"], c["A1"], 0, hH, hL)
            k.end_phase()
            project_gates(k, c, hH, hL)
            k.end_phase()
            project(k, c, hH, hL, dram["w_in7"], 0, 5, dram["proj_out"], False)
            k.end_phase()
            project(k, c, hH, hL, dram["w_in7"], 5, 2, dram["proj_out"], True)
            k.end_phase()
        attention(k, c)
        k.end_phase()
        with ExitStack() as s:
            gc = sbuf(nc, s, "gate_cols", [P, NT, 3, MH])
            dec = sbuf(nc, s, "decay", [P, NT, MH])
            gate_rows(k, c, gc, dec)
            k.end_phase()
            mlstm(k, c, gc, dec)
            k.end_phase()
        attention_sample(k, c)
        k.end_phase()
        output_projection(k, c)
        k.end_phase()
        with ExitStack() as s:
            hH = sbuf(nc, s, "h2H", [P, KD, TOK], F32R)
            hL = sbuf(nc, s, "h2L", [P, KD, TOK], F32R)
            normalise(k, c, dram["x1_d"], c["A2"], 24, hH, hL, "b")
            k.end_phase()
            ffn_up(k, c, hH, hL)
            k.end_phase()
        ffn_down(k, c)
        k.end_phase()


OUTS = {
    "y_out": [TOK, D],
    "conv_out": [2, 4 * NF, P],
    "m_out": [2, MH, 1],
    "c_out": [2, P, MH, MD + 1],
    "proj_out": [7, TOK, W5],
}


def layout(i):
    f = lambda a: np.ascontiguousarray(np.asarray(a))
    x = np.concatenate([np.asarray(i["x_prompt"])[0], np.asarray(i["x_sample"])[0],
                        np.zeros((P - DEC, D), np.float32)])
    cols = lambda a, n: f(np.asarray(a).reshape(n, P).T)
    w_in = np.asarray(i["w_in"])[0]
    c = np.stack([np.asarray(i["c_prompt"])[0], np.asarray(i["c_sample"])[0]])
    g = 4 * W5
    parts = [w_in[:, n * W5:(n + 1) * W5] for n in range(4)]
    sb = w_in[:, g + 2 * MH:]
    parts += [sb[:, 2 * W5:], sb[:, :W5], sb[:, W5:2 * W5]]
    norms = np.stack([np.asarray(i["sb_q_norm_w"])[0], np.asarray(i["sb_k_norm_w"])[0]])
    return {
        "x_all": f(x),
        "c_T": f(c.reshape(2, KD, P).transpose(2, 1, 0)),
        "w_ada": f(np.asarray(i["w_ada"])[0]),
        "b_ada_T": cols(i["b_ada"], 48),
        "norm1_T": cols(i["norm1_w"], KD),
        "norm2_T": cols(i["norm2_w"], KD),
        "w_in7": f(np.stack(parts)),
        "w_gate": f(w_in[:, g:g + 2 * MH]),
        "y_norms": f(np.broadcast_to(np.concatenate([np.asarray(i["ml_norm_w"]).reshape(W5),
                                                     np.asarray(i["sb_out_norm_w"])[0]]), (P, D))),
        "w_out": f(np.asarray(i["w_out"])[0]),
        "w_up": f(np.asarray(i["w_up"])[0]),
        "w_down": f(np.asarray(i["w_down"])[0]),
        "w_conv_T": f(np.asarray(i["w_conv"])[0].reshape(3, 2 * NF, P).transpose(2, 1, 0)),
        "b_conv_T": cols(i["b_conv"], 2 * NF),
        "conv_state_T": f(np.asarray(i["state_ffn_conv"])[0, 0].reshape(2, 2 * NF, P).transpose(2, 1, 0)),
        "b_gates": f(np.stack([np.asarray(i["b_ig"])[0], np.asarray(i["b_fg"])[0]], axis=1)),
        "m_init": f(np.asarray(i["state_mlstm_m"]).reshape(MH, 1)),
        "c_init": f(np.concatenate([np.asarray(i["state_mlstm_c"])[0, 0],
                                    np.asarray(i["state_mlstm_n"])[0, 0][:, :, None]], axis=2).transpose(1, 0, 2)),
        "past_k": f(np.asarray(i["cache_sb_k"]).reshape(PAST, W5)),
        "past_v": f(np.asarray(i["cache_sb_v"]).reshape(PAST, W5)),
        "sb_norms": f(np.broadcast_to(norms, (P, 2, SD))),
    }


def results(r):
    y, pr, cm, m, u = (np.asarray(r[n]) for n in ("y_out", "proj_out", "c_out", "m_out", "conv_out"))
    out = [y[:SEQ].reshape(1, SEQ, D), y[SEQ:SEQ + DEC].reshape(1, DEC, D)]
    for n, rows in enumerate((slice(0, SEQ), slice(SEQ, SEQ + DEC))):
        mem = cm[n].transpose(1, 0, 2)
        out += [mem[None, None, :, :, :MD], mem[None, None, :, :, MD], m[n].reshape(1, 1, MH)]
        out += [pr[g, rows].reshape(1, 1, -1, SH, SD) for g in (6, 4)]
        out += [u[n].reshape(1, 1, 2, 2 * FF)]
    return tuple(np.ascontiguousarray(a) for a in out)


def kernel(**inputs):
    import concourse.bacc as bacc
    from concourse.bass_utils import run_bass_kernel_spmd

    nc = bacc.Bacc("TRN2", target_bir_lowering=False, num_devices=1)
    arrays = layout(inputs)
    dram = {n: nc.dram_tensor(n, a.shape, mybir.dt.from_np(a.dtype), kind="ExternalInput").ap() for n, a in arrays.items()}
    for n, shape in OUTS.items():
        dram[n] = nc.dram_tensor(n, shape, F32, kind="ExternalOutput").ap()
    build(nc, dram)
    r = run_bass_kernel_spmd(nc, [arrays], core_ids=[0])
    return results(r.results[0])
```

```python
from contextlib import ExitStack

import numpy as np
import concourse.bass as bass
from concourse import mybir

F32 = mybir.dt.float32
F32R = mybir.dt.float32r
ACT = mybir.ActivationFunctionType
ALU = mybir.AluOpType
AX = mybir.AxisListType

P = 128
D = 1024
KD = D // P
SEQ, DEC, PAST = 2048, 32, 1024
NPT = SEQ // P
NT = NPT + 1
TOK = NT * P
MH, MD = 4, 128
SH, SD = 8, 64
W5 = 512
FF = 2816
NF = FF // P
EPS = 1e-6
FAR = -1e30
NPB = PAST // P
NMOD = 2 * KD


def tiles(eng, body):
    body(0, 0, 0, True)
    body(1, 1, 0, True)
    with eng.Fori(1, NPT // 2) as i:
        body(2 * i, 0, i, False)
        body(2 * i + 1, 1, i, False)
    body(NPT, 0, NPT // 2, False)


def at_least(eng, sem, value):
    if not (isinstance(value, int) and value <= 0):
        eng.wait_ge(sem, value)


def tok(t):
    return bass.ds(t * P, P)


class Kernel:
    def __init__(self, nc, ctx, dram):
        self.nc, self.ctx, self.d = nc, ctx, dram
        self.nsem, self.own = 0, []

    def sem(self, name):
        self.nsem += 1
        self.own.append(self.nc.alloc_semaphore(f"{name}_{self.nsem}"))
        return self.own[-1]

    def end_phase(self):
        self.nc.clear_and_free_semaphores(self.own)
        self.own = []
        self.nc.all_engine_barrier()

    def sems(self, *names):
        return [self.sem(n) for n in names]

    def scratch(self, name, shape, dt=F32):
        self.d[name] = self.nc.dram_tensor(name, shape, dt, kind="Internal").ap()
        return self.d[name]


def sbuf(nc, ctx, name, shape, dt=F32):
    return ctx.enter_context(nc.sbuf_tensor(name, shape, dt))


def psum(nc, ctx, name, shape):
    return ctx.enter_context(nc.psum_tensor(name, shape, F32))


def modulation(k, c):
    nc, d = k.nc, k.d
    loaded, bias_in, zero, sig_ready, silu_ready, mod_psum, rows_ready, mod_turned, mod_ready, scale1, lead = k.sems(
        "c_loaded", "bias_loaded", "zeroed", "sigmoid_ready", "silu_ready", "mod_summed", "mod_rows_ready", "mod_turned",
        "mod_ready", "scale_ready", "scale_plus_one")
    NCH = NMOD // 4
    w_in = [k.sem(f"w_ada_loaded{n}") for n in range(NCH)]
    with ExitStack() as s:
        wa = sbuf(nc, s, "w_ada_sb", [P, NCH, KD, W5])
        cT = sbuf(nc, s, "cT", [P, KD, 2])
        sg = sbuf(nc, s, "sg", [P, KD, 2])
        sc, n2 = c["silu_c"], c["norm2"]
        rows = sbuf(nc, s, "mod_rows", [2, NCH, W5])
        bias = sbuf(nc, s, "b_ada_rows", [2, NCH * W5])
        n1 = sbuf(nc, s, "n1", [P, KD])
        pm = psum(nc, s, "pm", [2, NCH, W5])
        pt = psum(nc, s, "pt", [P, NMOD, 2])
        block = s.enter_context(nc.Block())

        @block.sync
        def _(sp):
            sp.dma_start(cT[:], d["c_T"]).then_inc(loaded, 16)
            src = d["w_ada"].rearrange("(k p) n -> p k n", p=P)

            for n in range(NCH):
                sp.dma_start(wa[:, n], src[:, :, n * W5:(n + 1) * W5]).then_inc(w_in[n], 16)

        @block.gpsimd
        def _(pool):
            nc.gpsimd.memset(c["ident"][:], 0.0).then_inc(zero, 1)
            nc.gpsimd.memset(c["tri"][:], -1.0).then_inc(zero, 1)
            nc.gpsimd.memset(c["keep"][:], 1.0).then_inc(zero, 1)
            nc.gpsimd.memset(c["far"][:], 0.0).then_inc(zero, 1)
            nc.gpsimd.memset(c["farc"][:], 0.0).then_inc(zero, 1)
            nc.gpsimd.memset(c["nones"][:], -1.0).then_inc(zero, 1)
            nc.gpsimd.memset(c["eps"][:], EPS).then_inc(zero, 1)
            nc.gpsimd.memset(c["fold"][:], 0.0).then_inc(zero, 1)
            nc.gpsimd.memset(c["one"][:], 1.0).then_inc(zero, 1)
            pool.wait_ge(zero, 9)
            sel = nc.gpsimd.affine_select
            sel(out=c["ident"][:], in_=c["ident"][:], compare_op=ALU.not_equal, fill=1.0, base=0,
                pattern=[[-1, P]], channel_multiplier=1).then_inc(zero, 1)
            sel(out=c["tri"][:], in_=c["tri"][:], compare_op=ALU.is_ge, fill=0.0, base=0,
                pattern=[[-1, P]], channel_multiplier=1).then_inc(zero, 1)
            sel(out=c["keep"][:], in_=c["keep"][:], compare_op=ALU.is_gt, fill=0.0, base=0,
                pattern=[[1, P]], channel_multiplier=-1).then_inc(zero, 1)
            sel(out=c["far"][:], in_=c["far"][:], compare_op=ALU.is_gt, fill=FAR, base=0,
                pattern=[[1, P]], channel_multiplier=-1).then_inc(zero, 1)
            sel(out=c["farc"][:], in_=c["farc"][:], compare_op=ALU.is_ge, fill=FAR, base=0,
                pattern=[[1, P]], channel_multiplier=-1).then_inc(zero, 1)
            for n in range(2):
                pool.wait_ge(zero, 14 + n)
                sel(out=c["fold"][:], in_=c["fold"][:], compare_op=ALU.not_equal, fill=1.0, base=-SD * n,
                    pattern=[[-1, SD]], channel_multiplier=1).then_inc(zero, 1)
            pool.wait_ge(zero, 16)
            nc.gpsimd.tensor_copy(c["tri_r"][:], c["tri"][:]).then_inc(zero, 1)
            nc.gpsimd.tensor_copy(c["far_r"][:], c["far"][:]).then_inc(zero, 1)
            nc.gpsimd.tensor_copy(c["ident_r"][:], c["ident"][:]).then_inc(zero, 1)

        @block.scalar
        def _(act):
            act.dma_start(bias[:], d["b_ada"][:, 0:NCH * W5].to_broadcast([2, NCH * W5])).then_inc(bias_in, 16)
            act.dma_start(n1[:], d["norm1_T"]).then_inc(bias_in, 16)
            act.dma_start(n2[:], d["norm2_T"]).then_inc(bias_in, 16)
            act.wait_ge(loaded, 16)
            nc.scalar.activation(sg[:], cT[:], ACT.Sigmoid).then_inc(sig_ready, 1)

        @block.vector
        def _(dve):
            dve.wait_ge(sig_ready, 1)
            nc.vector.tensor_tensor(sc[:], cT[:], sg[:], ALU.mult).then_inc(silu_ready, 1)
            dve.wait_ge(bias_in, 48)
            for n in range(NCH):
                dve.wait_ge(mod_psum, n + 1)
                nc.vector.tensor_tensor(rows[:, n], pm[:, n], bias[:, n * W5:(n + 1) * W5], ALU.add).then_inc(rows_ready, 1)
            dve.wait_ge(mod_turned, 1)
            nc.vector.tensor_copy(c["mod"][:, 0:NMOD], pt[:]).then_inc(mod_ready, 1)
            dve.wait_ge(mod_ready, 1)
            nc.vector.tensor_scalar(c["A1"][:], c["mod"][:, KD:2 * KD, :], 1.0, None, ALU.add).then_inc(lead, 1)
            dve.wait_ge(lead, 1)
            nc.vector.tensor_tensor(c["A1"][:], c["A1"][:], n1[:].unsqueeze(2).to_broadcast([P, KD, 2]),
                                    ALU.mult).then_inc(scale1, 1)

        @block.tensor
        def _(pe):
            pe.wait_ge(silu_ready, 1)
            for n in range(NCH):
                pe.wait_ge(w_in[n], 16)
                for kk in range(KD):
                    mm = nc.tensor.matmul(pm[:, n], sc[:, kk, :], wa[:, n, kk, :], start=(kk == 0), stop=(kk == KD - 1))
                mm.then_inc(mod_psum, 1)
            pe.wait_ge(zero, 16)
            pe.wait_ge(rows_ready, NCH)
            for j in range(NMOD):
                mm = nc.tensor.transpose(pt[:, j], rows[:, j // 4, j % 4 * P:(j % 4 + 1) * P], c["ident"][0:2, 0:2])
            mm.then_inc(mod_turned, 1)


class Turn:
    def __init__(self, t, j, q):
        self.t, self.j, self.q, self.u = t, j, q, j % 2

    def ahead(self, n):
        return Turn(self.t + n, (self.j + n) % 4, self.q + (self.j + n) // 4)

    def within(self, n):
        return not isinstance(self.t, int) or self.t + n < NT


def turns_of_four(eng, body):
    for t in range(4):
        body(Turn(t, t, 0))
    with eng.Fori(1, NPT // 4 - 1) as q:
        for j in range(4):
            body(Turn(4 * q + j, j, q))
    for t in range(NPT - 4, NT):
        body(Turn(t, t % 4, t // 4))


def normalise(k, c, src, scale, shift0, hH, hL, name="a"):
    nc, d = k.nc, k.d
    NX = 4
    x_in = [k.sem(f"x_loaded{n}") for n in range(NX)]
    BY_ACT = 2
    act_part, ssq_ready, std_ready, rstd_ready, x_scaled, x_turned, h_full, h_high, h_low = k.sems(
        "act_part_ready", "squares_summed", "std_ready", "rstd_ready", "x_scaled", "x_turned", "h_full", "h_high", "h_low")
    with ExitStack() as s:
        x = sbuf(nc, s, name + "nx", [P, NX, D])
        sq = sbuf(nc, s, name + "nsq", [P, D])
        tmp = sbuf(nc, s, name + "ntmp", [P, 2, KD, P])
        st = sbuf(nc, s, name + "nst", [P, NX, 3])
        pT = psum(nc, s, name + "npT", [P, 2, D])
        block = s.enter_context(nc.Block())
        eps = c["eps"]

        @block.sync
        def _(sp):
            def load(i):
                at_least(sp, x_turned, i.t - NX + 1)
                sp.dma_start(x[:, i.j], src[tok(i.t), :]).then_inc(x_in[i.j], 16)
            turns_of_four(sp, load)

        @block.scalar
        def _(act):
            def spread(i):
                act.wait_ge(x_in[i.j], 16 * i.q + 16)
                at_least(act, x_scaled, i.t - NX + 1)
                nc.scalar.activation(sq[:], x[:, i.j], ACT.Square, accum_out=st[:, i.j, 0:1]).then_inc(ssq_ready, 1)
                act.wait_ge(ssq_ready, i.t + 1)
                nc.scalar.activation(st[:, i.j, 1:2], st[:, i.j, 0:1], ACT.Sqrt, bias=eps[:],
                                     scale=1.0 / D).then_inc(std_ready, 1)

            def slot(i):
                if i.within(3):
                    spread(i.ahead(3))
                which = 1 if isinstance(i.t, int) and i.t == NPT else 0
                act.wait_ge(h_full, i.t + 1)
                for kk in range(BY_ACT):
                    op = nc.scalar.activation(tmp[:, i.u, kk], pT[:, i.u, kk * P:(kk + 1) * P], ACT.Identity,
                                              bias=c["mod"][:, shift0 + kk, which:which + 1],
                                              scale=scale[:, kk, which:which + 1])
                op.then_inc(act_part, 1)
                act.wait_ge(act_part, i.t + 1)
                nc.scalar.activation(hH[:, :, tok(i.t)], tmp[:, i.u], ACT.Copy).then_inc(h_high, 1)
            for t in range(3):
                spread(Turn(t, t, 0))
            turns_of_four(act, slot)

        @block.vector
        def _(dve):
            def scale_rows(i):
                dve.wait_ge(std_ready, i.t + 1)
                nc.vector.reciprocal(st[:, i.j, 2:3], st[:, i.j, 1:2]).then_inc(rstd_ready, 1)
                dve.wait_ge(rstd_ready, i.t + 1)
                nc.vector.tensor_scalar(x[:, i.j], x[:, i.j], st[:, i.j, 2:3], None, ALU.mult).then_inc(x_scaled, 1)

            def slot(i):
                if i.within(2):
                    scale_rows(i.ahead(2))
                which = 1 if isinstance(i.t, int) and i.t == NPT else 0
                dve.wait_ge(x_turned, i.t + 1)
                at_least(dve, h_high, i.t - 1)
                at_least(dve, h_low, i.t - 1)
                for kk in range(BY_ACT, KD):
                    op = nc.vector.tensor_scalar(tmp[:, i.u, kk], pT[:, i.u, kk * P:(kk + 1) * P],
                                                 scale[:, kk, which:which + 1],
                                                 c["mod"][:, shift0 + kk, which:which + 1], ALU.mult, ALU.add)
                op.then_inc(h_full, 1)
            for t in range(2):
                scale_rows(Turn(t, t, 0))
            turns_of_four(dve, slot)

        @block.gpsimd
        def _(pool):
            def low(i):
                pool.wait_ge(h_high, i.t + 1)
                nc.gpsimd.tensor_tensor(hL[:, :, tok(i.t)], tmp[:, i.u], hH[:, :, tok(i.t)].bitcast(F32),
                                        ALU.subtract).then_inc(h_low, 1)
            turns_of_four(pool, low)

        @block.tensor
        def _(pe):
            def turn(i):
                pe.wait_ge(x_scaled, i.t + 1)
                at_least(pe, act_part, i.t - 1)
                for kk in range(KD):
                    mm = nc.tensor.transpose(pT[:, i.u, kk * P:(kk + 1) * P], x[:, i.j, kk * P:(kk + 1) * P],
                                             c["ident"][:])
                mm.then_inc(x_turned, 1)
            turns_of_four(pe, turn)


def project(k, c, hH, hL, w_dram, group0, n_groups, out_dram, normed):
    nc, d = k.nc, k.d
    NB, NS, NR, NW = 5 if normed else 6, 4, 4, 11 if normed else 12
    raw_in = [k.sem(f"w_raw_loaded{n}") for n in range(NR)]
    w_high, w_low, w_used, summed, taken = k.sems("w_high", "w_low", "w_used", "projected", "psum_taken")
    stored = [k.sem(f"proj_stored{n}") for n in range(NS)]
    if normed:
        squared, reduced, std_ready, rstd_ready, scaled, weighted, norm_in, q_scaled, turned, turn_taken = k.sems(
            "squared", "reduced", "std_ready", "rstd_ready", "scaled", "weighted", "norm_w_loaded", "q_weight_scaled",
            "qk_turned", "turn_taken")
        turn_stored = [k.sem("turn_stored0"), k.sem("turn_stored1")]
    done = weighted if normed else taken
    AHEAD = NW - KD
    with ExitStack() as s:
        raw = sbuf(nc, s, f"praw{group0}", [P, NR, W5])
        wH = sbuf(nc, s, f"pwH{group0}", [P, NW, W5], F32R)
        wL = sbuf(nc, s, f"pwL{group0}", [P, NW, W5], F32R)
        stage = sbuf(nc, s, f"pstage{group0}", [P, NS, W5])
        acc = psum(nc, s, f"pacc{group0}", [P, NB, W5])
        if normed:
            nst = sbuf(nc, s, "pnst", [P, 2, 3, SH])
            nw = sbuf(nc, s, "pnw", [P, 2, SD])
            sq = psum(nc, s, "psq", [P, 2, W5])
            pT = psum(nc, s, "ppT", [P, 4, P])
            xT = sbuf(nc, s, "pxT", [P, 2, 4, P])
        block = s.enter_context(nc.Block())

        def slot(eng, g, kk):
            return bass.ds(eng.snap((g * KD + kk) % NW), 1)

        def stored_before(eng, g, t):
            rank, per = t // NS, len(range(t % NS, NT, NS))
            if not (isinstance(g, int) and g == 0 and rank == 0):
                eng.wait_ge(stored[t % NS], 16 * (g * per + rank))

        @block.sync
        def _(sp):
            def load(g, kk, first=False):
                if not (first and kk < NR):
                    sp.wait_ge(w_low, g * KD + kk - NR + 1)
                sp.dma_start(raw[:, kk % NR],
                             w_dram[bass.ds(group0 + g, 1), kk * P:(kk + 1) * P, :].rearrange("o p n -> (o p) n")
                             ).then_inc(raw_in[kk % NR], 16)

            def group(g, last):
                for t in range(NT):
                    if t % 2 == 0 and t // 2 < KD and not last:
                        load(g + 1, t // 2)
                    sp.wait_ge(done, g * NT + t + 1)
                    dst = out_dram[bass.ds(group0 + g, 1), t * P:(t + 1) * P, :].rearrange("o p n -> (o p) n")
                    sp.dma_start(dst, stage[:, t % NS]).then_inc(stored[t % NS], 16)
            for kk in range(KD):
                load(0, kk, True)
            if n_groups > 1:
                with sp.Fori(0, n_groups - 1) as g:
                    group(g, False)
            group(n_groups - 1, True)
            for n in range(NS):
                sp.wait_ge(stored[n], 16 * n_groups * len(range(n, NT, NS)))

        @block.scalar
        def _(act):
            def split(g, kk, free=False):
                act.wait_ge(raw_in[kk % NR], 16 * (g * (KD // NR) + kk // NR + 1))
                if not free and kk < AHEAD:
                    act.wait_ge(summed, (g - 1) * NT)
                elif not free:
                    act.wait_ge(w_used, (g - 1) * (KD - AHEAD) + kk - AHEAD + 1)
                nc.scalar.activation(wH[:, slot(act, g, kk), :], raw[:, kk % NR].unsqueeze(1),
                                     ACT.Copy).then_inc(w_high, 1)

            def take(g, t, last):
                stored_before(act, g, t)
                if normed:
                    rank = t // NS
                    at_least(act, turned, g * NT + t - NS + 1 if rank else (g - 1) * NT + max(range(t % NS, NT, NS)) + 1)
                act.wait_ge(summed, g * NT + t + 1)
                nc.scalar.activation(stage[:, t % NS], acc[:, t % NB], ACT.Sigmoid if last and not normed else ACT.Copy)\
                    .then_inc(taken, 1)

            def std(g, t):
                act.wait_ge(reduced, g * NT + t + 1)
                nc.scalar.activation(nst[:, t % 2, 1], nst[:, t % 2, 0], ACT.Sqrt, bias=c["eps"][:],
                                     scale=1.0 / SD).then_inc(std_ready, 1)

            def take_turned(n):
                act.wait_ge(turned, n + 1)
                at_least(act, turn_stored[n % 2], 16 * (n // 2))
                nc.scalar.activation(xT[:, n % 2], pT[:], ACT.Copy).then_inc(turn_taken, 1)

            def group(g, last, first=False):
                for t in range(NT):
                    if normed and g * NT + t >= 2:
                        take_turned(g * NT + t - 2)
                    take(g, t, last)
                    if normed:
                        std(g, t)
                    if t % 2 == 1 and t // 2 < AHEAD and not last:
                        split(g + 1, t // 2, free=first)
                if not last:
                    for kk in range(AHEAD, KD):
                        split(g + 1, kk)
            for kk in range(KD):
                split(0, kk, free=True)
            group(0, n_groups == 1, first=True)
            if n_groups > 2:
                with act.Fori(1, n_groups - 1) as g:
                    group(g, False)
            if n_groups > 1:
                group(n_groups - 1, True)
            for n in range(n_groups * NT - 2, n_groups * NT) if normed else ():
                take_turned(n)

        @block.gpsimd
        def _(pool):
            if normed:
                pool.dma_start(nw[:], d["sb_norms"]).then_inc(norm_in, 16)

            def store_turned(n):
                g, t = n // NT, n % NT
                pool.wait_ge(turn_taken, n + 1)
                dst = d["qk_T"][g, :, :, t * P:(t + 1) * P].rearrange("(j a) e t -> (a e) j t", a=2)
                pool.dma_start(dst, xT[:, n % 2]).then_inc(turn_stored[n % 2], 16)

            def split_low(g, kk):
                pool.wait_ge(w_high, g * KD + kk + 1)
                at = slot(pool, g, kk)
                nc.gpsimd.tensor_tensor(wL[:, at, :], raw[:, kk % NR].unsqueeze(1),
                                        wH[:, at, :].bitcast(F32), ALU.subtract).then_inc(w_low, 1)
            if normed:
                for kk in range(KD):
                    split_low(0, kk)
                for g in range(n_groups):
                    for t in range(NT):
                        if t % 2 == 1 and t // 2 < AHEAD and g + 1 < n_groups:
                            split_low(g + 1, t // 2)
                        if g * NT + t >= 2:
                            store_turned(g * NT + t - 2)
                    for kk in range(AHEAD, KD):
                        if g + 1 < n_groups:
                            split_low(g + 1, kk)
                for n in range(n_groups * NT - 2, n_groups * NT):
                    store_turned(n)
                for u in range(2):
                    pool.wait_ge(turn_stored[u], 16 * n_groups * NT // 2)
            else:
                with pool.Fori(0, n_groups) as g:
                    for kk in range(KD):
                        split_low(g, kk)

        if normed:
            @block.vector
            def _(dve):
                dve.wait_ge(norm_in, 16)
                nc.vector.tensor_scalar(nw[:, 0], nw[:, 0], SD ** -0.5, None, ALU.mult).then_inc(q_scaled, 1)
                dve.wait_ge(q_scaled, 1)
                with dve.Fori(0, n_groups) as g:
                    for t in range(NT):
                        n = g * NT + t
                        st = stage[:, t % NS]
                        heads = st.rearrange("p (h e) -> p h e", e=SD)
                        dve.wait_ge(taken, n + 1)
                        nc.vector.tensor_tensor(sq[:, t % 2], st, st, ALU.mult).then_inc(squared, 1)
                        dve.wait_ge(squared, n + 1)
                        nc.vector.tensor_reduce(nst[:, t % 2, 0], sq[:, t % 2].rearrange("p (h e) -> p h e", e=SD),
                                                AX.X, ALU.add).then_inc(reduced, 1)
                        dve.wait_ge(std_ready, n + 1)
                        nc.vector.reciprocal(nst[:, t % 2, 2], nst[:, t % 2, 1]).then_inc(rstd_ready, 1)
                        dve.wait_ge(rstd_ready, n + 1)
                        nc.vector.tensor_tensor(heads, heads, nst[:, t % 2, 2].unsqueeze(2).to_broadcast([P, SH, SD]),
                                                ALU.mult).then_inc(scaled, 1)
                        dve.wait_ge(scaled, n + 1)
                        nc.vector.tensor_tensor(heads, heads, nw[:, bass.ds(g, 1), :].to_broadcast([P, SH, SD]),
                                                ALU.mult).then_inc(weighted, 1)

        @block.tensor
        def _(pe):
            def group(g, first):
                at = [slot(pe, g, kk) for kk in range(KD)]
                for t in range(NT):
                    if t >= NB:
                        pe.wait_ge(taken, g * NT + t - NB + 1)
                    elif t == 0 and not first:
                        pe.wait_ge(taken, g * NT)
                    for kk in range(KD):
                        if t == 0:
                            pe.wait_ge(w_high, g * KD + kk + 1)
                            pe.wait_ge(w_low, g * KD + kk + 1)
                        for n, (a, w) in enumerate(((hH, wH), (hL, wH), (hH, wL))):
                            mm = nc.tensor.matmul(acc[:, t % NB].unsqueeze(1), a[:, kk, t * P:(t + 1) * P],
                                                  w[:, at[kk], :], start=(kk == 0 and n == 0),
                                                  stop=(kk == KD - 1 and n == 2))
                        if t == NT - 1 and kk < KD - AHEAD:
                            mm.then_inc(w_used, 1)
                    mm.then_inc(summed, 1)
                    if normed and g * NT + t >= 2:
                        turn(g * NT + t - 2)

            def turn(n):
                pe.wait_ge(weighted, n + 1)
                at_least(pe, turn_taken, n)
                for j in range(4):
                    mm = nc.tensor.transpose(pT[:, j], stage[:, n % NT % NS, j * P:(j + 1) * P], c["ident"][:])
                mm.then_inc(turned, 1)
            group(0, True)
            if normed:
                group(1, False)
                turn(2 * NT - 2)
                turn(2 * NT - 1)
            elif n_groups > 1:
                with pe.Fori(1, n_groups) as g:
                    group(g, False)


def project_gates(k, c, hH, hL):
    nc, d = k.nc, k.d
    raw_in, high, low, summed, taken, stored = k.sems("wg_loaded", "wg_high", "wg_low", "gates_summed", "gates_taken",
                                                      "gates_stored")
    spans = [(n * W5, W5) for n in range(SEQ // W5)] + [(SEQ, P)]
    with ExitStack() as s:
        raw = sbuf(nc, s, "graw", [P, KD, 8])
        wH = sbuf(nc, s, "gwH", [P, KD, 8], F32R)
        wL = sbuf(nc, s, "gwL", [P, KD, 8], F32R)
        out = sbuf(nc, s, "gout", [8, TOK])
        acc = psum(nc, s, "gacc", [8, 5, W5])
        block = s.enter_context(nc.Block())

        @block.sync
        def _(sp):
            sp.dma_start(raw[:], d["w_gate"].rearrange("(k p) n -> p k n", p=P)).then_inc(raw_in, 16)
            sp.wait_ge(taken, len(spans))
            sp.dma_start(d["gates_d"], out[:]).then_inc(stored, 16)
            sp.wait_ge(stored, 16)

        @block.vector
        def _(dve):
            dve.wait_ge(raw_in, 16)
            nc.vector.tensor_copy(wH[:], raw[:]).then_inc(high, 1)
            dve.wait_ge(high, 1)
            nc.vector.tensor_tensor(wL[:], raw[:], wH[:].bitcast(F32), ALU.subtract).then_inc(low, 1)
            for n, (a, w) in enumerate(spans):
                dve.wait_ge(summed, n + 1)
                nc.vector.tensor_copy(out[:, a:a + w], acc[:, n, 0:w]).then_inc(taken, 1)

        @block.tensor
        def _(pe):
            pe.wait_ge(low, 1)
            for n, (a, w) in enumerate(spans):
                for kk in range(KD):
                    for m, (wt, h) in enumerate(((wH, hH), (wH, hL), (wL, hH))):
                        mm = nc.tensor.matmul(acc[:, n, 0:w], wt[:, kk], h[:, kk, a:a + w],
                                              start=(kk == 0 and m == 0), stop=(kk == KD - 1 and m == 2))
                mm.then_inc(summed, 1)


LEADS = dict(A=-1, E=2, L=2, LO=0, SP=1, B=3, AL=-2, z=4, av=-3)


def attention(k, c):
    nc, d = k.nc, k.d
    NG = SEQ // W5
    steps = [(T, b) for T in reversed(range(NG)) for b in reversed(range(4 * T + 4))]
    N = len(steps)
    NZ, R = 5, 4
    x_in = [k.sem("qkv_loaded0"), k.sem("qkv_loaded1")]
    (z_ready, e_ready, l_ready, sp_ready, high, low, later_ready, z_full, a_ready, ah_ready, al_ready, av_done,
     o_taken, folded, fold_taken, raw_sp, z_bound, ops_high, ops_ready) = k.sems(
        "z_ready", "exp_ready", "ln_ready", "softplus_ready", "softplus_high", "softplus_low", "later_sum_ready",
        "exponent_ready", "a_ready", "a_high", "a_low", "av_done", "o_taken", "o_folded", "fold_taken", "softplus_raw",
        "z_bounded", "operands_high", "operands_ready")
    stored = [k.sem("o_stored0"), k.sem("o_stored1")]
    with ExitStack() as s:
        Q = sbuf(nc, s, "aq", [P, 2, SEQ], F32R)
        K = sbuf(nc, s, "ak", [P, SEQ], F32R)
        V = sbuf(nc, s, "av", [P, NPT, 2, SD], F32R)
        xq = sbuf(nc, s, "axq", [P, 2, W5])
        xk = sbuf(nc, s, "axk", [P, 2, W5])
        VF = sbuf(nc, s, "avf", [P, NPT, SD])
        ring = {n: sbuf(nc, s, f"a{n}", [P, R, W5], dt) for n, dt in (
            ("E", F32), ("L", F32), ("SP", F32), ("SH", F32R), ("SL", F32R), ("A", F32), ("AH", F32R), ("AL", F32R),
            ("CA", F32))}
        Osb = sbuf(nc, s, "aO", [P, 2, W5])
        of = sbuf(nc, s, "aof", [P, 2, 4, SD])
        Z = psum(nc, s, "a_z", [P, NZ, W5])
        O = psum(nc, s, "a_out", [P, 2, W5])
        F = psum(nc, s, "a_fold", [P, 4, SD])
        block = s.enter_context(nc.Block())
        last = {m: T for m, (T, b) in enumerate(steps) if b == 0}
        first = {m: T for m, (T, b) in enumerate(steps) if b == 4 * T + 3}

        def cols(m):
            T, b = steps[m]
            return slice(max(0, b - 4 * T) * P, W5)

        def own(m):
            T, b = steps[m]
            return slice((b - 4 * T) * P, (b - 4 * T + 1) * P) if b >= 4 * T else None

        def at(name, m, span=None):
            return ring[name][:, m % R, span or cols(m)]

        def freed(eng, sem, h, m, depth=R):
            at_least(eng, sem, h * N + m - depth + 1)

        def splits(m):
            return own(m) is not None or m % 3 == 0
        n_splits = [sum(splits(x) for x in range(m + 1)) for m in range(N)]

        def nth_split(h, m):
            return h * n_splits[-1] + n_splits[m]

        def before(h, m, depth):
            if m >= depth:
                return h, m - depth
            return None if isinstance(h, int) and h == 0 else (h - 1, m - depth + N)

        def wait_exps(eng, h, m):
            if splits(m):
                at_least(eng, ah_ready, nth_split(h, m))
            else:
                at_least(eng, a_ready, h * N + m + 1)

        def pipeline(eng, ops):
            def slots(h, span, back, ahead):
                for n in span:
                    for op, lead in ops:
                        m = n + lead
                        if 0 <= m < N:
                            op(h, m)
                        elif m < 0 and back:
                            op(h - 1, m + N)
                        elif m >= N and ahead:
                            op(h + 1, m - N)
            most, least = max(0, *(a for _, a in ops)), min(0, *(a for _, a in ops))
            slots(0, range(-most, N), False, True)
            with eng.Fori(1, SH - 1) as h:
                slots(h, range(N), True, True)
            slots(SH - 1, range(N - least), True, False)

        def next_group(body):
            def op(h, m):
                if m in last and not (isinstance(h, int) and h == SH - 1):
                    body(h + 1, NG - 1 - last[m], m)
            return op

        @block.sync
        def _(sp):
            def load(h, n):
                G = NG - 1 - n
                at_least(sp, ops_ready, h * NG + n - 1)
                for x, which in ((xq, 0), (xk, 1)):
                    src = d["qk_T"][which, bass.ds(h, 1), :, G * W5:(G + 1) * W5].rearrange("o e t -> (o e) t")
                    for half in range(2):
                        sp.dma_start(x[half * SD:(half + 1) * SD, n % 2], src).then_inc(x_in[n % 2], 16)
                if not isinstance(h, int):
                    sp.wait_ge(av_done, (h - 1) * N + max(m for m in last if last[m] == G) + 1)
                sp.dma_start(VF[:, 4 * G:4 * G + 4], d["proj_out"][3, G * W5:(G + 1) * W5, bass.ds(h * SD, SD)]
                             .rearrange("(b p) e -> p b e", p=P)).then_inc(x_in[n % 2], 16)

            def store(h, n):
                G = NG - 1 - n
                sp.wait_ge(fold_taken, h * NG + n + 1)
                dst = d["o_d"][bass.ds(G * W5, W5), bass.ds(h * SD, SD)].rearrange("(j p) e -> p j e", p=P)
                sp.dma_start(dst, of[:, n % 2]).then_inc(stored[n % 2], 16)
            for n in range(NG):
                load(0, n)
            with sp.Fori(0, SH - 1) as h:
                for n in range(NG):
                    load(h + 1, n)
                    store(h, n)
            for n in range(NG):
                store(SH - 1, n)
            for n in range(2):
                sp.wait_ge(stored[n], 16 * SH * NG // 2)

        @block.scalar
        def _(act):
            def E(h, m):
                act.wait_ge(z_bound, h * N + m + 1)
                nc.scalar.activation(at("E", m), at("E", m), ACT.Exp).then_inc(e_ready, 1)

            def L(h, m):
                act.wait_ge(e_ready, h * N + m + 1)
                freed(act, raw_sp, h, m)
                nc.scalar.activation(at("L", m), at("E", m), ACT.Ln, bias=1.0).then_inc(l_ready, 1)

            def A(h, m):
                act.wait_ge(z_full, h * N + m + 1)
                old = before(h, m, R)
                if old and splits(old[1]):
                    act.wait_ge(al_ready, nth_split(*old))
                freed(act, av_done, h, m)
                nc.scalar.activation(at("A", m), Z[:, m % NZ, cols(m)], ACT.Exp).then_inc(a_ready, 1)
                if splits(m):
                    nc.scalar.activation(at("AH", m), Z[:, m % NZ, cols(m)], ACT.Exp).then_inc(ah_ready, 1)

            def split(h, n, m=None):
                G = NG - 1 - n
                span = slice(G * W5, (G + 1) * W5)
                act.wait_ge(x_in[n % 2], 80 * (h * (NG // 2) + n // 2 + 1))
                if m is not None:
                    act.wait_ge(av_done, (h - 1) * N + m + 1)
                cp = nc.scalar.activation
                cp(K[:, span], xk[:, n % 2], ACT.Copy)
                cp(Q[:, 0, span], xq[:, n % 2], ACT.Copy)
                cp(Q[:, 1, span], xq[:, n % 2], ACT.Copy)
                cp(V[:, 4 * G:4 * G + 4, 0, :], VF[:, 4 * G:4 * G + 4], ACT.Copy).then_inc(ops_high, 1)
            act.preload_act_table_set("natural_log_exp_and_others")
            for n in range(NG):
                split(0, n)
            pipeline(act, [(A, LEADS["A"]), (E, LEADS["E"]), (L, LEADS["L"]), (next_group(split), -4)])

        @block.vector
        def _(dve):
            v = nc.vector

            def SP(h, m):
                dve.wait_ge(l_ready, h * N + m + 1)
                freed(dve, later_ready, h, m)
                freed(dve, low, h, m)
                v.tensor_tensor(at("SP", m), at("L", m), Z[:, m % NZ, cols(m)], ALU.max).then_inc(raw_sp, 1)
                if own(m):
                    dve.wait_ge(raw_sp, h * N + m + 1)
                    v.tensor_tensor(at("SP", m, own(m)), at("SP", m, own(m)), c["keep"][:], ALU.mult).then_inc(sp_ready, 1)

            def BOUND(h, m):
                dve.wait_ge(z_ready, h * N + m + 1)
                freed(dve, l_ready, h, m)
                v.tensor_scalar(at("E", m), Z[:, m % NZ, cols(m)], 41.0, None, ALU.min).then_inc(z_bound, 1)

            def LO(h, m):
                dve.wait_ge(high, h * N + m + 1)
                freed(dve, z_full, h, m)
                v.tensor_tensor(at("SL", m), at("SP", m), at("SH", m).bitcast(F32), ALU.subtract).then_inc(low, 1)

            def AL(h, m):
                if not splits(m):
                    return
                dve.wait_ge(a_ready, h * N + m + 1)
                dve.wait_ge(ah_ready, nth_split(h, m))
                freed(dve, av_done, h, m)
                v.tensor_tensor(at("AL", m), at("A", m), at("AH", m).bitcast(F32), ALU.subtract).then_inc(al_ready, 1)

            def OUT(h, m):
                if m in last:
                    n = NG - 1 - last[m]
                    dve.wait_ge(av_done, h * N + m + 1)
                    at_least(dve, folded, h * NG + n - 1)
                    v.tensor_copy(Osb[:, n % 2], O[:, n % 2]).then_inc(o_taken, 1)

            def FOLDED(h, m):
                if m in last:
                    n = NG - 1 - last[m]
                    dve.wait_ge(folded, h * NG + n + 1)
                    at_least(dve, stored[n % 2], 16 * (h * (NG // 2) + n // 2))
                    v.tensor_copy(of[:, n % 2], F[:]).then_inc(fold_taken, 1)

            def split(h, n, m=None):
                G = NG - 1 - n
                span = slice(G * W5, (G + 1) * W5)
                top, bottom = slice(0, SD), slice(SD, P)
                dve.wait_ge(ops_high, h * NG + n + 1)
                for dst, x, rows in ((K[:, span], xk[:, n % 2], bottom), (Q[:, 0, span], xq[:, n % 2], bottom),
                                     (Q[:, 1, span], xq[:, n % 2], top)):
                    v.tensor_tensor(dst[rows], x[rows], dst[rows].bitcast(F32), ALU.subtract)
                blocks = slice(4 * G, 4 * G + 4)
                v.tensor_tensor(V[:, blocks, 1, :], VF[:, blocks], V[:, blocks, 0, :].bitcast(F32),
                                ALU.subtract).then_inc(ops_ready, 1)
            for n in range(NG):
                split(0, n)
            pipeline(dve, [(SP, LEADS["SP"]), (LO, LEADS["LO"]), (BOUND, LEADS["B"]), (AL, LEADS["AL"]), (OUT, -4),
                           (FOLDED, -6), (next_group(split), -5)])

        @block.gpsimd
        def _(pool):
            ones = lambda n: c["one"][:].to_broadcast([P, n])
            masked = [sum(own(x) is not None for x in range(m + 1)) for m in range(N)]
            tt = nc.gpsimd.tensor_tensor

            def HI(h, m):
                pool.wait_ge(raw_sp, h * N + m + 1)
                at_least(pool, sp_ready, h * masked[-1] + masked[m])
                freed(pool, z_full, h, m)
                tt(at("SH", m), at("SP", m), ones(W5 - cols(m).start), ALU.mult).then_inc(high, 1)

            def SUM(h, m):
                at_least(pool, later_ready, h * N + m)
                freed(pool, z_full, h, m + 1)
                rest = slice(cols(m).start + (P if own(m) else 0), W5)
                if own(m):
                    op = tt(at("CA", m + 1, own(m)), at("SP", m, own(m)), ones(P), ALU.mult)
                if rest.start < W5:
                    op = tt(at("CA", m + 1, rest), at("CA", m, rest), at("SP", m, rest), ALU.add)
                op.then_inc(later_ready, 1)
            pipeline(pool, [(HI, 1), (SUM, 1)])

        @block.tensor
        def _(pe):
            go = dict(start=False, stop=True, skip_group_check=True)

            def z(h, m):
                T, b = steps[m]
                if T == NG - 1 and b % 4 == 3:
                    pe.wait_ge(ops_ready, h * NG + NG - b // 4)
                old = before(h, m, NZ)
                if old:
                    wait_exps(pe, *old)
                span = slice(4 * T * P + cols(m).start, 4 * T * P + W5)
                for part in range(2):
                    mm = nc.tensor.matmul(Z[:, m % NZ, cols(m)], K[:, b * P:(b + 1) * P], Q[:, part, span],
                                          start=(part == 0), stop=(part == 1))
                mm.then_inc(z_ready, 1)

            def sub(h, m):
                to = Z[:, m % NZ]
                pe.wait_ge(raw_sp, h * N + m + 1)
                if m not in first:
                    rest = slice(cols(m).start + (P if own(m) else 0), W5)
                    pe.wait_ge(later_ready, h * N + m)
                    nc.tensor.matmul(to[:, rest], c["nones"][:], at("CA", m, rest), **go)
                if own(m):
                    nc.tensor.matmul(to[:, own(m)], c["ident_r"][:], c["far_r"][:], **go)
                pe.wait_ge(high, h * N + m + 1)
                nc.tensor.matmul(to[:, cols(m)], c["tri_r"][:], at("SH", m), **go)
                pe.wait_ge(low, h * N + m + 1)
                nc.tensor.matmul(to[:, cols(m)], c["tri_r"][:], at("SL", m), **go).then_inc(z_full, 1)

            def av(h, m):
                T, b = steps[m]
                n = NG - 1 - T
                if m in first:
                    at_least(pe, o_taken, h * NG + n - 1)
                wait_exps(pe, h, m)
                if not splits(m):
                    nc.tensor.matmul(O[0:SD, n % 2, cols(m)], VF[:, b], at("A", m), start=False, stop=(m in last),
                                     skip_group_check=True).then_inc(av_done, 1)
                    return
                vb = V[:, b].rearrange("p n e -> p (n e)")
                nc.tensor.matmul(O[:, n % 2, cols(m)], vb, at("AH", m), start=(m in first), stop=False,
                                 skip_group_check=True)
                pe.wait_ge(al_ready, nth_split(h, m))
                nc.tensor.matmul(O[:, n % 2, cols(m)], vb, at("AL", m), start=False, stop=(m in last),
                                 skip_group_check=True).then_inc(av_done, 1)

            def fold(h, m):
                if m in last:
                    n = NG - 1 - last[m]
                    pe.wait_ge(o_taken, h * NG + n + 1)
                    at_least(pe, fold_taken, h * NG + n)
                    for j in range(4):
                        mm = nc.tensor.matmul(F[:, j, :], Osb[:, n % 2, j * P:(j + 1) * P], c["fold"][:],
                                              start=(j == 0), stop=True, skip_group_check=True)
                    mm.then_inc(folded, 1)
            pipeline(pe, [(sub, 0), (av, LEADS["av"]), (z, LEADS["z"]), (fold, -5)])


def attention_sample(k, c, w_out):
    nc, d = k.nc, k.d
    N, NZ, W = NPB + 1, 3, SH * DEC
    qk_high, qk_low, qk_turned, qk_taken, v_in, v_high, v_low, w_in = k.sems(
        "qk_high", "qk_low", "qk_turned", "qk_taken", "v_loaded", "v_high", "v_low", "w_out_loaded")
    (q_in, k_in, z_ready, z_bound, e_ready, l_ready, sp_raw, sp_ready, high, low, later_ready, z_full, a_ready, ah_ready,
     al_ready, av_done, zeroed, o_taken, folded, fold_taken, stored) = k.sems(
        "q_loaded", "k_loaded", "z_ready", "z_bounded", "exp_ready", "ln_ready", "softplus_raw", "softplus_ready",
        "softplus_high", "softplus_low", "later_sum_ready", "exponent_ready", "a_ready", "a_high", "a_low", "av_done",
        "zeroed", "o_taken", "o_folded", "fold_taken", "o_stored")
    with ExitStack() as s:
        q = sbuf(nc, s, "bq", [P, 2, SH, P], F32R)
        K = sbuf(nc, s, "bK", [P, N, SH, P], F32R)
        V = sbuf(nc, s, "bV", [P, N, SH, 2, SD], F32R)
        xq = sbuf(nc, s, "bxq", [P, SH, SD])
        xk = sbuf(nc, s, "bxk", [P, N, W5])
        xv = sbuf(nc, s, "bxv", [P, N, W5])
        parts = sbuf(nc, s, "bparts", [P, 2, SH, 3, SD], F32R)
        ring = {n: sbuf(nc, s, f"b{n}", [P, 2, W], dt) for n, dt in (
            ("E", F32), ("L", F32), ("SP", F32), ("SH", F32R), ("SL", F32R), ("A", F32), ("AH", F32R), ("AL", F32R),
            ("CA", F32))}
        Osb = sbuf(nc, s, "bO", [P, W])
        out = sbuf(nc, s, "bout", [P, W5])
        Z = psum(nc, s, "b_z", [P, NZ, W5])
        O = psum(nc, s, "b_out", [P, W5])
        F = psum(nc, s, "b_fold", [DEC, W5])
        pT = psum(nc, s, "b_turn", [P, 2, 4, P])
        block = s.enter_context(nc.Block())
        heads = lambda ap: ap.rearrange("p (h t) -> p h t", t=DEC)
        over_heads = lambda ap: ap[:, 0:DEC].unsqueeze(1).to_broadcast([P, SH, DEC])
        col = lambda h: slice(h * DEC, (h + 1) * DEC)

        @block.sync
        def _(sp):
            own = tok(NPT)
            sp.dma_start(xq[:].rearrange("p h e -> p (h e)"), d["proj_out"][5, own, :]).then_inc(q_in, 16)
            for x, g, cache, sem in ((xk, 6, "past_k", k_in), (xv, 3, "past_v", v_in)):
                sp.dma_start(x[:, 0], d["proj_out"][g, own, :]).then_inc(sem, 16)
                sp.dma_start(x[:, 1:], d[cache].rearrange("(b p) n -> p b n", p=P)).then_inc(sem, 16)
            sp.dma_start(w_out[:], d["w_out"].rearrange("(k p) n -> p k n", p=P)).then_inc(w_in, 16)
            sp.wait_ge(w_in, 16)
            sp.wait_ge(fold_taken, 1)
            sp.dma_start(d["o_d"][SEQ:, :], out[:]).then_inc(stored, 16)
            sp.wait_ge(stored, 16)

        def blk(m):
            return 0 if m == 0 else NPB + 1 - m

        turns = [(None, half, form, q[:, form, 4 * half:4 * half + 4]) for form in range(2) for half in range(2)]
        turns += [(n, half, 0, K[:, n, 4 * half:4 * half + 4]) for n in range(N) for half in range(2)]
        turns_of = lambda i: range(0, 4) if i == 0 else range(2 * i + 2, 2 * i + 4)

        @block.scalar
        def _(act):
            def parts_high(i):
                if i > 0:
                    act.wait_ge(k_in, 32)
                else:
                    act.wait_ge(q_in, 16)
                if i >= 2:
                    act.wait_ge(qk_turned, turns_of(i - 2)[-1] + 1)
                src = xq[:] if i == 0 else xk[:, i - 1].rearrange("p (h e) -> p h e", e=SD)
                for part in (0, 2) if i == 0 else (0,):
                    op = nc.scalar.activation(parts[:, i % 2, :, part], src, ACT.Copy)
                op.then_inc(qk_high, 1)
            parts_high(0)
            for i in range(N + 1):
                if i < N:
                    parts_high(i + 1)
                for n in turns_of(i):
                    act.wait_ge(qk_turned, n + 1)
                    nc.scalar.activation(turns[n][3], pT[:, n % 2], ACT.Copy).then_inc(qk_taken, 1)
            act.preload_act_table_set("natural_log_exp_and_others")
            for m in range(N + 1):
                if m < N:
                    act.wait_ge(z_bound, m + 1)
                    at = ring["E"][:, m % 2]
                    nc.scalar.activation(at, at, ACT.Exp).then_inc(e_ready, 1)
                    act.wait_ge(e_ready, m + 1)
                    if m >= 2:
                        act.wait_ge(sp_raw, m - 1)
                    nc.scalar.activation(ring["L"][:, m % 2], at, ACT.Ln, bias=1.0).then_inc(l_ready, 1)
                n = m - 1
                if n >= 0:
                    act.wait_ge(z_full, n + 1)
                    if n >= 2:
                        act.wait_ge(al_ready, n - 1)
                        act.wait_ge(av_done, n - 1)
                    nc.scalar.activation(ring["A"][:, n % 2], Z[:, n % NZ, 0:W], ACT.Exp).then_inc(a_ready, 1)
                    nc.scalar.activation(ring["AH"][:, n % 2], Z[:, n % NZ, 0:W], ACT.Exp).then_inc(ah_ready, 1)

        @block.vector
        def _(dve):
            v = nc.vector

            def bound(m):
                dve.wait_ge(z_ready, m + 1)
                if m >= 2:
                    dve.wait_ge(l_ready, m - 1)
                v.tensor_scalar(ring["E"][:, m % 2], Z[:, m % NZ, 0:W], 41.0, None, ALU.min).then_inc(z_bound, 1)
            for i in range(N + 1):
                src = xq[:] if i == 0 else xk[:, i - 1].rearrange("p (h e) -> p h e", e=SD)
                dve.wait_ge(qk_high, i + 1)
                v.tensor_tensor(parts[:, i % 2, :, 1], src, parts[:, i % 2, :, 0].bitcast(F32),
                                ALU.subtract).then_inc(qk_low, 1)
            dve.wait_ge(v_high, 1)
            v.tensor_tensor(V[:, :, :, 1], xv[:].rearrange("p b (h e) -> p b h e", e=SD), V[:, :, :, 0].bitcast(F32),
                            ALU.subtract).then_inc(v_low, 1)
            bound(0)
            for m in range(N):
                if m + 1 < N:
                    bound(m + 1)
                at = ring["SP"][:, m % 2]
                dve.wait_ge(l_ready, m + 1)
                if m >= 2:
                    dve.wait_ge(later_ready, m - 1)
                    dve.wait_ge(low, m - 1)
                    dve.wait_ge(high, m - 1)
                v.tensor_tensor(at, ring["L"][:, m % 2], Z[:, m % NZ, 0:W], ALU.max).then_inc(sp_raw, 1)
                if m == 0:
                    dve.wait_ge(sp_raw, 1)
                    v.tensor_tensor(heads(at), heads(at), over_heads(c["keep"]), ALU.mult).then_inc(sp_ready, 1)
                dve.wait_ge(high, m + 1)
                if m >= 2:
                    dve.wait_ge(z_full, m - 1)
                v.tensor_tensor(ring["SL"][:, m % 2], at, ring["SH"][:, m % 2].bitcast(F32), ALU.subtract).then_inc(low, 1)
                dve.wait_ge(ah_ready, m + 1)
                dve.wait_ge(a_ready, m + 1)
                if m >= 2:
                    dve.wait_ge(av_done, m - 1)
                v.tensor_tensor(ring["AL"][:, m % 2], ring["A"][:, m % 2], ring["AH"][:, m % 2].bitcast(F32),
                                ALU.subtract).then_inc(al_ready, 1)
            dve.wait_ge(av_done, N)
            v.tensor_copy(Osb[:], O[:, 0:W]).then_inc(o_taken, 1)
            dve.wait_ge(folded, 1)
            dve.wait_ge(zeroed, 2)
            v.tensor_copy(out[0:DEC, :], F[:]).then_inc(fold_taken, 1)

        @block.gpsimd
        def _(pool):
            g = nc.gpsimd
            pool.wait_ge(v_in, 32)
            g.tensor_copy(V[:, :, :, 0], xv[:].rearrange("p b (h e) -> p b h e", e=SD)).then_inc(v_high, 1)
            g.memset(ring["CA"][:], 0.0).then_inc(zeroed, 1)
            g.memset(out[:], 0.0).then_inc(zeroed, 1)
            pool.wait_ge(zeroed, 2)
            for m in range(N):
                pool.wait_ge(sp_raw, m + 1)
                pool.wait_ge(sp_ready, 1)
                if m >= 2:
                    pool.wait_ge(z_full, m - 1)
                g.tensor_copy(ring["SH"][:, m % 2], ring["SP"][:, m % 2]).then_inc(high, 1)
                if m > 0:
                    pool.wait_ge(later_ready, m)
                    pool.wait_ge(z_full, m)
                g.tensor_tensor(ring["CA"][:, (m + 1) % 2], ring["CA"][:, m % 2], ring["SP"][:, m % 2],
                                ALU.add).then_inc(later_ready, 1)

        @block.tensor
        def _(pe):
            mm = nc.tensor.matmul
            go = dict(start=False, stop=True, skip_group_check=True)

            def z(m):
                if m >= NZ:
                    pe.wait_ge(ah_ready, m - NZ + 1)
                for h in range(SH):
                    for part in range(2):
                        op = mm(Z[:, m % NZ, col(h)], K[:, blk(m), h], q[:, part, h, 0:DEC],
                                start=(h == 0 and part == 0), stop=(part == 1), skip_group_check=True)
                op.then_inc(z_ready, 1)

            def av(m):
                for n, (src, sem) in enumerate((("AH", ah_ready), ("AL", al_ready))):
                    pe.wait_ge(sem, m + 1)
                    for h in range(SH):
                        op = mm(O[:, col(h)], V[:, blk(m), h].rearrange("p n e -> p (n e)"), ring[src][:, m % 2, col(h)],
                                start=(m == 0 and n == 0 and h == 0), stop=(m == N - 1 and n == 1),
                                skip_group_check=True)
                op.then_inc(av_done, 1)
            for n, (blk_n, half, form, _) in enumerate(turns):
                i = 0 if blk_n is None else blk_n + 1
                pe.wait_ge(qk_low, i + 1)
                if n >= 2:
                    pe.wait_ge(qk_taken, n - 1)
                for h in range(4):
                    op = nc.tensor.transpose(pT[:, n % 2, h], parts[:, i % 2, 4 * half + h, form:form + 2]
                                             .rearrange("p n e -> p (n e)").bitcast(F32), c["ident"][:])
                op.then_inc(qk_turned, 1)
            pe.wait_ge(v_low, 1)
            pe.wait_ge(qk_taken, len(turns))
            z(0)
            for m in range(N):
                if m + 1 < N:
                    z(m + 1)
                if m > 0:
                    av(m - 1)
                at = Z[:, m % NZ, 0:W]
                pe.wait_ge(sp_raw, m + 1)
                if m > 0:
                    pe.wait_ge(later_ready, m)
                    mm(at, c["nones"][:], ring["CA"][:, m % 2], **go)
                else:
                    for h in range(SH):
                        mm(Z[:, 0, col(h)], c["ident_r"][:], c["far_r"][:, 0:DEC], **go)
                pe.wait_ge(high, m + 1)
                mm(at, c["tri_r"][:], ring["SH"][:, m % 2], **go)
                pe.wait_ge(low, m + 1)
                mm(at, c["tri_r"][:], ring["SL"][:, m % 2], **go).then_inc(z_full, 1)
            av(N - 1)
            pe.wait_ge(o_taken, 1)
            for h in range(SH):
                op = mm(F[:, h * SD:(h + 1) * SD], Osb[:, col(h)], c["fold"][:], start=(h == 0), stop=True,
                        skip_group_check=True)
            op.then_inc(folded, 1)


def gate_rows(k, c, gc, dec):
    nc, d = k.nc, k.d
    (loaded, mask_ready, biased, abs_ready, e_ready, l_ready, lf_ready, padded, b_ready, m_ready, mp_ready, u_ready, args_ready,
     w_ready, stored, zeroed, turned, taken, dec_args, dec_sum) = k.sems(
        "gates_loaded", "chunk_mask_ready", "gates_biased", "abs_ready", "exp_ready", "ln_ready", "log_forget_ready",
        "padding_set", "b_ready", "m_ready", "m_before_ready", "u_ready", "arguments_ready", "weights_ready", "rows_stored",
        "rows_zeroed", "weights_turned", "weights_taken", "decay_rows", "decay_sum")
    with ExitStack() as s:
        def row(name):
            return sbuf(nc, s, name, [MH, NT, P])
        IG, FG, AB, LF, B, M, U, G, cm = map(row, ("rIG", "rFG", "rAB", "rLF", "rB", "rM", "rU", "rG", "rcm"))
        gb = sbuf(nc, s, "rgb", [MH, 2])
        m0 = sbuf(nc, s, "rm0", [MH, 1])
        mp = sbuf(nc, s, "rmp", [MH, NT])
        dl = sbuf(nc, s, "rdl", [MH, NT])
        W = sbuf(nc, s, "rW", [96, NT, P])
        dd = sbuf(nc, s, "rdd", [MH, NT, MH])
        pw = psum(nc, s, "rpw", [P, 4, W5])
        pd = psum(nc, s, "rpd", [P, W5])
        block = s.enter_context(nc.Block())
        flat = lambda x: x[:].rearrange("h n t -> h (n t)")
        bc = lambda x: x.unsqueeze(2).to_broadcast([MH, NT, P])

        @block.sync
        def _(sp):
            sp.dma_start(flat(IG), d["gates_d"][0:MH, :]).then_inc(loaded, 16)
            sp.dma_start(flat(FG), d["gates_d"][MH:2 * MH, :]).then_inc(loaded, 16)
            sp.dma_start(gb[:], d["b_gates"]).then_inc(loaded, 16)
            sp.dma_start(m0[:], d["m_init"]).then_inc(loaded, 16)
            sp.wait_ge(u_ready, 2)
            sp.dma_start(d["ug_d"][0], flat(G)).then_inc(stored, 16)
            sp.dma_start(d["ug_d"][1], flat(U)).then_inc(stored, 16)
            sp.dma_start(d["m_out"][0], M[:, NPT - 1, P - 1:P]).then_inc(stored, 16)
            sp.dma_start(d["m_out"][1], M[:, NT - 1, P - 1:P]).then_inc(stored, 16)
            sp.wait_ge(stored, 64)

        @block.gpsimd
        def _(pool):
            nc.gpsimd.memset(cm[:], 1.0).then_inc(mask_ready, 1)
            pool.wait_ge(mask_ready, 1)
            nc.gpsimd.memset(cm[:, :, 0:1], 0.0).then_inc(mask_ready, 1)
            nc.gpsimd.memset(W[:], 0.0).then_inc(zeroed, 1)

        @block.scalar
        def _(act):
            act.preload_act_table_set("natural_log_exp_and_others")
            act.wait_ge(abs_ready, 1)
            nc.scalar.activation(AB[:], AB[:], ACT.Exp, scale=-1.0).then_inc(e_ready, 1)
            act.wait_ge(e_ready, 1)
            nc.scalar.activation(AB[:], AB[:], ACT.Ln, bias=1.0).then_inc(l_ready, 1)
            act.wait_ge(zeroed, 1)
            act.wait_ge(m_ready, 2)
            nc.scalar.activation(W[64:64 + MH], M[:], ACT.Exp, scale=-1.0).then_inc(w_ready, 1)
            act.wait_ge(args_ready, 1)
            nc.scalar.activation(W[0:MH], IG[:], ACT.Exp).then_inc(w_ready, 1)
            act.wait_ge(args_ready, 2)
            nc.scalar.activation(W[32:32 + MH], FG[:], ACT.Exp).then_inc(w_ready, 1)

        @block.vector
        def _(dve):
            v = nc.vector
            dve.wait_ge(loaded, 64)
            v.tensor_scalar(IG[:], IG[:], gb[:, 0:1], None, ALU.add).then_inc(biased, 1)
            v.tensor_scalar(FG[:], FG[:], gb[:, 1:2], None, ALU.add).then_inc(biased, 1)
            dve.wait_ge(biased, 2)
            v.scalar_tensor_tensor(out=AB[:], in0=FG[:], scalar=-1.0, in1=FG[:], op0=ALU.mult,
                                   op1=ALU.max).then_inc(abs_ready, 1)
            dve.wait_ge(l_ready, 1)
            v.scalar_tensor_tensor(out=LF[:], in0=FG[:], scalar=0.0, in1=AB[:], op0=ALU.min,
                                   op1=ALU.subtract).then_inc(lf_ready, 1)
            dve.wait_ge(lf_ready, 1)
            v.memset(LF[:, NT - 1, DEC:], 0.0).then_inc(padded, 1)
            v.memset(IG[:, NT - 1, DEC:], FAR).then_inc(padded, 1)
            dve.wait_ge(padded, 2)
            dve.wait_ge(mask_ready, 2)
            v.tensor_tensor_scan(flat(B), flat(cm), flat(LF), 0.0, ALU.mult, ALU.add).then_inc(b_ready, 1)
            v.tensor_tensor_scan(flat(M)[:, 0:SEQ], flat(LF)[:, 0:SEQ], flat(IG)[:, 0:SEQ], 0.0, ALU.add,
                                 ALU.max).then_inc(m_ready, 1)
            v.tensor_tensor_scan(flat(M)[:, SEQ:], flat(LF)[:, SEQ:], flat(IG)[:, SEQ:], m0[:], ALU.add,
                                 ALU.max).then_inc(m_ready, 1)
            v.memset(mp[:, 0:1], 0.0).then_inc(mp_ready, 1)
            v.tensor_copy(mp[:, NT - 1:NT], m0[:]).then_inc(mp_ready, 1)
            dve.wait_ge(m_ready, 2)
            v.tensor_copy(mp[:, 1:NPT], M[:, 0:NPT - 1, P - 1]).then_inc(mp_ready, 1)
            dve.wait_ge(b_ready, 1)
            v.tensor_tensor(dl[:], B[:, :, P - 1], M[:, :, P - 1], ALU.subtract).then_inc(mp_ready, 1)
            v.tensor_tensor(U[:], B[:], M[:], ALU.subtract).then_inc(u_ready, 1)
            v.tensor_tensor(G[:], IG[:], B[:], ALU.subtract).then_inc(u_ready, 1)
            dve.wait_ge(u_ready, 2)
            dve.wait_ge(mp_ready, 4)
            v.tensor_tensor(IG[:], U[:], bc(mp[:]), ALU.add).then_inc(args_ready, 1)
            v.tensor_tensor(FG[:], G[:], bc(dl[:]), ALU.add).then_inc(args_ready, 1)
            dve.wait_ge(w_ready, 3)
            v.scalar_tensor_tensor(out=dd[:], in0=W[0:MH, :, P - 1].unsqueeze(2).to_broadcast([MH, NT, MH]), scalar=-1.0,
                                   in1=c["ident"][0:MH, 0:MH].unsqueeze(1).to_broadcast([MH, NT, MH]), op0=ALU.mult,
                                   op1=ALU.mult).then_inc(dec_args, 1)
            dve.wait_ge(turned, 1)
            for n in range(0, NT, 5):
                m = min(5, NT - n)
                src = pw[:, n // 5, 0:m * 96].rearrange("p (n q x) -> p n q x", q=3, x=32)[:, :, :, 0:MH]
                v.tensor_copy(gc[:, n:n + m], src).then_inc(taken, 1)
            dve.wait_ge(dec_sum, 1)
            v.tensor_copy(dec[:], pd[:, 0:NT * MH].rearrange("p (n h) -> p n h", h=MH)).then_inc(taken, 1)

        @block.tensor
        def _(pe):
            pe.wait_ge(w_ready, 3)
            for n in range(NT):
                mm = nc.tensor.transpose(pw[:, n // 5, (n % 5) * 96:(n % 5 + 1) * 96], W[:, n], c["ident"][0:96, 0:96])
            mm.then_inc(turned, 1)
            pe.wait_ge(dec_args, 1)
            nc.tensor.matmul(pd[:, 0:NT * MH], c["nones"][0:MH, :], dd[:].rearrange("h n g -> h (n g)"),
                             start=True, stop=True).then_inc(dec_sum, 1)


def mlstm(k, c, gc, dec):
    nc, d = k.nc, k.d
    MA = MD + 1
    qkv_in = [k.sem("qkv_loaded0"), k.sem("qkv_loaded1")]
    ug_in = [k.sem("ug_loaded0"), k.sem("ug_loaded1")]
    stored = [k.sem("h_stored0"), k.sem("h_stored1")]
    (ones_ready, state_in, k_scaled, q_weighted, v_ready, vw_ready, turned, q_taken, k_taken, qw_taken, d_ready, s_ready,
     dm_ready, w_ready, sw_ready, num_ready, u_ready, decayed, c_ready, dn_ready, ab_ready, fl_ready, rd_ready, h_ready,
     c_stored) = k.sems(
        "ones_ready", "state_loaded", "k_scaled", "q_weighted", "v_ready", "v_weighted", "qk_turned", "q_taken", "k_taken",
        "qw_taken", "exponent_ready", "scores_ready", "exponent_masked", "weights_ready", "scores_weighted",
        "numerator_ready", "update_ready", "memory_decayed", "memory_ready", "den_ready", "den_abs", "den_floored",
        "den_inverse", "h_ready", "memory_stored")
    w_in = [k.sem("w_ada_loaded0"), k.sem("w_ada_loaded1")]
    bias_in, mod_psum, mod_ready, mod_turned, mod_row, mod_stored, plus_one, scale_ready = k.sems(
        "bias_loaded", "mod_summed", "mod_ready", "mod_turned", "mod_row_ready", "mod_stored", "scale_plus_one", "scale_ready")
    NM = 6 * KD - NMOD
    with ExitStack() as s:
        wa = sbuf(nc, s, "mwa", [P, 2, KD, 2 * P])
        mod_rows = sbuf(nc, s, "mmod_rows", [2, NM * P])
        bias = sbuf(nc, s, "mbias", [2, NM * P])
        pm = psum(nc, s, "mpm", [P, W5])
        x = sbuf(nc, s, "mx", [P, 2, 3, MH, MD])
        LG = sbuf(nc, s, "mLG", [2, 2, MH, P])
        RU = sbuf(nc, s, "mRU", [2, 2, MH, P])
        ks = sbuf(nc, s, "mks", [P, 2, MH, MD])
        qw = sbuf(nc, s, "mqw", [P, 2, MH, MD])
        VI = sbuf(nc, s, "mVI", [P, 2, MH, MA])
        VU = sbuf(nc, s, "mVU", [P, 2, MH, MA])
        T = sbuf(nc, s, "mT", [P, 2, 3, MH, P])
        DM = sbuf(nc, s, "mDM", [P, MH, P])
        WX = sbuf(nc, s, "mWX", [P, MH, P])
        SW = sbuf(nc, s, "mSW", [P, 2, MH, P])
        C = [sbuf(nc, s, "mC0", [P, MH, MA]), sbuf(nc, s, "mC1", [P, MH, MA])]
        dn = sbuf(nc, s, "mdn", [P, 4, MH])
        H = sbuf(nc, s, "mH", [P, 2, MH, MD])
        pT = psum(nc, s, "mpT", [P, 3, W5])
        pD = psum(nc, s, "mpD", [P, W5])
        pS = psum(nc, s, "mpS", [P, W5])
        pN = psum(nc, s, "mpN", [P, 2, W5])
        block = s.enter_context(nc.Block())
        pairs = lambda ap: ap[:, :, 0:2 * MA].rearrange("p b (h e) -> p b h e", e=MA)
        heads = lambda ap: ap.rearrange("p (b h) e -> p b h e", b=2)
        per_head = lambda col, n: col.unsqueeze(2).to_broadcast([P, MH, n])

        def chunks(eng, before, slot, after):
            before((0, 0, 0))
            for t in range(2):
                slot((t, t, 0), (t + 1, 1 - t, t))
            with eng.Fori(1, NPT // 2 - 1) as i:
                slot((2 * i, 0, i), (2 * i + 1, 1, i))
                slot((2 * i + 1, 1, i), (2 * i + 2, 0, i + 1))
            for t in range(NPT - 2, NPT):
                slot((t, t % 2, t // 2), (t + 1, (t + 1) % 2, (t + 1) // 2))
            after((NPT, 0, NPT // 2))

        @block.sync
        def _(sp):
            sp.dma_start(C[1][:], d["c_init"]).then_inc(state_in, 16)
            sp.dma_start(bias[:], d["b_ada"][:, NMOD * P:].to_broadcast([2, NM * P])).then_inc(bias_in, 16)

            def body(t, u, r, first):
                if not first:
                    sp.wait_ge(turned, t - 1)
                    sp.wait_ge(vw_ready, t - 1)
                    sp.wait_ge(d_ready, t - 1)
                for n in range(3):
                    sp.dma_start(x[:, u, n].rearrange("p h e -> p (h e)"), d["proj_out"][n, tok(t), :]).then_inc(qkv_in[u], 16)
                sp.wait_ge(ones_ready, 2)
                sp.dma_start(LG[0:1, u], d["ug_d"][0:1, :, tok(t)]).then_inc(ug_in[u], 16)
                sp.dma_start(RU[1:2, u], d["ug_d"][1:2, :, tok(t)]).then_inc(ug_in[u], 16)
                if not (isinstance(t, int) and t == NPT):
                    if not first:
                        sp.wait_ge(mod_psum, t - 1)
                    sp.dma_start(wa[:, u], d["w_ada"].rearrange("(k p) n -> p k n", p=P)
                                 [:, :, bass.ds(t * 2 * P + NMOD * P, 2 * P)]).then_inc(w_in[u], 16)
            tiles(sp, body)
            sp.wait_ge(mod_row, NPT)
            sp.dma_start(d["mods"], mod_rows[:]).then_inc(mod_stored, 16)
            sp.wait_ge(mod_stored, 16)
            sp.wait_ge(c_ready, NPT)
            sp.dma_start(d["c_out"][0], C[0][:]).then_inc(c_stored, 16)
            sp.wait_ge(c_ready, NT)
            sp.dma_start(d["c_out"][1], C[1][:]).then_inc(c_stored, 16)
            sp.wait_ge(c_stored, 32)
            for u in range(2):
                sp.wait_ge(stored[u], 16 * len(range(u, NT, 2)))

        @block.gpsimd
        def _(pool):
            nc.gpsimd.memset(LG[:], 1.0).then_inc(ones_ready, 1)
            nc.gpsimd.memset(RU[:], 1.0).then_inc(ones_ready, 1)
            nc.gpsimd.memset(VI[:], 1.0).then_inc(ones_ready, 1)
            nc.gpsimd.memset(C[0][:], 0.0).then_inc(ones_ready, 1)

            def body(t, u, r, first):
                pool.wait_ge(h_ready, t + 1)
                pool.dma_start(d["h_d"][tok(t), :], H[:, u].rearrange("p h e -> p (h e)")).then_inc(stored[u], 16)
            tiles(pool, body)

        @block.scalar
        def _(act):
            act.preload_act_table_set("natural_log_exp_and_others")
            act.wait_ge(ones_ready, 4)

            def body(t, u, r, first):
                act.wait_ge(qkv_in[u], 48 * r + 48)
                if not first:
                    act.wait_ge(turned, t - 1)
                    act.wait_ge(u_ready, t - 1)
                nc.scalar.activation(ks[:, u], x[:, u, 1], ACT.Copy, scale=MD ** -0.5).then_inc(k_scaled, 1)
                nc.scalar.activation(VI[:, u, :, 0:MD], x[:, u, 2], ACT.Copy).then_inc(v_ready, 1)
                act.wait_ge(turned, t + 1)
                nc.scalar.activation(T[:, u, 0], pT[:, 0].rearrange("p (h e) -> p h e", e=P), ACT.Copy).then_inc(q_taken, 1)
                act.wait_ge(dm_ready, t + 1)
                at_least(act, sw_ready, t)
                nc.scalar.activation(WX[:], DM[:], ACT.Exp).then_inc(w_ready, 1)
            tiles(act, body)

        @block.vector
        def _(dve):
            v = nc.vector

            gates = lambda t: gc[:, bass.ds(t, 1)].rearrange("p o q h -> p (o q) h")

            def prepare(chunk):
                t, u, r = chunk
                g = gates(t)
                dve.wait_ge(qkv_in[u], 48 * r + 48)
                at_least(dve, turned, t - 1)
                v.tensor_tensor(qw[:, u], x[:, u, 0], per_head(g[:, 0], MD), ALU.mult).then_inc(q_weighted, 1)
                dve.wait_ge(v_ready, t + 1)
                v.tensor_tensor(VU[:, u], VI[:, u], per_head(g[:, 1], MA), ALU.mult).then_inc(vw_ready, 1)
                dve.wait_ge(d_ready, t + 1)
                v.tensor_tensor(DM[:], pD[:].rearrange("p (h e) -> p h e", e=P),
                                c["farc"][:].unsqueeze(1).to_broadcast([P, MH, P]), ALU.add).then_inc(dm_ready, 1)
                dve.wait_ge(turned, t + 1)
                v.tensor_copy(T[:, u, 2], pT[:, 2].rearrange("p (h e) -> p h e", e=P)).then_inc(k_taken, 1)
                v.tensor_copy(T[:, u, 1], pT[:, 1].rearrange("p (h e) -> p h e", e=P)).then_inc(qw_taken, 1)

            def weigh(chunk):
                t, u, r = chunk
                dve.wait_ge(s_ready, t + 1)
                dve.wait_ge(w_ready, t + 1)
                v.tensor_tensor(SW[:, u], pS[:].rearrange("p (h e) -> p h e", e=P), WX[:], ALU.mult).then_inc(sw_ready, 1)

            def memory(t):
                return C[1] if isinstance(t, int) and t == NPT else C[0]

            def decay(chunk):
                t, u, r = chunk
                state = memory(t)
                dve.wait_ge(num_ready, t + 1)
                if isinstance(t, int) and t == NPT:
                    dve.wait_ge(state_in, 16)
                v.tensor_tensor(state[:], state[:], dec[:, bass.ds(t, 1)].rearrange("p o h -> p (o h)").unsqueeze(2)
                                .to_broadcast([P, MH, MA]), ALU.mult).then_inc(decayed, 1)

            def finish(chunk):
                t, u, r = chunk
                g, state = gates(t), memory(t)
                dve.wait_ge(u_ready, t + 1)
                dve.wait_ge(decayed, t + 1)
                v.tensor_tensor(heads(state[:]), heads(state[:]), pairs(pT[:, 1:3]), ALU.add).then_inc(c_ready, 1)
                num = pairs(pN[:])
                v.tensor_copy(dn[:, 0].rearrange("p (b h) -> p b h", b=2), num[:, :, :, MD]).then_inc(dn_ready, 1)
                dve.wait_ge(dn_ready, t + 1)
                v.scalar_tensor_tensor(out=dn[:, 1], in0=dn[:, 0], scalar=-1.0, in1=dn[:, 0], op0=ALU.mult,
                                       op1=ALU.max).then_inc(ab_ready, 1)
                dve.wait_ge(ab_ready, t + 1)
                v.tensor_tensor(dn[:, 2], dn[:, 1], g[:, 2], ALU.max).then_inc(fl_ready, 1)
                dve.wait_ge(fl_ready, t + 1)
                v.reciprocal(dn[:, 3], dn[:, 2]).then_inc(rd_ready, 1)
                dve.wait_ge(rd_ready, t + 1)
                at_least(dve, stored[u], 16 * r)
                v.tensor_tensor(heads(H[:, u]), num[:, :, :, 0:MD],
                                dn[:, 3].rearrange("p (b h) -> p b h", b=2).unsqueeze(3).to_broadcast([P, 2, 2, MD]),
                                ALU.mult).then_inc(h_ready, 1)

            def modulation_row(t):
                dve.wait_ge(mod_psum, t + 1)
                span = bass.ds(t * 2 * P, 2 * P)
                v.tensor_tensor(mod_rows[:, span], pm[0:2, 0:2 * P], bias[:, span], ALU.add).then_inc(mod_row, 1)

            def slot(chunk, nxt):
                prepare(nxt)
                if not (isinstance(chunk[0], int) and chunk[0] == 0):
                    modulation_row(chunk[0] - 1)
                decay(chunk)
                weigh(nxt)
                finish(chunk)
            dve.wait_ge(bias_in, 16)
            chunks(dve, lambda i: (prepare(i), weigh(i)), slot,
                   lambda i: (decay(i), finish(i), modulation_row(NPT - 1)))
            dve.wait_ge(mod_turned, 1)
            v.tensor_copy(c["mod"][:, 3 * KD:5 * KD], pm[:, 0:4 * KD].rearrange("p (j c) -> p j c", c=2)).then_inc(mod_ready, 1)
            dve.wait_ge(mod_ready, 1)
            v.tensor_scalar(c["A2"][:], c["mod"][:, 4 * KD:5 * KD, :], 1.0, None, ALU.add).then_inc(plus_one, 1)
            dve.wait_ge(plus_one, 1)
            v.tensor_tensor(c["A2"][:], c["A2"][:], c["norm2"][:].unsqueeze(2).to_broadcast([P, KD, 2]),
                            ALU.mult).then_inc(scale_ready, 1)

        @block.tensor
        def _(pe):
            t_ = nc.tensor

            def turn(chunk):
                t, u, r = chunk
                pe.wait_ge(ug_in[u], 32 * r + 32)
                at_least(pe, dm_ready, t)
                for h in range(MH):
                    mm = t_.matmul(pD[:, h * P:(h + 1) * P], LG[:, u, h], RU[:, u, h], start=(h == 0), stop=True,
                                   skip_group_check=True)
                mm.then_inc(d_ready, 1)
                pe.wait_ge(k_scaled, t + 1)
                pe.wait_ge(q_weighted, t + 1)
                at_least(pe, c_ready, t - 1)
                at_least(pe, q_taken, t)
                for n, src in enumerate((x[:, u, 0], qw[:, u], ks[:, u])):
                    for h in range(MH):
                        mm = t_.transpose(pT[:, n, h * P:(h + 1) * P], src[:, h], c["ident"][:])
                mm.then_inc(turned, 1)

            def modulate(chunk):
                t, u, r = chunk
                pe.wait_ge(w_in[u], 16 * r + 16)
                at_least(pe, mod_row, t)
                for kk in range(KD):
                    mm = t_.matmul(pm[0:2, 0:2 * P], c["silu_c"][:, kk, :], wa[:, u, kk], start=(kk == 0),
                                   stop=(kk == KD - 1))
                mm.then_inc(mod_psum, 1)

            def scores(chunk):
                t, u, r = chunk
                pe.wait_ge(q_taken, t + 1)
                pe.wait_ge(k_taken, t + 1)
                at_least(pe, sw_ready, t)
                for h in range(MH):
                    mm = t_.matmul(pS[:, h * P:(h + 1) * P], T[:, u, 2, h], T[:, u, 0, h], start=(h == 0), stop=True,
                                   skip_group_check=True)
                mm.then_inc(s_ready, 1)

            def numerator(chunk):
                t, u, r = chunk
                last = isinstance(t, int) and t == NPT
                state = C[1] if last else C[0]
                pe.wait_ge(qw_taken, t + 1)
                at_least(pe, h_ready, t)
                if last:
                    pe.wait_ge(state_in, 16)
                elif isinstance(t, int) and t == 0:
                    pe.wait_ge(ones_ready, 4)
                at_least(pe, c_ready, t)
                for h in range(MH):
                    t_.matmul(pN[:, h // 2, (h % 2) * MA:(h % 2 + 1) * MA], T[:, u, 1, h], state[:, h],
                              start=(h % 2 == 0), stop=False, skip_group_check=True)
                pe.wait_ge(sw_ready, t + 1)
                for h in range(MH):
                    mm = t_.matmul(pN[:, h // 2, (h % 2) * MA:(h % 2 + 1) * MA], SW[:, u, h], VI[:, u, h],
                                   start=False, stop=True, skip_group_check=True)
                mm.then_inc(num_ready, 1)

            def update(chunk):
                t, u, r = chunk
                pe.wait_ge(vw_ready, t + 1)
                if not (isinstance(t, int) and t == NPT):
                    pe.wait_ge(qw_taken, t + 2)
                    pe.wait_ge(k_taken, t + 2)
                for h in range(MH):
                    mm = t_.matmul(pT[:, 1 + h // 2, (h % 2) * MA:(h % 2 + 1) * MA], ks[:, u, h], VU[:, u, h],
                                   start=(h % 2 == 0), stop=True, skip_group_check=True)
                mm.then_inc(u_ready, 1)

            def slot(chunk, nxt):
                turn(nxt)
                numerator(chunk)
                scores(nxt)
                update(chunk)
                modulate(chunk)
            chunks(pe, lambda i: (turn(i), scores(i)), slot, lambda i: (numerator(i), update(i)))
            pe.wait_ge(mod_row, NPT)
            for j in range(2 * KD):
                at = (3 * KD - NMOD + j) * P
                mm = t_.transpose(pm[:, 2 * j:2 * j + 2], mod_rows[:, at:at + P], c["ident"][0:2, 0:2])
            mm.then_inc(mod_turned, 1)


def output_projection(k, c, raw):
    nc, d = k.nc, k.d
    x_in = [k.sem(f"tile_loaded{n}") for n in range(4)]
    res_in = [k.sem("residual_loaded0"), k.sem("residual_loaded1")]
    stored = [k.sem("x1_stored0"), k.sem("x1_stored1")]
    w_low = [k.sem("w_low_even"), k.sem("w_low_odd")]
    (w_high, rows_in, summed, std_ready, rstd_ready, normed, weighted, y_ready, turned,
     y_high, y_low, mix_ready, gated, x1_ready) = k.sems(
        "w_high", "rows_loaded", "squares_summed", "std_ready", "rstd_ready",
        "normed", "weighted", "y_ready", "y_turned", "y_high", "y_low", "mix_ready", "gated", "x1_ready")
    with ExitStack() as s:
        wH = sbuf(nc, s, "ewH", [P, KD, D], F32R)
        wL = sbuf(nc, s, "ewL", [P, KD, D], F32R)
        gate = sbuf(nc, s, "egate", [P, 2, D])
        wrow = sbuf(nc, s, "ewrow", [P, D])
        x = sbuf(nc, s, "ex", [P, 2, D])
        y = sbuf(nc, s, "ey", [P, 4, D])
        o = sbuf(nc, s, "eo", [P, 4, W5])
        st = sbuf(nc, s, "est", [P, 4, 4, 8])
        yH = sbuf(nc, s, "eyH", [P, 2, KD, P], F32R)
        yL = sbuf(nc, s, "eyL", [P, 2, KD, P], F32R)
        mix = sbuf(nc, s, "emix", [P, 2, D])
        sq = sbuf(nc, s, "esq", [P, D])
        pT = psum(nc, s, "epT", [P, 2, D])
        acc = psum(nc, s, "eacc", [P, 2, D])
        block = s.enter_context(nc.Block())
        sample = lambda i: int(isinstance(i.t, int) and i.t == NPT)

        def weights_split(eng, kk):
            eng.wait_ge(w_high, kk + 1)
            (nc.gpsimd if kk % 2 == 0 else nc.vector).tensor_tensor(
                wL[:, kk], raw[:, kk], wH[:, kk].bitcast(F32), ALU.subtract).then_inc(w_low[kk % 2], 1)

        @block.sync
        def _(sp):
            for n in range(2):
                src = d["mods"][n:n + 1, (2 * KD - NMOD) * P:(3 * KD - NMOD) * P]
                sp.dma_start(gate[:, n], src.to_broadcast([P, D])).then_inc(rows_in, 16)
            sp.dma_start(wrow[:], d["y_norms"]).then_inc(rows_in, 16)

            def load(i):
                at_least(sp, turned, i.t - 3)
                sp.dma_start(y[:, i.j, 0:W5], d["h_d"][tok(i.t), :]).then_inc(x_in[i.j], 16)
                sp.dma_start(y[:, i.j, W5:], d["o_d"][tok(i.t), :]).then_inc(x_in[i.j], 16)
                sp.dma_start(o[:, i.j], d["proj_out"][4, tok(i.t), :]).then_inc(x_in[i.j], 16)

            def residual(i):
                at_least(sp, x1_ready, i.t - 1)
                sp.dma_start(x[:, i.u], d["x_all"][tok(i.t), :]).then_inc(res_in[i.u], 16)

            def slot(i):
                residual(i)
                if i.within(3):
                    load(i.ahead(3))
            for t in range(3):
                load(Turn(t, t, 0))
            turns_of_four(sp, slot)

        @block.gpsimd
        def _(pool):
            for kk in range(0, KD, 2):
                weights_split(pool, kk)

            def store(i):
                pool.wait_ge(x1_ready, i.t + 1)
                pool.dma_start(d["x1_d"][tok(i.t), :], mix[:, i.u]).then_inc(stored[i.u], 16)
            turns_of_four(pool, store)
            for u in range(2):
                pool.wait_ge(stored[u], 16 * len(range(u, NT, 2)))

        @block.scalar
        def _(act):
            for kk in range(KD):
                nc.scalar.activation(wH[:, kk], raw[:, kk], ACT.Copy).then_inc(w_high, 1)


            def spread(i):
                act.wait_ge(x_in[i.j], 48 * i.q + 48)
                at_least(act, rstd_ready, i.t - 3)
                for h in range(MH + 1):
                    span = slice(h * MD, (h + 1) * MD) if h < MH else slice(W5, D)
                    op = nc.scalar.activation(sq[:, span], y[:, i.j, span], ACT.Square, accum_out=st[:, i.j, 0, h:h + 1])
                op.then_inc(summed, 1)
                act.wait_ge(summed, i.t + 1)
                nc.scalar.activation(st[:, i.j, 2, 0:MH], st[:, i.j, 0, 0:MH], ACT.Sqrt, bias=c["eps"][:], scale=1.0 / MD)
                nc.scalar.activation(st[:, i.j, 2, MH:MH + 1], st[:, i.j, 0, MH:MH + 1], ACT.Sqrt, bias=c["eps"][:],
                                     scale=1.0 / W5).then_inc(std_ready, 1)

            def high(i):
                act.wait_ge(turned, i.t + 1)
                at_least(act, mix_ready, i.t - 1)
                nc.scalar.activation(yH[:, i.u], pT[:, i.u].rearrange("p (j e) -> p j e", e=P), ACT.Copy).then_inc(y_high, 1)

            def slot(i):
                if i.within(2):
                    high(i.ahead(2))
                if i.within(3):
                    spread(i.ahead(3))
            for t in range(3):
                spread(Turn(t, t, 0))
            for t in range(2):
                high(Turn(t, t, 0))
            turns_of_four(act, slot)

        @block.vector
        def _(dve):
            v = nc.vector
            dve.wait_ge(rows_in, 48)

            for kk in range(1, KD, 2):
                weights_split(dve, kk)

            def norm(i):
                t, st_, y_ = i.t, st[:, i.j], y[:, i.j]
                dve.wait_ge(std_ready, t + 1)
                v.reciprocal(st_[:, 3, 0:5], st_[:, 2, 0:5]).then_inc(rstd_ready, 1)
                dve.wait_ge(rstd_ready, t + 1)
                ya = y_[:, 0:W5].rearrange("p (h e) -> p h e", e=MD)
                v.tensor_tensor(ya, ya, st_[:, 3, 0:4].unsqueeze(2).to_broadcast([P, MH, MD]), ALU.mult).then_inc(normed, 1)
                dve.wait_ge(normed, t + 1)
                v.tensor_tensor(y_[:, 0:W5], y_[:, 0:W5], wrow[:, 0:W5], ALU.mult).then_inc(weighted, 1)
                v.scalar_tensor_tensor(out=y_[:, W5:], in0=y_[:, W5:], scalar=st_[:, 3, 4:5], in1=wrow[:, W5:],
                                       op0=ALU.mult, op1=ALU.mult).then_inc(y_ready, 1)
                dve.wait_ge(weighted, t + 1)
                v.tensor_tensor(y_[:, 0:W5], y_[:, 0:W5], o[:, i.j], ALU.mult).then_inc(y_ready, 1)

            def low(i):
                dve.wait_ge(y_high, i.t + 1)
                at_least(dve, mix_ready, i.t - 1)
                v.tensor_tensor(yL[:, i.u], pT[:, i.u].rearrange("p (j e) -> p j e", e=P), yH[:, i.u].bitcast(F32),
                                ALU.subtract).then_inc(y_low, 1)

            def finish(i):
                count = 16 * (2 * i.q + i.j // 2)
                dve.wait_ge(mix_ready, i.t + 1)
                at_least(dve, stored[i.u], count)
                dve.wait_ge(res_in[i.u], count + 16)
                v.tensor_tensor(mix[:, i.u], acc[:, i.u], gate[:, sample(i)], ALU.mult).then_inc(gated, 1)
                dve.wait_ge(gated, i.t + 1)
                v.tensor_tensor(mix[:, i.u], mix[:, i.u], x[:, i.u], ALU.add).then_inc(x1_ready, 1)

            def slot(i):
                if i.within(2):
                    norm(i.ahead(2))
                finish(i)
                if i.within(2):
                    low(i.ahead(2))
            for t in range(2):
                norm(Turn(t, t, 0))
                low(Turn(t, t, 0))
            turns_of_four(dve, slot)

        @block.tensor
        def _(pe):
            def turn(i):
                pe.wait_ge(y_ready, 2 * i.t + 2)
                at_least(pe, y_low, i.t - 1)
                for kk in range(KD):
                    mm = nc.tensor.transpose(pT[:, i.u, kk * P:(kk + 1) * P], y[:, i.j, kk * P:(kk + 1) * P],
                                             c["ident"][:])
                mm.then_inc(turned, 1)

            def slot(i):
                pe.wait_ge(y_low, i.t + 1)
                at_least(pe, gated, i.t - 1)
                for half in range(2):
                    cols = slice(half * W5, (half + 1) * W5)
                    for kk in range(KD):
                        if isinstance(i.t, int) and i.t == 0 and half == 0:
                            pe.wait_ge(w_low[kk % 2], kk // 2 + 1)
                        for n, (a, w) in enumerate(((yH, wH), (yL, wH), (yH, wL))):
                            mm = nc.tensor.matmul(acc[:, i.u, cols], a[:, i.u, kk], w[:, kk, cols],
                                                  start=(kk == 0 and n == 0), stop=(kk == KD - 1 and n == 2))
                mm.then_inc(mix_ready, 1)
                if i.within(2):
                    turn(i.ahead(2))
            turn(Turn(0, 0, 0))
            turn(Turn(1, 1, 0))
            turns_of_four(pe, slot)


def ffn_up(k, c, hH, hL):
    nc, d = k.nc, k.d
    NV = 5
    WT = (SEQ + DEC) // NV
    NU = 2 + SEQ + 2 + DEC
    S0 = 2 + SEQ + 2
    parts = ((0, 0, SEQ), (SEQ, S0 - 2, DEC))
    raw_in = [k.sem("w_raw_loaded0"), k.sem("w_raw_loaded1")]
    (w_high, w_low, up_done, up_taken, consts_in, zeroed, first_tap, second_tap, conv_done, silu_ready, act_ready, kept,
     turned, ends_taken, ends_stored, history_set, stored) = k.sems(
        "w_high", "w_low", "up_done", "up_taken", "constants_loaded", "zeroed", "first_tap", "second_tap", "conv_done",
        "silu_ready", "act_ready", "last_rows_kept", "last_rows_turned", "last_rows_taken", "last_rows_stored",
        "history_set", "act_stored")
    with ExitStack() as s:
        raw = sbuf(nc, s, "fraw", [P, 2, KD, P])
        wH = sbuf(nc, s, "fwH", [P, 2, KD, P], F32R)
        wL = sbuf(nc, s, "fwL", [P, 2, KD, P], F32R)
        U = sbuf(nc, s, "fU", [P, 2, NU])
        V = sbuf(nc, s, "fV", [P, 2, SEQ + DEC])
        cw = sbuf(nc, s, "fcw", [P, 2 * NF, 3])
        cb = sbuf(nc, s, "fcb", [P, 2 * NF])
        cs = sbuf(nc, s, "fcs", [P, 2 * NF, 2])
        ends = sbuf(nc, s, "fends", [P, 2, 2, 2 * NF])
        ends_t = sbuf(nc, s, "fends_t", [4 * NF, 2, P])
        acc = psum(nc, s, "facc", [P, NV, W5])
        block = s.enter_context(nc.Block())

        def pairs(eng, body):
            body(0, True)
            with eng.Fori(1, NF) as i:
                body(i, False)

        @block.sync
        def _(sp):
            for t, n in ((cw, "w_conv_T"), (cb, "b_conv_T"), (cs, "conv_state_T")):
                sp.dma_start(t[:], d[n]).then_inc(consts_in, 16)

            def load(i, first):
                for j in range(2):
                    if not first:
                        sp.wait_ge(w_low, 2 * i + j - 1)
                    sp.dma_start(raw[:, j], d["w_up"].rearrange("(q p) n -> p q n", p=P)
                                 [:, :, bass.ds(j * FF + i * P, P)]).then_inc(raw_in[j], 16)

            def store(i):
                sp.wait_ge(act_ready, i + 1)
                sp.dma_start(d["act_d"][0:NPT, :, bass.ds(i, 1), :].rearrange("t p o e -> p t (o e)"),
                             V[:, 0, 0:SEQ].rearrange("p (t e) -> p t e", e=P)).then_inc(stored, 16)
                sp.dma_start(d["act_d"][NPT, :, bass.ds(i, 1), 0:DEC].rearrange("p o e -> p (o e)"),
                             V[:, 0, SEQ:]).then_inc(stored, 16)
            load(0, True)
            with sp.Fori(1, NF) as i:
                load(i, False)
                store(i - 1)
            store(NF - 1)
            sp.wait_ge(ends_taken, 1)
            for t in range(2):
                sp.dma_start(d["conv_out"][t], ends_t[:, t]).then_inc(ends_stored, 16)
            sp.wait_ge(ends_stored, 32)
            sp.wait_ge(stored, 32 * NF)

        @block.scalar
        def _(act):
            def split(i, j, free=False):
                act.wait_ge(raw_in[j], 16 * i + 16)
                if not free:
                    act.wait_ge(up_done, NV * (2 * i + j - 1))
                nc.scalar.activation(wH[:, j], raw[:, j], ACT.Copy).then_inc(w_high, 1)

            def take(i, j, first=False):
                n = 2 * i + j
                if not first:
                    act.wait_ge(conv_done, n - 1)
                    act.wait_ge(kept, n - 1)
                for w in range(NV):
                    act.wait_ge(up_done, NV * n + w + 1)
                    at, end = w * WT, min((w + 1) * WT, SEQ)
                    op = nc.scalar.activation(U[:, j, 2 + at:2 + end], acc[:, w, 0:end - at], ACT.Copy)
                    if end == SEQ:
                        op = nc.scalar.activation(U[:, j, S0:], acc[:, w, SEQ - at:WT], ACT.Copy)
                    op.then_inc(up_taken, 1)

            def silu(i):
                act.wait_ge(conv_done, 2 * i + 1)
                nc.scalar.activation(V[:, 0], V[:, 0], ACT.Silu).then_inc(silu_ready, 1)

            split(0, 0, free=True)
            split(0, 1, free=True)
            take(0, 0, first=True)
            split(1, 0)
            take(0, 1, first=True)
            silu(0)
            split(1, 1)
            with act.Fori(1, NF - 1) as i:
                take(i, 0)
                split(i + 1, 0)
                take(i, 1)
                silu(i)
                split(i + 1, 1)
            take(NF - 1, 0)
            take(NF - 1, 1)
            silu(NF - 1)

        @block.gpsimd
        def _(pool):
            def body(i, first):
                for j in range(2):
                    pool.wait_ge(w_high, 2 * i + j + 1)
                    if not first:
                        pool.wait_ge(up_done, NV * (2 * i + j - 1))
                    nc.gpsimd.tensor_tensor(wL[:, j], raw[:, j], wH[:, j].bitcast(F32), ALU.subtract).then_inc(w_low, 1)
            pairs(pool, body)

        @block.vector
        def _(dve):
            v = nc.vector
            v.memset(U[:, :, 0:2], 0.0).then_inc(zeroed, 1)
            dve.wait_ge(consts_in, 48)

            def conv(i, j, first):
                n = 2 * i + j
                ft = bass.ds(i + j * NF, 1)
                tap = lambda m: cw[:, ft, m:m + 1].rearrange("p o m -> p (o m)")
                if not first:
                    dve.wait_ge(conv_done, n - 1)
                v.tensor_copy(U[:, j:j + 1, S0 - 2:S0], cs[:, ft, :]).then_inc(history_set, 1)
                dve.wait_ge(up_taken, NV * (n + 1))
                dve.wait_ge(history_set, n + 1)
                if not first:
                    dve.wait_ge(act_ready, i)
                    dve.wait_ge(stored, 32 * i)
                for at, u0, width in parts:
                    v.tensor_scalar(V[:, j, at:at + width], U[:, j, u0:u0 + width], tap(0), cb[:, ft],
                                    ALU.mult, ALU.add).then_inc(first_tap, 1)
                for m, (at, u0, width) in enumerate(parts):
                    dve.wait_ge(first_tap, 2 * n + m + 1)
                    v.scalar_tensor_tensor(out=V[:, j, at:at + width], in0=U[:, j, u0 + 1:u0 + 1 + width],
                                           scalar=tap(1), in1=V[:, j, at:at + width], op0=ALU.mult,
                                           op1=ALU.add).then_inc(second_tap, 1)
                for m, (at, u0, width) in enumerate(parts):
                    dve.wait_ge(second_tap, 2 * n + m + 1)
                    op = v.scalar_tensor_tensor(out=V[:, j, at:at + width], in0=U[:, j, u0 + 2:u0 + 2 + width],
                                                scalar=tap(2), in1=V[:, j, at:at + width], op0=ALU.mult, op1=ALU.add)
                op.then_inc(conv_done, 1)
                for m, rows in enumerate((U[:, j, SEQ:SEQ + 2], U[:, j, NU - 2:NU])):
                    op = v.tensor_copy(ends[:, m, :, ft].rearrange("p r o -> p (r o)"), rows)
                op.then_inc(kept, 1)

            def body(i, first):
                if first:
                    dve.wait_ge(zeroed, 1)
                conv(i, 0, first)
                conv(i, 1, first)
                dve.wait_ge(silu_ready, i + 1)
                dve.wait_ge(conv_done, 2 * i + 2)
                v.tensor_tensor(V[:, 0], V[:, 0], V[:, 1], ALU.mult).then_inc(act_ready, 1)
            pairs(dve, body)
            dve.wait_ge(turned, 1)
            v.tensor_copy(ends_t[:], acc[0:4 * NF, 0, 0:2 * P].rearrange("p (m e) -> p m e", e=P)).then_inc(ends_taken, 1)

        @block.tensor
        def _(pe):
            def body(i, first):
                for j in range(2):
                    n = 2 * i + j
                    pe.wait_ge(w_high, n + 1)
                    pe.wait_ge(w_low, n + 1)
                    for w in range(NV):
                        at_least(pe, up_taken, NV * (n - 1) + w + 1 if not first or j else 0)
                        dst, cols = acc[:, w, 0:WT], slice(w * WT, (w + 1) * WT)
                        for kk in range(KD):
                            for m, (a, h) in enumerate(((wH, hH), (wH, hL), (wL, hH))):
                                mm = nc.tensor.matmul(dst, a[:, j, kk], h[:, kk, cols],
                                                      start=(kk == 0 and m == 0), stop=(kk == KD - 1 and m == 2))
                        mm.then_inc(up_done, 1)
            pairs(pe, body)
            pe.wait_ge(kept, 2 * NF)
            pe.wait_ge(up_taken, NV * 2 * NF)
            for m in range(2):
                mm = nc.tensor.transpose(acc[0:4 * NF, 0, m * P:(m + 1) * P],
                                         ends[:, m].rearrange("p r n -> p (r n)"), c["ident"][:])
            mm.then_inc(turned, 1)


def ffn_down(k, c):
    nc, d = k.nc, k.d
    NR = 8
    raw_in = [k.sem(f"w_raw_loaded{n}") for n in range(NR)]
    act_in = [k.sem("act_loaded0"), k.sem("act_loaded1")]
    x_in = [k.sem("x1_loaded0"), k.sem("x1_loaded1")]
    stored = [k.sem("y_stored0"), k.sem("y_stored1")]
    w_low = [k.sem("w_low_even"), k.sem("w_low_odd")]
    gate_in, w_high, w_used, a_high, a_low, down_done, gated, y_ready = k.sems(
        "gate_loaded", "w_high", "w_used", "act_high", "act_low", "down_done", "gated", "y_ready")
    with ExitStack() as s:
        raw = sbuf(nc, s, "draw", [P, NR, W5])
        wH = sbuf(nc, s, "dwH", [P, NF, W5], F32R)
        wL = sbuf(nc, s, "dwL", [P, NF, W5], F32R)
        a = sbuf(nc, s, "da", [P, 2, NF, P])
        aH = sbuf(nc, s, "daH", [P, 2, NF, P], F32R)
        aL = sbuf(nc, s, "daL", [P, 2, NF, P], F32R)
        gate = sbuf(nc, s, "dgate", [P, 2, D])
        x = sbuf(nc, s, "dx", [P, 2, W5])
        y = sbuf(nc, s, "dy", [P, 2, W5])
        acc = psum(nc, s, "dacc", [P, 2, W5])
        block = s.enter_context(nc.Block())

        class Tile:
            def __init__(self, half, t, u, r):
                self.half, self.t, self.n, self.b = half, t, half * NT + t, u ^ half
                self.r = half * (NT // 2) + r + (half & u)
                self.sample = isinstance(t, int) and t == NPT
                self.width = DEC if self.sample else P
                self.cols = slice(half * W5, (half + 1) * W5)
                self.first = isinstance(t, int) and self.n < 2

        def half_tiles(eng, half, body, start=0):
            for t in range(start, 2):
                body(Tile(half, t, t, 0))
            with eng.Fori(1, NPT // 2 - 1) as i:
                body(Tile(half, 2 * i, 0, i))
                body(Tile(half, 2 * i + 1, 1, i))
            for t in range(NPT - 2, NT):
                body(Tile(half, t, t % 2, t // 2))

        def weights_split(eng, half, kk):
            q = half * NF + kk
            eng.wait_ge(w_high, q + 1)
            (nc.gpsimd if kk % 2 == 0 else nc.vector).tensor_tensor(
                wL[:, kk], raw[:, q % NR], wH[:, kk].bitcast(F32), ALU.subtract).then_inc(w_low[kk % 2], 1)

        @block.sync
        def _(sp):
            def weights(half, kk):
                q = half * NF + kk
                if q >= NR:
                    sp.wait_ge(w_low[kk % 2], (q - NR) // 2 + 1)
                sp.dma_start(raw[:, q % NR], d["w_down"][kk * P:(kk + 1) * P, half * W5:(half + 1) * W5])\
                    .then_inc(raw_in[q % NR], 16)

            def load(i):
                if not i.first:
                    sp.wait_ge(a_low, i.n - 1)
                sp.dma_start(a[:, i.b, :, 0:i.width],
                             d["act_d"][bass.ds(i.t, 1), :, :, 0:i.width].rearrange("o p n e -> (o p) n e"))\
                    .then_inc(act_in[i.b], 16)
                if not i.first:
                    sp.wait_ge(y_ready, i.n - 1)
                sp.dma_start(x[:, i.b], d["x1_d"][tok(i.t), i.cols]).then_inc(x_in[i.b], 16)
            for kk in range(2):
                weights(0, kk)
            load(Tile(0, 0, 0, 0))
            for kk in range(2, NF):
                weights(0, kk)
            for n in range(2):
                src = d["mods"][n:n + 1, (5 * KD - NMOD) * P:(6 * KD - NMOD) * P]
                sp.dma_start(gate[:, n], src.to_broadcast([P, D])).then_inc(gate_in, 16)
            half_tiles(sp, 0, load, start=1)
            for kk in range(NR):
                weights(1, kk)
            load(Tile(1, 0, 0, 0))
            for kk in range(NR, NF):
                weights(1, kk)
            half_tiles(sp, 1, load, start=1)

        @block.gpsimd
        def _(pool):
            def store(i):
                pool.wait_ge(y_ready, i.n + 1)
                pool.dma_start(d["y_out"][tok(i.t), i.cols], y[:, i.b]).then_inc(stored[i.b], 16)
            for kk in range(0, NF, 2):
                weights_split(pool, 0, kk)
            for t in range(2):
                store(Tile(0, t, t, 0))
            with pool.Fori(1, NPT // 2) as i:
                store(Tile(0, 2 * i, 0, i))
                store(Tile(0, 2 * i + 1, 1, i))
            for kk in range(0, NF, 2):
                weights_split(pool, 1, kk)
            store(Tile(0, NPT, 0, NPT // 2))
            half_tiles(pool, 1, store)
            for u in range(2):
                pool.wait_ge(stored[u], 16 * NT)

        @block.scalar
        def _(act):
            def split(half):
                for kk in range(NF):
                    q = half * NF + kk
                    act.wait_ge(raw_in[q % NR], 16 * (q // NR) + 16)
                    if half and kk < NF - 1:
                        act.wait_ge(w_used, kk + 1)
                    elif half:
                        act.wait_ge(down_done, NT)
                    nc.scalar.activation(wH[:, kk], raw[:, q % NR], ACT.Copy).then_inc(w_high, 1)

            def high(i):
                act.wait_ge(act_in[i.b], 16 * i.r + 16)
                if not i.first:
                    act.wait_ge(down_done, i.n - 1)
                nc.scalar.activation(aH[:, i.b, :, 0:i.width], a[:, i.b, :, 0:i.width], ACT.Copy).then_inc(a_high, 1)
            for half in range(2):
                high(Tile(half, 0, 0, 0))
                split(half)
                half_tiles(act, half, high, start=1)

        @block.vector
        def _(dve):
            v = nc.vector

            def low(i):
                dve.wait_ge(a_high, i.n + 1)
                if not i.first:
                    dve.wait_ge(down_done, i.n - 1)
                v.tensor_tensor(aL[:, i.b, :, 0:i.width], a[:, i.b, :, 0:i.width], aH[:, i.b, :, 0:i.width].bitcast(F32),
                                ALU.subtract).then_inc(a_low, 1)

            def finish(i):
                w, b = i.width, i.b
                dve.wait_ge(down_done, i.n + 1)
                at_least(dve, stored[b], 16 * i.r)
                v.tensor_tensor(y[0:w, b], acc[0:w, b], gate[0:w, int(i.sample), i.cols], ALU.mult).then_inc(gated, 1)
                dve.wait_ge(gated, i.n + 1)
                dve.wait_ge(x_in[b], 16 * i.r + 16)
                v.tensor_tensor(y[0:w, b], y[0:w, b], x[0:w, b], ALU.add).then_inc(y_ready, 1)

            for half in range(2):
                low(Tile(half, 0, 0, 0))
                for kk in range(1, NF, 2):
                    weights_split(dve, half, kk)
                if half:
                    finish(Tile(0, NPT, 0, NPT // 2))
                else:
                    dve.wait_ge(gate_in, 32)
                for t in range(2):
                    low(Tile(half, t + 1, (t + 1) % 2, (t + 1) // 2))
                    finish(Tile(half, t, t, 0))
                with dve.Fori(1, NPT // 2 - 1) as i:
                    low(Tile(half, 2 * i + 1, 1, i))
                    finish(Tile(half, 2 * i, 0, i))
                    low(Tile(half, 2 * i + 2, 0, i + 1))
                    finish(Tile(half, 2 * i + 1, 1, i))
                for t in range(NPT - 2, NPT):
                    low(Tile(half, t + 1, (t + 1) % 2, (t + 1) // 2))
                    finish(Tile(half, t, t % 2, t // 2))
            finish(Tile(1, NPT, 0, NPT // 2))

        @block.tensor
        def _(pe):
            def body(i):
                w, start = i.width, isinstance(i.t, int) and i.t == 0
                pe.wait_ge(a_high, i.n + 1)
                pe.wait_ge(a_low, i.n + 1)
                if not i.first:
                    pe.wait_ge(gated, i.n - 1)
                for kk in range(NF):
                    if start:
                        pe.wait_ge(w_low[kk % 2], i.half * (NF // 2) + kk // 2 + 1)
                    for n, (l, m) in enumerate(((aH, wH), (aL, wH), (aH, wL))):
                        mm = nc.tensor.matmul(acc[0:w, i.b], l[:, i.b, kk, 0:w], m[:, kk], start=(kk == 0 and n == 0),
                                              stop=(kk == NF - 1 and n == 2))
                    if i.sample and i.half == 0:
                        mm.then_inc(w_used if kk < NF - 1 else down_done, 1)
                if not (i.sample and i.half == 0):
                    mm.then_inc(down_done, 1)
            for half in range(2):
                half_tiles(pe, half, body)


def build(nc, dram):
    with ExitStack() as ctx:
        k = Kernel(nc, ctx, dram)
        k.scratch("mods", [2, (6 * KD - NMOD) * P])
        dram["qk_T"] = k.scratch("qk_rows", [2, SH, SD, P + TOK])[:, :, :, P:]
        dram["o_d"] = k.scratch("o_rows", [P + TOK, W5])[P:, :]
        k.scratch("h_d", [TOK, W5])
        k.scratch("ug_d", [2, MH, TOK])
        k.scratch("x1_d", [TOK, D])
        k.scratch("act_d", [NT, P, NF, P])
        k.scratch("gates_d", [8, TOK])
        c = {}
        for name, shape, dt in (("ident", [P, P], F32), ("ident_r", [P, P], F32R), ("tri", [P, P], F32),
                                ("tri_r", [P, P], F32R), ("keep", [P, P], F32), ("far", [P, P], F32),
                                ("far_r", [P, P], F32R), ("farc", [P, P], F32), ("nones", [P, P], F32),
                                ("fold", [P, SD], F32), ("eps", [P, 1], F32), ("one", [P, 1], F32), ("mod", [P, 48, 2], F32),
                                ("A1", [P, KD, 2], F32), ("A2", [P, KD, 2], F32), ("silu_c", [P, KD, 2], F32),
                                ("norm2", [P, KD], F32)):
            c[name] = sbuf(nc, ctx, name, shape, dt)
        modulation(k, c)
        k.end_phase()
        with ExitStack() as s:
            hH = sbuf(nc, s, "h1H", [P, KD, TOK], F32R)
            hL = sbuf(nc, s, "h1L", [P, KD, TOK], F32R)
            normalise(k, c, dram["x_all"], c["A1"], 0, hH, hL)
            k.end_phase()
            project_gates(k, c, hH, hL)
            k.end_phase()
            project(k, c, hH, hL, dram["w_in7"], 0, 5, dram["proj_out"], False)
            k.end_phase()
            project(k, c, hH, hL, dram["w_in7"], 5, 2, dram["proj_out"], True)
            k.end_phase()
        attention(k, c)
        k.end_phase()
        with ExitStack() as s:
            gc = sbuf(nc, s, "gate_cols", [P, NT, 3, MH])
            dec = sbuf(nc, s, "decay", [P, NT, MH])
            gate_rows(k, c, gc, dec)
            k.end_phase()
            mlstm(k, c, gc, dec)
            k.end_phase()
        with ExitStack() as s:
            w_out = sbuf(nc, s, "w_out_sb", [P, KD, D])
            attention_sample(k, c, w_out)
            k.end_phase()
            output_projection(k, c, w_out)
            k.end_phase()
        with ExitStack() as s:
            hH = sbuf(nc, s, "h2H", [P, KD, TOK], F32R)
            hL = sbuf(nc, s, "h2L", [P, KD, TOK], F32R)
            normalise(k, c, dram["x1_d"], c["A2"], 24, hH, hL, "b")
            k.end_phase()
            ffn_up(k, c, hH, hL)
            k.end_phase()
        ffn_down(k, c)
        k.end_phase()


OUTS = {
    "y_out": [TOK, D],
    "conv_out": [2, 4 * NF, P],
    "m_out": [2, MH, 1],
    "c_out": [2, P, MH, MD + 1],
    "proj_out": [7, TOK, W5],
}


def layout(i):
    f = lambda a: np.ascontiguousarray(np.asarray(a))
    x = np.concatenate([np.asarray(i["x_prompt"])[0], np.asarray(i["x_sample"])[0],
                        np.zeros((P - DEC, D), np.float32)])
    cols = lambda a, n: f(np.asarray(a).reshape(n, P).T)
    w_in = np.asarray(i["w_in"])[0]
    c = np.stack([np.asarray(i["c_prompt"])[0], np.asarray(i["c_sample"])[0]])
    g = 4 * W5
    mq, mk, mv, mo = (w_in[:, n * W5:(n + 1) * W5] for n in range(4))
    sq, sk, sv = (w_in[:, n:n + W5] for n in range(g + 2 * MH, g + 2 * MH + 3 * W5, W5))
    parts = [mq, mk, mv, sv, mo, sq, sk]
    norms = np.stack([np.asarray(i["sb_q_norm_w"])[0], np.asarray(i["sb_k_norm_w"])[0]])
    return {
        "x_all": f(x),
        "c_T": f(c.reshape(2, KD, P).transpose(2, 1, 0)),
        "w_ada": f(np.asarray(i["w_ada"])[0]),
        "b_ada": f(np.asarray(i["b_ada"]).reshape(1, 6 * D)),
        "norm1_T": cols(i["norm1_w"], KD),
        "norm2_T": cols(i["norm2_w"], KD),
        "w_in7": f(np.stack(parts)),
        "w_gate": f(w_in[:, g:g + 2 * MH]),
        "y_norms": f(np.broadcast_to(np.concatenate([np.asarray(i["ml_norm_w"]).reshape(W5),
                                                     np.asarray(i["sb_out_norm_w"])[0]]), (P, D))),
        "w_out": f(np.asarray(i["w_out"])[0]),
        "w_up": f(np.asarray(i["w_up"])[0]),
        "w_down": f(np.asarray(i["w_down"])[0]),
        "w_conv_T": f(np.asarray(i["w_conv"])[0].reshape(3, 2 * NF, P).transpose(2, 1, 0)),
        "b_conv_T": cols(i["b_conv"], 2 * NF),
        "conv_state_T": f(np.asarray(i["state_ffn_conv"])[0, 0].reshape(2, 2 * NF, P).transpose(2, 1, 0)),
        "b_gates": f(np.stack([np.asarray(i["b_ig"])[0], np.asarray(i["b_fg"])[0]], axis=1)),
        "m_init": f(np.asarray(i["state_mlstm_m"]).reshape(MH, 1)),
        "c_init": f(np.concatenate([np.asarray(i["state_mlstm_c"])[0, 0],
                                    np.asarray(i["state_mlstm_n"])[0, 0][:, :, None]], axis=2).transpose(1, 0, 2)),
        "past_k": f(np.asarray(i["cache_sb_k"]).reshape(PAST, W5)),
        "past_v": f(np.asarray(i["cache_sb_v"]).reshape(PAST, W5)),
        "sb_norms": f(np.broadcast_to(norms, (P, 2, SD))),
    }


def results(r):
    y, pr, cm, m, u = (np.asarray(r[n]) for n in ("y_out", "proj_out", "c_out", "m_out", "conv_out"))
    out = [y[:SEQ].reshape(1, SEQ, D), y[SEQ:SEQ + DEC].reshape(1, DEC, D)]
    for n, rows in enumerate((slice(0, SEQ), slice(SEQ, SEQ + DEC))):
        mem = cm[n].transpose(1, 0, 2)
        out += [mem[None, None, :, :, :MD], mem[None, None, :, :, MD], m[n].reshape(1, 1, MH)]
        out += [pr[g, rows].reshape(1, 1, -1, SH, SD) for g in (6, 3)]
        out += [u[n].reshape(1, 1, 2, 2 * FF)]
    return tuple(np.ascontiguousarray(a) for a in out)


def kernel(**inputs):
    import concourse.bacc as bacc
    from concourse.bass_utils import run_bass_kernel_spmd

    nc = bacc.Bacc("TRN2", target_bir_lowering=False, num_devices=1)
    arrays = layout(inputs)
    dram = {n: nc.dram_tensor(n, a.shape, mybir.dt.from_np(a.dtype), kind="ExternalInput").ap() for n, a in arrays.items()}
    for n, shape in OUTS.items():
        dram[n] = nc.dram_tensor(n, shape, F32, kind="ExternalOutput").ap()
    build(nc, dram)
    r = run_bass_kernel_spmd(nc, [arrays], core_ids=[0])
    return results(r.results[0])
```
